# Optimizing a Trainium2 kernel written in Bass

```python
import jax, jax.numpy as jnp
from jax import lax
import numpy as np

D_MODEL = 4096
BATCH = 1
SEQ = 512
DEPTH = 1

N_MEM = 256
D_MIX = D_MODEL
HEAD_DIM = 128
ATT_WIDTH = D_MIX // 2
ATT_HEADS = ATT_WIDTH // HEAD_DIM
ATT_KV_HEADS = 4
KV_WIDTH = ATT_KV_HEADS * HEAD_DIM
WINDOW = 128
BLOCK = 128
ROPE_THETA = 500000.0
ROT_DIM = HEAD_DIM // 4
LRU_WIDTH = D_MIX // 4
LRU_BLOCKS = 8
LRU_BLOCK_DIM = LRU_WIDTH // LRU_BLOCKS
CONV_WIDTH = 4
CONV_PAD = (2, 1)
LRU_C = 8.0
MEM_HEADS = 4
MEM_WIDTH = D_MIX // 4
MEM_HEAD_DIM = MEM_WIDTH // MEM_HEADS
EPS = 1e-6
SPLIT_WIDTHS = [ATT_WIDTH, KV_WIDTH, KV_WIDTH, LRU_WIDTH, MEM_WIDTH, ATT_WIDTH, LRU_WIDTH, MEM_WIDTH]
IN_WIDTH = sum(SPLIT_WIDTHS)

kernel_name = "hymba_bidir_swa_rglru_memxattn"

def rmsnorm(t, g):
    tf = t.astype(jnp.float32)
    y = tf * lax.rsqrt(jnp.mean(tf * tf, axis=-1, keepdims=True) + EPS)
    return (y * g.astype(jnp.float32)).astype(t.dtype)

def partial_rope(t, pos):
    half = ROT_DIM // 2
    inv_freq = jnp.power(jnp.float32(ROPE_THETA), -jnp.arange(half, dtype=jnp.float32) * 2.0 / ROT_DIM)
    ang = pos.astype(jnp.float32)[:, None] * inv_freq[None, :]
    cos = jnp.cos(ang)[None, :, None, :]
    sin = jnp.sin(ang)[None, :, None, :]
    tf = t.astype(jnp.float32)
    x1 = tf[..., :half]
    x2 = tf[..., half:ROT_DIM]
    out = jnp.concatenate([x1 * cos - x2 * sin, x2 * cos + x1 * sin, tf[..., ROT_DIM:]], axis=-1)
    return out.astype(t.dtype)

def windowed_gqa_sink(q, k, v, sink):
    B, S, H, D = q.shape
    KVH = k.shape[2]
    G = H // KVH
    nb = S // BLOCK
    qb = q.reshape(B, nb, BLOCK, KVH, G, D)

    def band(t):
        tp = jnp.pad(t, ((0, 0), (BLOCK, BLOCK), (0, 0), (0, 0)))
        tb = tp.reshape(B, nb + 2, BLOCK, KVH, D)
        return jnp.concatenate([tb[:, :-2], tb[:, 1:-1], tb[:, 2:]], axis=2)

    kw = band(k)
    vw = band(v)
    s = jnp.einsum('bnqhgd,bnkhd->bnhgqk', qb, kw).astype(jnp.float32) * (D ** -0.5)
    qpos = jnp.arange(nb)[:, None, None] * BLOCK + jnp.arange(BLOCK)[None, :, None]
    kpos = (jnp.arange(nb)[:, None, None] - 1) * BLOCK + jnp.arange(3 * BLOCK)[None, None, :]
    valid = (jnp.abs(kpos - qpos) <= WINDOW) & (kpos >= 0) & (kpos < S)
    s = jnp.where(valid[None, :, None, None, :, :], s, jnp.finfo(jnp.float32).min)
    sk = sink.astype(jnp.float32).reshape(KVH, G)[None, None, :, :, None, None]
    m = jnp.maximum(jnp.max(s, axis=-1, keepdims=True), sk)
    p = jnp.exp(s - m)
    denom = jnp.sum(p, axis=-1, keepdims=True) + jnp.exp(sk - m)
    attn = (p / denom).astype(v.dtype)
    out = jnp.einsum('bnhgqk,bnkhd->bnqhgd', attn, vw)
    return out.reshape(B, S, H * D)

def centred_depthwise_conv(t, w, b):
    C = t.shape[-1]
    y = lax.conv_general_dilated(t, w[:, None, :], window_strides=(1,), padding=[CONV_PAD],
                                 dimension_numbers=('NWC', 'WIO', 'NWC'), feature_group_count=C)
    return y + b

def _linear_combine(e1, e2):
    a1, b1 = e1
    a2, b2 = e2
    return a1 * a2, a2 * b1 + b2

def rglru_direction(xc, w_a, b_a, w_x, b_x, lam, reverse):
    B, S, C = xc.shape
    xb = xc.reshape(B, S, LRU_BLOCKS, LRU_BLOCK_DIM)
    r = jax.nn.sigmoid((jnp.einsum('bsnc,ncd->bsnd', xb, w_a).reshape(B, S, C) + b_a).astype(jnp.float32))
    i = jax.nn.sigmoid((jnp.einsum('bsnc,ncd->bsnd', xb, w_x).reshape(B, S, C) + b_x).astype(jnp.float32))
    log_a = -LRU_C * r * jax.nn.softplus(-lam.astype(jnp.float32))
    a = jnp.exp(log_a)
    mult = jnp.sqrt(-jnp.expm1(2.0 * log_a))
    b_in = mult * i * xc.astype(jnp.float32)
    _, h = lax.associative_scan(_linear_combine, (a, b_in), reverse=reverse, axis=1)
    return h

def memory_cross_attention(q, mem, mem_g, w_mem_kv):
    B, S, _ = q.shape
    M = mem.shape[1]
    kv = rmsnorm(mem, mem_g) @ w_mem_kv
    km, vm = jnp.split(kv, 2, axis=-1)
    qh = q.reshape(B, S, MEM_HEADS, MEM_HEAD_DIM)
    km = km.reshape(B, M, MEM_HEADS, MEM_HEAD_DIM)
    vm = vm.reshape(B, M, MEM_HEADS, MEM_HEAD_DIM)
    s = jnp.einsum('bshd,bmhd->bhsm', qh, km).astype(jnp.float32) * (MEM_HEAD_DIM ** -0.5)
    p = jax.nn.softmax(s, axis=-1).astype(vm.dtype)
    return jnp.einsum('bhsm,bmhd->bshd', p, vm).reshape(B, S, MEM_WIDTH)

def hybrid_layer(h, mem, pos, pre_g, w_in, sink, conv_w, conv_b, w_a, b_a, w_x, b_x, lam,
                 mem_g, w_mem_kv, g_att, g_lru, g_mem, w_out, post_g):
    B, S, _ = h.shape
    u = rmsnorm(h, pre_g)
    proj = u @ w_in
    idx = list(np.cumsum(SPLIT_WIDTHS)[:-1])
    q_att, k_att, v_att, x_lru, q_mem, z_att, z_lru, z_mem = jnp.split(proj, idx, axis=-1)
    q_att = partial_rope(q_att.reshape(B, S, ATT_HEADS, HEAD_DIM), pos)
    k_att = partial_rope(k_att.reshape(B, S, ATT_KV_HEADS, HEAD_DIM), pos)
    v_att = v_att.reshape(B, S, ATT_KV_HEADS, HEAD_DIM)
    y_att = windowed_gqa_sink(q_att, k_att, v_att, sink)
    xc = centred_depthwise_conv(x_lru, conv_w, conv_b)
    h_fwd = rglru_direction(xc, w_a[0], b_a[0], w_x[0], b_x[0], lam[0], reverse=False)
    h_bwd = rglru_direction(xc, w_a[1], b_a[1], w_x[1], b_x[1], lam[1], reverse=True)
    y_lru = (h_fwd + h_bwd).astype(h.dtype)
    y_mem = memory_cross_attention(q_mem, mem, mem_g, w_mem_kv)
    y = jnp.concatenate([rmsnorm(y_att, g_att) * jax.nn.silu(z_att),
                         rmsnorm(y_lru, g_lru) * jax.nn.silu(z_lru),
                         rmsnorm(y_mem, g_mem) * jax.nn.silu(z_mem)], axis=-1)
    out = y @ w_out
    return h + rmsnorm(out, post_g)

def setup_inputs(seed: int = 0) -> dict:
    key = jax.random.key(seed)
    ks = jax.random.split(key, 20)
    f32 = jnp.float32
    nrm = lambda k, shape, scale: jax.random.normal(k, shape, f32) * scale
    gain = lambda k, shape: 1.0 + 0.1 * jax.random.normal(k, shape, f32)
    u = jax.random.uniform(ks[11], (DEPTH, 2, LRU_WIDTH), f32, 0.9, 0.999)
    a0 = jnp.power(u, 1.0 / LRU_C)
    lam = jnp.log(a0) - jnp.log1p(-a0)
    return {
        "x": nrm(ks[0], (BATCH, SEQ, D_MODEL), 1.0),
        "mem": nrm(ks[1], (BATCH, N_MEM, D_MODEL), 1.0),
        "pre_norm_gain": gain(ks[2], (DEPTH, D_MODEL)),
        "w_in": nrm(ks[3], (DEPTH, D_MODEL, IN_WIDTH), D_MODEL ** -0.5),
        "att_sink": nrm(ks[4], (DEPTH, ATT_HEADS), 0.5),
        "conv_w": nrm(ks[5], (DEPTH, CONV_WIDTH, LRU_WIDTH), CONV_WIDTH ** -0.5),
        "conv_b": nrm(ks[6], (DEPTH, LRU_WIDTH), 0.02),
        "lru_w_a": nrm(ks[7], (DEPTH, 2, LRU_BLOCKS, LRU_BLOCK_DIM, LRU_BLOCK_DIM), LRU_BLOCK_DIM ** -0.5),
        "lru_b_a": nrm(ks[8], (DEPTH, 2, LRU_WIDTH), 0.02),
        "lru_w_x": nrm(ks[9], (DEPTH, 2, LRU_BLOCKS, LRU_BLOCK_DIM, LRU_BLOCK_DIM), LRU_BLOCK_DIM ** -0.5),
        "lru_b_x": nrm(ks[10], (DEPTH, 2, LRU_WIDTH), 0.02),
        "lru_lambda": lam,
        "mem_norm_gain": gain(ks[12], (DEPTH, D_MODEL)),
        "w_mem_kv": nrm(ks[13], (DEPTH, D_MODEL, 2 * MEM_WIDTH), D_MODEL ** -0.5),
        "att_out_gain": gain(ks[14], (DEPTH, ATT_WIDTH)),
        "lru_out_gain": gain(ks[15], (DEPTH, LRU_WIDTH)),
        "mem_out_gain": gain(ks[16], (DEPTH, MEM_WIDTH)),
        "w_out": nrm(ks[17], (DEPTH, D_MIX, D_MODEL), D_MIX ** -0.5),
        "post_norm_gain": gain(ks[18], (DEPTH, D_MODEL)),
    }

def reference(x, mem, pre_norm_gain, w_in, att_sink, conv_w, conv_b, lru_w_a, lru_b_a, lru_w_x,
              lru_b_x, lru_lambda, mem_norm_gain, w_mem_kv, att_out_gain, lru_out_gain,
              mem_out_gain, w_out, post_norm_gain):
    S = x.shape[1]
    pos = jnp.arange(S, dtype=jnp.int32)
    h = x
    for l in range(DEPTH):
        h = hybrid_layer(h, mem, pos, pre_norm_gain[l], w_in[l], att_sink[l], conv_w[l], conv_b[l],
                         lru_w_a[l], lru_b_a[l], lru_w_x[l], lru_b_x[l], lru_lambda[l],
                         mem_norm_gain[l], w_mem_kv[l], att_out_gain[l], lru_out_gain[l],
                         mem_out_gain[l], w_out[l], post_norm_gain[l])
    return h


_drawn_inputs = setup_inputs


def setup_inputs(seed=0):
    import zlib

    import numpy as np

    out = dict(_drawn_inputs(seed))
    spreads = {}
    factors = {'att_sink': 8.0, 'lru_b_a': 38.373, 'lru_b_x': 23.35}
    for name, (base, spread) in spreads.items():
        noise = np.random.default_rng([zlib.crc32(name.encode()), seed]).standard_normal(out[name].shape)
        drawn = base * np.exp(spread * noise) if base else spread * noise
        out[name] = __import__('jax').numpy.asarray(drawn.astype(out[name].dtype))
    for name, factor in factors.items():
        out[name] = (out[name] * factor).astype(out[name].dtype)
    return out
```

```python
from contextlib import ExitStack, contextmanager

import numpy as np
import concourse.bass as bass
from concourse import mybir

F32 = mybir.dt.float32
F32R = mybir.dt.float32r
ALU = mybir.AluOpType
ACT = mybir.ActivationFunctionType
AX = mybir.AxisListType

P = 128
D_MODEL = 4096
SEQ = 512
N_MEM = 256
EPS = 1e-6
KT = D_MODEL // P
NT = 4
BW = NT * P
SB = SEQ // P
MB = N_MEM // P
HEADS = 16
GROUPS = 4
ATT_SCALE = float(P) ** -0.5
MEM_HEADS = 4
MEM_D = 256
MEM_SCALE = float(MEM_D) ** -0.5
LRU_TILES = 8
LRU_C = 8.0
ROT = 32
MASKED = -1.0e30
FIRST = 1

B_K, B_V, B_Q, B_XLRU, B_QMEM, B_Z, B_OUT, B_END = 4, 5, 6, 10, 12, 14, 22, 30
B_ATT, B_LRU, B_MEMATT = 8, 12, 14
RAW = 4
RING = 4
LEAD = 3
HEAD_AT = (1, 8, 15, 22)
TILE_AT = (0, 7, 14, 21)
MEMHEAD_AT = (1, 8, 15, 22)
BAND = [(max(i - 1, 0), min(i + 1, SB - 1) - max(i - 1, 0) + 1) for i in range(SB)]
PT_FIRST = (0, 1, 4, 7)
PT_AT = (0, 2, 5, 8)
G_MEM, G_PRE, G_OUT, G_POST = 0, 32, 64, 96
PAR = 88
C_CONVW, C_CONVB, C_BA, C_BX, C_LAM = 0, 32, 40, 56, 72


def hymba(nc, x, mem, pre_g, w_in, sink, conv_w, conv_b, w_a, b_a, w_x, b_x, lam, mem_g, w_mem,
          g_att, g_lru, g_mem, w_out, post_g, rope_cos, rope_sin, band_mask, identity, out):
    ctx = ExitStack()
    with ctx:
        def sem(name):
            return ctx.enter_context(nc.semaphore(name))

        used = {}

        def at(offset, name, shape, dt=F32):
            used[name] = offset + 32 * ((int(np.prod(shape[1:])) + 7) // 8)
            return nc.alloc_sbuf_tensor_at(name, shape, dt, offset=offset)

        class Region:
            def __init__(self, start, end):
                self.now, self.end = start, end

            def __call__(self, name, shape, dt=F32):
                t = at(self.now, name, shape, dt)
                self.now = used[name]
                assert self.now <= self.end, (name, self.now, self.end)
                return t

        HI = 32 * ((nc.sbuf_base + 31) // 32)
        LO = HI + KT * SEQ * 4
        u_hi = at(HI, "u_hi", [P, KT, SEQ], F32R)
        u_lo = at(LO, "u_lo", [P, KT, SEQ], F32R)
        u_raw = at(LO, "u_raw", [P, KT * SEQ])
        m_hi = at(HI, "m_hi", [P, KT, N_MEM], F32R)
        m_lo = at(HI + KT * N_MEM * 4, "m_lo", [P, KT, N_MEM], F32R)
        y_hi = at(HI, "y_hi", [P, KT, SEQ], F32R)
        y_lo = at(LO, "y_lo", [P, KT, SEQ], F32R)
        mem_rows = at(LO, "mem_rows", [P, MB, D_MODEL])
        x_rows = at(LO + MB * D_MODEL * 4, "x_rows", [P, 2, D_MODEL])
        x_fin = at(HI, "x_fin", [P, SB, D_MODEL])
        o_fin = at(LO, "o_fin", [P, SB, D_MODEL])

        top = nc.sbuf_usable_end
        W = Region(LO + KT * SEQ * 4, top)
        w_raw = W("w_raw", [P, RAW, BW])
        w_hi = W("w_hi", [P, RING, BW], F32R)
        w_lo = W("w_lo", [P, RING, BW], F32R)
        ident = W("ident", [P, P])
        ones = W("ones", [P, P])
        mask = W("mask", [P, 3 * P])
        gains = W("gains", [P, P])
        par = W("par", [P, PAR])
        sinks = W("sinks", [P, HEADS])
        eps = W("eps", [P, 1])
        cdec = W("cdec", [P, 2 * LRU_TILES])
        tiny = W("tiny", [P, 48])
        stage = W("stage", [P, NT, SEQ])
        sq_acc = W("sq_acc", [P, SEQ])
        sq_tmp = W("sq_tmp", [P, SEQ])
        at_side = W.now

        R = Region(at_side, top)
        par_rows = R("par_rows", [P, 2, P])
        m_scaled = R("m_scaled", [P, 2, N_MEM])
        m_bn = R("m_bn", [P, MB, 8 * 6])
        m_mv = R("m_mv", [P, MB, 2])
        m_rstd = R("m_rstd", [P, MB])
        x_ss = R("x_ss", [P, SB, 4])
        x_rstd = R("x_rstd", [P, SB])
        x_chunk = R("x_chunk", [P, 2, SB, 2 * P])
        x_scaled = R("x_scaled", [P, 2, SB, P])

        R = Region(at_side, top)
        rope_c = R("rope_c", [ROT, SEQ])
        rope_s = R("rope_s", [ROT, SEQ])
        rot = R("rot", [ROT, SEQ])
        q_raw = R("q_raw", [P, SEQ])
        q_hi = R("q_hi", [P, SEQ], F32R)
        q_lo = R("q_lo", [P, SEQ], F32R)
        k_raw = R("k_raw", [P, SEQ])
        v_raw = R("v_raw", [P, SEQ])
        k_hi = R("k_hi", [P, SEQ], F32R)
        k_lo = R("k_lo", [P, SEQ], F32R)
        v_hi = R("v_hi", [P, SEQ], F32R)
        v_lo = R("v_lo", [P, SEQ], F32R)
        probs = R("probs", [P, 2, 3 * P])
        pt_hi = R("pt_hi", [P, 10, P], F32R)
        pt_lo = R("pt_lo", [P, 10, P], F32R)
        y_sb = R("y_sb", [P, SEQ])
        sink4 = R("sink4", [P, 4])
        srow = R("srow", [P, 24])

        R = Region(at_side, top)
        r_bc = R("r_bc", [P, 3, SEQ])
        at_late = R.now
        l_in = R("l_in", [P, SEQ + 4])
        l_w = R("l_w", [P, 2, 2, P])
        xc = R("xc", [P, SEQ])
        l_r = R("l_r", [P, 2, SEQ])
        l_i = R("l_i", [P, 2, SEQ])
        l_a = R("l_a", [P, 2, SEQ])
        l_t = R("l_t", [P, 2, SEQ])
        l_n = R("l_n", [P, 2, SEQ])
        l_h = R("l_h", [P, 2, SEQ])
        l_y = R("l_y", [P, SEQ])

        R = Region(at_late, top)
        mq_raw = R("mq_raw", [P, SEQ])
        mq_hi = R("mq_hi", [P, 2, SEQ], F32R)
        mq_lo = R("mq_lo", [P, 2, SEQ], F32R)
        mk_raw = R("mk_raw", [P, 2 * N_MEM])
        mv_raw = R("mv_raw", [P, 2 * N_MEM])
        mk_hi = R("mk_hi", [P, 2 * N_MEM], F32R)
        mk_lo = R("mk_lo", [P, 2 * N_MEM], F32R)
        mv_hi = R("mv_hi", [P, MB * MEM_D], F32R)
        mv_lo = R("mv_lo", [P, MB * MEM_D], F32R)
        mp = R("mp", [P, SB, N_MEM])
        mpt_hi = R("mpt_hi", [P, MB, SEQ], F32R)
        mpt_lo = R("mpt_lo", [P, MB, SEQ], F32R)
        mrow = R("mrow", [P, 16])

        R = Region(at_late, top)
        g_y = R("g_y", [P, NT, SEQ])
        g_hi = R("g_hi", [P, 2, SEQ], F32R)
        g_lo = R("g_lo", [P, 2, SEQ], F32R)
        og = R("og", [P, 2, SEQ])
        o_nat = R("o_nat", [P, SB, BW])

        G = [ctx.enter_context(nc.psum_tensor(f"gemm{n}", [P, SEQ], F32)) for n in range(NT)]
        X = [ctx.enter_context(nc.psum_tensor(f"side{n}", [P, SEQ], F32)) for n in range(4)]

        def scratch(name, shape, dt=F32):
            return nc.dram_tensor(name, shape, dt, kind="Internal").ap()

        kvT = scratch("kvT", [4 * BW, N_MEM])
        projT = scratch("projT", [10 * BW, SEQ])
        yT = scratch("yT", [D_MODEL, SEQ])
        gT_hi = scratch("gT_hi", [D_MODEL, SEQ])
        gT_lo = scratch("gT_lo", [D_MODEL, SEQ])
        o_rows = scratch("o_rows", [SEQ, D_MODEL])

        raw_in = [sem(f"raw_in{s}") for s in range(RAW)]
        hi_ready, lo_ready, unit_done = sem("hi_ready"), sem("lo_ready"), sem("unit_done")
        tile_done, act_evac, dve_evac = sem("tile_done"), sem("act_evac"), sem("dve_evac")
        sig_done, z_held = sem("sig_done"), sem("z_held")
        proj_stored, y_stored, g_stored = sem("proj_stored"), sem("y_stored"), sem("g_stored")
        const_in, par_in, par_tr, par_ready = (sem(n) for n in ("const_in", "par_in", "par_tr", "par_ready"))
        memset_done, rope_in, cd_dve, cd_act = (sem(n) for n in ("memset_done", "rope_in", "cd_dve", "cd_act"))
        mem_in = [sem(f"mem_in{i}") for i in range(MB)]
        m_stat, m_sqrt, m_rs = sem("m_stat"), sem("m_sqrt"), sem("m_rs")
        m_scl, m_trd, m_hid, m_lod = (sem(n) for n in ("m_scl", "m_trd", "m_hid", "m_lod"))
        xrow_in = [sem(f"xrow_in{i}") for i in range(2)]
        x_sq, x_sum, x_sqrt, x_rs = (sem(n) for n in ("x_sq", "x_sum", "x_sqrt", "x_rs"))
        chunk_in = [sem(f"chunk_in{i}") for i in range(2)]
        x_scl, x_trd, x_ev, u_split = (sem(n) for n in ("x_scl", "x_trd", "x_ev", "u_split"))
        swapped, rope_mul, rope_done = sem("swapped"), sem("rope_mul"), sem("rope_done")
        q_in, k_in, v_in = sem("q_in"), sem("k_in"), sem("v_in")
        q_hid, q_lod, k_hid, k_lod = (sem(n) for n in ("q_hid", "q_lod", "k_hid", "k_lod"))
        v_trd, v_hid, v_lod = sem("v_trd"), sem("v_hid"), sem("v_lod")
        scored, row_max, max_neg, sink_diff = (sem(n) for n in ("scored", "row_max", "max_neg", "sink_diff"))
        sink_set = sem("sink_set")
        exped, sink_exp, denom, recip, normed = (sem(n) for n in ("exped", "sink_exp", "denom", "recip", "normed"))
        p_trd, pt_hid, pt_lod, pv_done = (sem(n) for n in ("p_trd", "pt_hid", "pt_lod", "pv_done"))
        y_out, y_sq, y_acc, y_free = sem("y_out"), sem("y_sq"), sem("y_acc"), sem("y_free")
        l_zero, l_xin, l_win, conv = (sem(n) for n in ("l_zero", "l_xin", "l_win", "conv"))
        l_mm, l_sig, l_exp, l_asq, l_ix = (sem(n) for n in ("l_mm", "l_sig", "l_exp", "l_asq", "l_ix"))
        l_neg, l_mult, l_b, l_scan, l_sum = (sem(n) for n in ("l_neg", "l_mult", "l_b", "l_scan", "l_sum"))
        mq_in, mk_in, mv_in = sem("mq_in"), sem("mk_in"), sem("mv_in")
        mq_hid, mq_lod, mk_hid, mk_lod = (sem(n) for n in ("mq_hid", "mq_lod", "mk_hid", "mk_lod"))
        mv_trd, mv_hid, mv_lod = sem("mv_trd"), sem("mv_hid"), sem("mv_lod")
        m_scored, m_max, m_neg, m_exp, m_rec, m_norm = (
            sem(n) for n in ("m_scored", "m_max", "m_neg", "m_exp", "m_rec", "m_norm"))
        mp_trd, mp_hid, mp_lod, m_pv = (sem(n) for n in ("mp_trd", "mp_hid", "mp_lod", "m_pv"))
        r_sum, r_sqrt, r_ready = sem("r_sum"), sem("r_sqrt"), sem("r_ready")
        gy_in = [sem(f"gy_in{n}") for n in range(NT)]
        g_norm, g_mul, g_hid, g_lod = (sem(n) for n in ("g_norm", "g_mul", "g_hid", "g_lod"))
        y_in = [sem(f"y_in{i}") for i in range(4)]
        acc_zero, o_gain, o_sq, o_acc, o_trd = (sem(n) for n in ("acc_zero", "o_gain", "o_sq", "o_acc", "o_trd"))
        on_act, on_dve, o_stored, o_free = sem("on_act"), sem("on_dve"), sem("o_stored"), sem("o_free")
        passed_dve, passed_pool = sem("passed_dve"), sem("passed_pool")
        fin_in = [sem(f"fin_in{i}") for i in range(SB)]
        f_sum, f_sqrt, f_rs, f_done, stored = (sem(n) for n in ("f_sum", "f_sqrt", "f_rs", "f_done", "stored"))

        block = ctx.enter_context(nc.Block())

        def f32(ap):
            return ap.bitcast(F32)

        def start_counts(eng, *sems):
            for s in sems:
                eng.sem_inc(s, FIRST)

        GATED = B_OUT - B_Z

        @block.sync
        def _(sp):
            half = D_MODEL // 2
            for b in range(MB):
                for h in range(2):
                    sp.dma_start(mem_rows[:, b, h * half:(h + 1) * half],
                                 mem[0, b * P:(b + 1) * P, h * half:(h + 1) * half]).then_inc(mem_in[b], 16)
            sp.dma_start(ident[:, :], identity).then_inc(const_in, 16)
            rows = lambda v: v.rearrange("a (t p) -> (a t) p", p=P)
            for at_row, v in ((G_MEM, mem_g), (G_PRE, pre_g), (G_OUT, g_att), (G_OUT + 16, g_lru),
                              (G_OUT + 24, g_mem), (G_POST, post_g)):
                n = v.shape[1] // P
                sp.dma_start(par_rows[at_row:at_row + n, 0, :], rows(v)).then_inc(par_in, 16)
            for at_row, v in ((C_CONVW, conv_w.rearrange("a j c -> (a j) c")), (C_CONVB, conv_b),
                              (C_BA, b_a.rearrange("a d c -> (a d) c")),
                              (C_BX, b_x.rearrange("a d c -> (a d) c")),
                              (C_LAM, lam.rearrange("a d c -> (a d) c"))):
                n = v.shape[0] * v.shape[1] // P
                sp.dma_start(par_rows[at_row:at_row + n, 1, :], rows(v)).then_inc(par_in, 16)

            def x_row_load(b):
                if b >= 2:
                    sp.wait_ge(x_sq, 4 * (b - 1))
                sp.dma_start(x_rows[:, b % 2, :], x[0, b * P:(b + 1) * P, :]).then_inc(xrow_in[b % 2], 16)

            def weights(B, k, src):
                if not (isinstance(B, int) and B == 0 and k < RAW):
                    sp.wait_ge(lo_ready, 32 * B + k - RAW + 1)
                sp.dma_start(w_raw[:, k % RAW, :], src).then_inc(raw_in[k % RAW], 16)

            def w_block(B, mat, col, at_unit=None):
                for k in range(KT):
                    weights(B, k, mat[0, k * P:(k + 1) * P, bass.ds(col * BW, BW)])
                    if at_unit:
                        at_unit(k)

            def first_rows(k):
                if k == 0:
                    x_row_load(0)
                if k == 1:
                    x_row_load(1)
                if k == 14:
                    x_row_load(2)
                if k == 24:
                    x_row_load(3)
                if k == 4:
                    sp.dma_start(mask[:, :], band_mask).then_inc(const_in, 16)
                    sp.dma_start(sinks[:, :], sink.partition_broadcast(P)).then_inc(const_in, 16)

            w_block(0, w_mem, 0, first_rows)
            with sp.Fori(1, 3) as B:
                def chunk(k):
                    if k % 4 == 2:
                        c = k // 4
                        sp.wait_ge(x_scl, FIRST + 16 * B - 16 + max(2 * c - 2, 0))
                        sp.dma_start(x_chunk[:, c % 2, :, :], x[0, :, bass.ds(B * 2048 - 2048 + c * 256, 256)]
                                     .rearrange("(b p) n -> p b n", p=P)).then_inc(chunk_in[c % 2], 16)
                w_block(B, w_mem, B, chunk)
            w_block(3, w_mem, 3)

            def ropes(k):
                if k == 0:
                    sp.dma_start(rope_c[:, :], rope_cos).then_inc(rope_in, 16)
                    sp.dma_start(rope_s[:, :], rope_sin).then_inc(rope_in, 16)
            w_block(B_K, w_in, 4, ropes)
            w_block(B_V, w_in, 5)
            with sp.Fori(B_Q, B_ATT) as B:
                w_block(B, w_in, B - B_Q)

            def att_loads(B):
                def go(k):
                    g = B - B_ATT
                    if k == 0:
                        sp.wait_ge(proj_stored, 64 * 6)
                        sp.wait_ge(k_lod, FIRST + g)
                        sp.dma_start(k_raw[:, :], projT[bass.ds(g * P, P), :]).then_inc(k_in, 16)
                        sp.wait_ge(v_trd, FIRST + g)
                        sp.dma_start(v_raw[:, :], projT[bass.ds(g * P + BW, P), :]).then_inc(v_in, 16)
                    for i, s in enumerate(HEAD_AT):
                        if k == (1 if i == 0 else HEAD_AT[i - 1] + 9):
                            if i == 0:
                                sp.wait_ge(proj_stored, 64 * B - 64)
                            sp.wait_ge(q_lod, FIRST + 4 * g + i)
                            sp.dma_start(q_raw[:, :], projT[bass.ds(g * BW + (2 * BW + i * P), P), :])\
                              .then_inc(q_in, 16)
                return go
            with sp.Fori(B_ATT, B_ATT + 2) as B:
                w_block(B, w_in, B - B_Q, att_loads(B))
            with sp.Fori(B_ATT + 2, B_LRU) as B:
                w_block(B, w_in, B - 4, att_loads(B))

            with sp.Fori(B_LRU, B_MEMATT) as B:
                def lru_loads(k):
                    for i, s in enumerate(TILE_AT):
                        if k == s + 3:
                            t = (B - B_LRU) * 4 + i
                            sp.wait_ge(l_zero, 2)
                            if i == 0:
                                sp.wait_ge(proj_stored, 64 * B - 64)
                            sp.wait_ge(conv, FIRST + 4 * t)
                            sp.dma_start(l_in[:, 2:2 + SEQ],
                                         projT[bass.ds((B - B_LRU) * BW + (6 * BW + i * P), P), :])\
                              .then_inc(l_xin, 16)
                            sp.wait_ge(l_mm, FIRST + 4 * t)
                            for which, w in enumerate((w_a, w_x)):
                                sp.dma_start(l_w[:, which, :, :],
                                             w[0, :, bass.ds(t, 1), :, :].rearrange("d t c e -> c (d t) e"))\
                                  .then_inc(l_win, 16)
                w_block(B, w_in, B - 4, lru_loads)

            def mem_loads(k):
                for h, s in enumerate(MEMHEAD_AT):
                    at0 = s + 4
                    if k == at0:
                        if h == 0:
                            sp.wait_ge(proj_stored, 64 * 14)
                            sp.wait_ge(y_stored, 16 * 24)
                            sp.wait_ge(l_mult, 16)
                        sp.wait_ge(mk_lod, h)
                        sp.dma_start(mk_raw[:, :].rearrange("p (t m) -> p t m", t=2),
                                     kvT[h * MEM_D:(h + 1) * MEM_D, :].rearrange("(t p) m -> p t m", p=P))\
                          .then_inc(mk_in, 16)
                        sp.wait_ge(mv_trd, h)
                        sp.dma_start(mv_raw[:, :].rearrange("p (t m) -> p t m", t=2),
                                     kvT[2 * BW + h * MEM_D:2 * BW + (h + 1) * MEM_D, :]
                                     .rearrange("(t p) m -> p t m", p=P)).then_inc(mv_in, 16)
                    for t in range(2):
                        if k == at0 + 2 * t + (1 if t else 0):
                            sp.wait_ge(mq_lod, 2 * h + t)
                            sp.dma_start(mq_raw[:, :], projT[8 * BW + (2 * h + t) * P:8 * BW + (2 * h + t + 1) * P, :])\
                              .then_inc(mq_in, 16)
            w_block(B_MEMATT, w_in, 10, mem_loads)

            def gate_loads(B):
                def go(k):
                    n = k - 9
                    if 0 <= n < NT:
                        if n == 0:
                            sp.wait_ge(y_stored, 16 * 32)
                        sp.wait_ge(g_mul, FIRST + 4 * (B - 15) + n)
                        if not (isinstance(B, int) and B == 15):
                            sp.wait_ge(g_norm, FIRST + 4 * (B - 15))
                        sp.wait_ge(g_lod, FIRST + 4 * (B - 15))
                        sp.dma_start(g_y[:, n, :], yT[bass.ds((B - 15) * BW + n * P, P), :]).then_inc(gy_in[n], 16)
                return go
            with sp.Fori(B_Z + 1, B_OUT) as B:
                w_block(B, w_in, B - 4, gate_loads(B))

            def y_loads(k):
                gate_loads(B_OUT)(k)
                tiles = (2 * k, 2 * k + 1) if k < 14 else (28, 29, 30, 31) if k == 22 else ()
                for t in tiles:
                    sp.wait_ge(unit_done, 32 * (B_OUT - 1) + t + 1)
                    sp.wait_ge(g_stored, (128 * 7 if t < 28 else 128 * 8))
                    sp.dma_start(f32(y_hi[:, t, :]), gT_hi[t * P:(t + 1) * P, :]).then_inc(y_in[t // 8], 16)
                    sp.dma_start(f32(y_lo[:, t, :]), gT_lo[t * P:(t + 1) * P, :]).then_inc(y_in[t // 8], 16)
            w_block(B_OUT, w_out, 0, y_loads)
            with sp.Fori(B_OUT + 1, B_END - 1) as B:
                w_block(B, w_out, B - B_OUT)

            def fin_load(c):
                sp.wait_ge(unit_done, 32 * (B_END - 1) + 8 * c + 8)
                sp.wait_ge(o_stored, 16 * 7)
                sp.dma_start(x_fin[:, c, :], x[0, c * P:(c + 1) * P, :]).then_inc(fin_in[c], 16)
                sp.dma_start(o_fin[:, c, 0:7 * BW], o_rows[c * P:(c + 1) * P, 0:7 * BW]).then_inc(fin_in[c], 16)

            def last_loads(k):
                if k == 24:
                    fin_load(0)
            w_block(B_END - 1, w_out, 7, last_loads)
            for c in range(1, SB):
                fin_load(c)
            for c in range(SB):
                for h in range(2):
                    sp.wait_ge(f_done, 2 * c + h + 1)
                    sp.dma_start(out[0, c * P:(c + 1) * P, h * half:(h + 1) * half],
                                 o_fin[:, c, h * half:(h + 1) * half]).then_inc(stored, 16)
            sp.wait_ge(stored, 16 * 2 * SB)

        @block.tensor
        def _(pe):
            start_counts(pe, l_mm, o_trd, p_trd, pv_done, scored, v_trd, x_trd)
            def unit(B, k, hi, lo, width, bank_free):
                pe.wait_ge(lo_ready, 32 * B + k + 1)
                slot = k % RING
                for n in range(NT):
                    if k == 0:
                        bank_free(n)
                    cols = slice(n * P, (n + 1) * P)
                    acc = G[n][:, 0:width]
                    pe.matmul(acc, w_hi[:, slot, cols], hi[:, k, :], start=(k == 0), stop=False)
                    pe.matmul(acc, w_hi[:, slot, cols], lo[:, k, :], start=False, stop=False)
                    mm = pe.matmul(acc, w_lo[:, slot, cols], hi[:, k, :], start=False, stop=(k == KT - 1))
                    if n == NT - 1:
                        mm.then_inc(unit_done, 1)
                    elif k == KT - 1:
                        mm.then_inc(tile_done, 1)

            def after_copy(B, gated=0):
                done = 2 * (B - gated) - 2
                def wait(n):
                    pe.wait_ge(dve_evac if n % 2 else act_evac, done + n // 2 + 1)
                return wait

            def after_gate(B):
                def wait(n):
                    pe.wait_ge(z_held, 4 * (B - 1 - B_Z) + n + 1)
                return wait

            def gemm(B, hi, lo, width=SEQ, bank_free=None, at_unit=None):
                for k in range(KT):
                    if at_unit:
                        at_unit(k)
                    unit(B, k, hi, lo, width, bank_free or after_copy(B))

            pe.wait_ge(const_in, 16)
            pe.wait_ge(par_in, 16 * 11)
            pe.transpose(X[2][:, 0:P], par_rows[:, 0, :], ident[:, :]).then_inc(par_tr, 1)
            pe.transpose(X[3][:, 0:PAR], par_rows[0:PAR, 1, :], ident[0:PAR, 0:PAR]).then_inc(par_tr, 1)

            def mem_transpose(t):
                if t >= KT:
                    return
                pe.wait_ge(m_scl, t + 1)
                if t >= 4:
                    pe.wait_ge(m_lod, t - 3)
                elif t >= 2:
                    pe.wait_ge(par_ready, 2)
                for b in range(MB):
                    tr = pe.transpose(X[t % 4][:, b * P:(b + 1) * P], m_scaled[:, t % 2, b * P:(b + 1) * P],
                                      ident[:, :])
                tr.then_inc(m_trd, 1)

            for t in range(4):
                mem_transpose(t)
            gemm(0, m_hi, m_lo, N_MEM, lambda n: None, lambda k: mem_transpose(k + 4))

            with pe.Fori(1, 3) as B:
                def x_transpose(k):
                    if k % 2:
                        e = k // 2
                        t = 16 * (B - 1) + e
                        pe.wait_ge(x_scl, FIRST + t + 1)
                        if e >= 4:
                            pe.wait_ge(x_ev, FIRST + t - 3)
                        else:
                            pe.wait_ge(x_ev, FIRST + 16 * (B - 1))
                            pe.wait_ge(m_lod, KT)
                        for b in range(SB):
                            tr = pe.transpose(X[e % 4][:, b * P:(b + 1) * P], x_scaled[:, e % 2, b, :],
                                              ident[:, :])
                        tr.then_inc(x_trd, 1)
                gemm(B, m_hi, m_lo, N_MEM, at_unit=x_transpose)
            gemm(3, m_hi, m_lo, N_MEM)
            gemm(B_K, u_hi, u_lo)
            with pe.Fori(B_V, B_ATT) as B:
                gemm(B, u_hi, u_lo)

            def attention(B):
                g = B - B_ATT

                def scores(h, i):
                    if i < 2:
                        pe.wait_ge(row_max, FIRST + 4 * h)
                    else:
                        pe.wait_ge(row_max, FIRST + 4 * h + i - 1)
                    k0, nk = BAND[i]
                    q, kk = slice(i * P, (i + 1) * P), slice(k0 * P, (k0 + nk) * P)
                    s = X[i % 2][:, 0:nk * P]
                    pe.matmul(s, q_hi[:, q], k_hi[:, kk], start=True, stop=False)
                    pe.matmul(s, q_hi[:, q], k_lo[:, kk], start=False, stop=False)
                    pe.matmul(s, q_lo[:, q], k_hi[:, kk], start=False, stop=True).then_inc(scored, 1)

                def turn(h, i):
                    pe.wait_ge(normed, 4 * h + i + 1)
                    if i < 2:
                        pe.wait_ge(pt_lod, FIRST + 4 * h)
                        pe.wait_ge(y_sq, FIRST + h)
                    else:
                        pe.wait_ge(pt_lod, FIRST + 4 * h + i - 1)
                    for j in range(BAND[i][1]):
                        tr = pe.transpose(X[2 + i % 2][:, j * P:(j + 1) * P], probs[:, i % 2, j * P:(j + 1) * P],
                                          ident[:, :])
                    tr.then_inc(p_trd, 1)

                def values(h):
                    pe.wait_ge(pt_lod, FIRST + 4 * h + 4)
                    pe.wait_ge(v_lod, g + 1)
                    for kb in range(SB):
                        q0, nq = BAND[kb]
                        o = X[2][:, q0 * P:(q0 + nq) * P]
                        v = slice(kb * P, (kb + 1) * P)
                        ph = pt_hi[:, PT_AT[kb]:PT_AT[kb] + nq, :]
                        pl = pt_lo[:, PT_AT[kb]:PT_AT[kb] + nq, :]
                        pe.matmul(o, v_hi[:, v], ph, start=(kb == 0), stop=False, skip_group_check=True)
                        pe.matmul(o, v_hi[:, v], pl, start=False, stop=False, skip_group_check=True)
                        mm = pe.matmul(o, v_lo[:, v], ph, start=False, stop=(kb == SB - 1), skip_group_check=True)
                    mm.then_inc(pv_done, 1)

                def go(k):
                    if k == 1:
                        pe.wait_ge(v_in, 16 * g + 16)
                        pe.wait_ge(pt_lod, FIRST + 16 * g)
                        pe.wait_ge(y_sq, FIRST + 4 * g)
                        for kb in range(SB):
                            tr = pe.transpose(X[2][:, kb * P:(kb + 1) * P], v_raw[:, kb * P:(kb + 1) * P],
                                              ident[:, :])
                        tr.then_inc(v_trd, 1)
                    for i, s in enumerate(HEAD_AT):
                        h = 4 * g + i
                        if k == s + 8:
                            values(h)
                    for i, s in enumerate(HEAD_AT):
                        h = 4 * g + i
                        if k == s + 1:
                            pe.wait_ge(q_lod, FIRST + h + 1)
                            if i == 0:
                                pe.wait_ge(k_lod, FIRST + g + 1)
                            scores(h, 0)
                            scores(h, 1)
                        if k == s + 3:
                            if i == 0:
                                pe.wait_ge(v_lod, g + 1)
                            turn(h, 0)
                            turn(h, 1)
                            scores(h, 2)
                            scores(h, 3)
                        if k == s + 6:
                            turn(h, 2)
                            turn(h, 3)
                return go
            with pe.Fori(B_ATT, B_LRU) as B:
                gemm(B, u_hi, u_lo, at_unit=attention(B))

            with pe.Fori(B_LRU, B_MEMATT) as B:
                def lru(k):
                    for i, s in enumerate(TILE_AT):
                        if k == s + 1:
                            t = 4 * (B - B_LRU) + i
                            pe.wait_ge(conv, FIRST + 4 * t + 4)
                            pe.wait_ge(l_win, 32 * t + 32)
                            for which in range(2):
                                for d in range(2):
                                    n = 2 * which + d
                                    pe.wait_ge(l_sig, FIRST + 4 * t)
                                    pe.matmul(X[n][:, :], l_w[:, which, d, :], xc[:, :],
                                              start=True, stop=True).then_inc(l_mm, 1)
                gemm(B, u_hi, u_lo, at_unit=lru)

            def out_norm(which, squares, bank):
                pe.matmul(X[bank][:, :], ones[:, :], squares, start=True, stop=True).then_inc(r_sum, 1)

            def mem_attention(k):
                if k == 0:
                    pe.wait_ge(y_acc, FIRST + 24)
                    pe.wait_ge(l_sig, FIRST + 32)
                    pe.wait_ge(memset_done, 2)
                    out_norm(0, sq_acc[:, :], 2)
                    out_norm(1, r_bc[:, 1, :], 3)
                for h, s in enumerate(MEMHEAD_AT):
                    if k == s + 9:
                        mem_values(h)
                for h, s in enumerate(MEMHEAD_AT):
                    if k == s + 1:
                        pe.wait_ge(mv_in, 16 * h + 16)
                        if h:
                            pe.wait_ge(mp_lod, 2 * h)
                        else:
                            pe.wait_ge(r_sqrt, 2)
                        for b in range(MB):
                            for t in range(2):
                                tr = pe.transpose(X[2][:, (2 * b + t) * P:(2 * b + t + 1) * P],
                                                  mv_raw[:, t * N_MEM + b * P:t * N_MEM + (b + 1) * P], ident[:, :])
                        tr.then_inc(mv_trd, 1)
                    if k == s + 4:
                        pe.wait_ge(mk_lod, h + 1)
                        pe.wait_ge(mq_lod, 2 * h + 2)
                        pe.wait_ge(y_sq, FIRST + 24 + 2 * h)
                        for i in range(SB):
                            o = X[i // 2][:, (i % 2) * N_MEM:(i % 2 + 1) * N_MEM]
                            q = slice(i * P, (i + 1) * P)
                            for t in range(2):
                                kk = slice(t * N_MEM, (t + 1) * N_MEM)
                                pe.matmul(o, mq_hi[:, t, q], mk_hi[:, kk], start=(i % 2 == 0 and t == 0), stop=False,
                                          skip_group_check=True)
                                pe.matmul(o, mq_hi[:, t, q], mk_lo[:, kk], start=False, stop=False,
                                          skip_group_check=True)
                                mm = pe.matmul(o, mq_lo[:, t, q], mk_hi[:, kk], start=False,
                                               stop=(t == 1), skip_group_check=True)
                            if i % 2:
                                mm.then_inc(m_scored, 1)
                    if k == s + 7:
                        pe.wait_ge(m_norm, SB * h + SB)
                        pe.wait_ge(mv_lod, h + 1)
                        for b in range(MB):
                            for i in range(SB):
                                tr = pe.transpose(X[2 + b][:, i * P:(i + 1) * P], mp[:, i, b * P:(b + 1) * P],
                                                  ident[:, :])
                            tr.then_inc(mp_trd, 1)

            def mem_values(h):
                pe.wait_ge(mp_lod, 2 * h + 2)
                pe.wait_ge(m_exp, SB * h + SB)
                for t in range(2):
                    for b in range(MB):
                        v = slice(b * MEM_D + t * P, b * MEM_D + (t + 1) * P)
                        pe.matmul(X[t][:, :], mv_hi[:, v], mpt_hi[:, b, :], start=(b == 0), stop=False)
                        pe.matmul(X[t][:, :], mv_hi[:, v], mpt_lo[:, b, :], start=False, stop=False)
                        mm = pe.matmul(X[t][:, :], mv_lo[:, v], mpt_hi[:, b, :], start=False, stop=(b == MB - 1))
                    mm.then_inc(m_pv, 1)
            gemm(B_MEMATT, u_hi, u_lo, at_unit=mem_attention)

            def mem_norm(k):
                if k == 2:
                    pe.wait_ge(y_acc, FIRST + 32)
                    pe.wait_ge(y_sq, FIRST + 32)
                    out_norm(2, r_bc[:, 2, :], 2)
            gemm(B_Z + 1, u_hi, u_lo, bank_free=after_gate(B_Z + 1), at_unit=mem_norm)
            with pe.Fori(B_Z + 2, B_OUT) as B:
                gemm(B, u_hi, u_lo, bank_free=after_gate(B))

            def y_ready(k):
                if k % 8 == 0:
                    pe.wait_ge(y_in[k // 8], 256)
            gemm(B_OUT, y_hi, y_lo, bank_free=after_gate(B_OUT), at_unit=y_ready)

            def out_rows(B, n):
                pe.wait_ge(o_gain, 4 * (B - 1 - B_OUT) + n + 1)
                pe.wait_ge(on_act, FIRST + 2 * (B - 1 - B_OUT))
                pe.wait_ge(on_dve, FIRST + 2 * (B - 1 - B_OUT))
                for b in range(SB):
                    tr = pe.transpose(X[n][:, b * P:(b + 1) * P], og[:, n % 2, b * P:(b + 1) * P], ident[:, :])
                tr.then_inc(o_trd, 1)

            def out_side(B):
                def go(k):
                    if 2 <= k < 2 + 2 * NT and k % 2 == 0:
                        out_rows(B, (k - 2) // 2)
                return go
            with pe.Fori(B_OUT + 1, B_END - 1) as B:
                gemm(B, y_hi, y_lo, bank_free=after_copy(B, GATED), at_unit=out_side(B))
            gemm(B_END - 1, y_hi, y_lo, bank_free=after_copy(B_END - 1, GATED), at_unit=out_side(B_END - 1))
            pe.wait_ge(o_acc, FIRST + 32)
            for b in range(SB):
                mm = pe.matmul(G[0][:, b:b + 1], sq_acc[:, b * P:(b + 1) * P], ones[:, 0:1], start=(b == 0),
                               stop=(b == SB - 1), skip_group_check=True)
            mm.then_inc(f_sum, 1)
            for n in range(NT):
                out_rows(B_END, n)

        @block.scalar
        def _(act):
            start_counts(act, l_sig, on_act, x_ev, y_sq)
            def split(B, k):
                act.wait_ge(raw_in[k % RAW], 16 * (8 * B + k // RAW + 1))
                if not (isinstance(B, int) and 32 * B + k < RING):
                    act.wait_ge(unit_done, 32 * B + k - RING + 1)
                act.copy(w_hi[:, k % RING, :], w_raw[:, k % RAW, :]).then_inc(hi_ready, 1)

            def u_part(k):
                act.wait_ge(x_ev, FIRST + KT)
                act.copy(u_hi[:, k, :], u_raw[:, k * SEQ:(k + 1) * SEQ]).then_inc(u_split, 1)

            def evac(B, width=SEQ):
                for n in (0, 2):
                    act.wait_ge(tile_done, 3 * B + n + 1)
                    act.copy(stage[:, n, 0:width], G[n][:, 0:width]).then_inc(act_evac, 1)

            def body(B, side=None, before=None, evacuate=evac):
                for j in range(LEAD, KT + LEAD):
                    b, k = (B, j) if j < KT else (B + 1, j - KT)
                    if before:
                        before(j)
                    if not (isinstance(B, int) and B == B_END - 1 and j >= KT):
                        split(b, k)
                    if side:
                        side(j - LEAD)
                evacuate(B)

            def proj_evac(B, width=SEQ):
                act.wait_ge(proj_stored, 64 * B)
                evac(B, width)

            def m_part(t):
                act.wait_ge(m_trd, t + 1)
                act.activation(m_hi[:, t, :], X[t % 4][:, 0:N_MEM], ACT.Copy,
                               scale=gains[:, G_MEM + t:G_MEM + t + 1]).then_inc(m_hid, 1)

            act.wait_ge(par_tr, 1)
            act.copy(gains[:, :], X[2][:, 0:P]).then_inc(par_ready, 1)
            act.wait_ge(par_tr, 2)
            act.copy(par[:, :], X[3][:, 0:PAR]).then_inc(par_ready, 1)
            act.wait_ge(m_stat, 20)
            act.activation(m_rstd[:, :], m_mv[:, :, 1], ACT.Sqrt).then_inc(m_sqrt, 1)
            act.wait_ge(par_ready, 2)
            for k in range(LEAD):
                m_part(k)
                split(0, k)

            def x_squares(t):
                if t % 2 == 0:
                    q = t // 2
                    b, c = q // 4, q % 4
                    act.wait_ge(xrow_in[b % 2], 16 * (b // 2 + 1))
                    v = x_rows[:, b % 2, c * 1024:(c + 1) * 1024]
                    act.activation(v, v, ACT.Square, accum_out=x_ss[:, b, c:c + 1]).then_inc(x_sq, 1)
                if t == KT - 1:
                    act.wait_ge(x_sum, 2)
                    act.activation(x_rstd[:, :], x_rstd[:, :], ACT.Sqrt).then_inc(x_sqrt, 1)
            body(0, x_squares, lambda j: m_part(j) if j < KT else None, lambda B: proj_evac(B, N_MEM))

            with act.Fori(1, 3) as B:
                def x_out(t):
                    if t % 2 == 1:
                        e = t // 2
                        kt = 16 * (B - 1) + e
                        act.wait_ge(x_trd, FIRST + kt + 1)
                        act.activation(u_raw[:, bass.ds(kt * SEQ, SEQ)], X[e % 4][:, :], ACT.Copy,
                                       scale=gains[:, bass.ds(kt + G_PRE, 1)]).then_inc(x_ev, 1)
                body(B, x_out, evacuate=lambda B: proj_evac(B, N_MEM))
            body(3, before=lambda j: u_part(j - KT) if j >= KT else None,
                 evacuate=lambda B: proj_evac(B, N_MEM))
            body(B_K, before=lambda j: u_part(j) if j < KT else None, evacuate=proj_evac)

            def decay(t):
                if t == 12:
                    act.wait_ge(cd_dve, 2)
                    act.activation(tiny[:, 0:16], tiny[:, 0:16], ACT.Exp, scale=-1.0).then_inc(cd_act, 1)
            body(B_V, decay, evacuate=proj_evac)
            with act.Fori(B_Q, B_ATT) as B:
                body(B, evacuate=proj_evac)

            def attention(B):
                g = B - B_ATT

                def go(t):
                    if t == 0:
                        act.wait_ge(k_in, 16 * g + 16)
                        act.wait_ge(scored, FIRST + 16 * g)
                        act.copy(k_hi[:, :], k_raw[:, :]).then_inc(k_hid, 1)
                    if t == 2:
                        act.wait_ge(v_trd, FIRST + g + 1)
                        act.wait_ge(pv_done, FIRST + 4 * g)
                        act.copy(v_hi[:, :], X[2][:, :]).then_inc(v_hid, 1)
                    for i, s in enumerate(HEAD_AT):
                        h = 4 * g + i
                        if t == s + 8:
                            act.wait_ge(pv_done, FIRST + h + 1)
                            act.wait_ge(y_free, FIRST + h)
                            act.copy(y_sb[:, :], X[2][:, :]).then_inc(y_out, 1)
                            act.wait_ge(y_acc, FIRST + h)
                            act.activation(sq_tmp[:, :], X[2][:, :], ACT.Square).then_inc(y_sq, 1)
                    for i, s in enumerate(HEAD_AT):
                        h = 4 * g + i
                        if t == s:
                            act.wait_ge(q_in, 16 * h + 16)
                            act.wait_ge(scored, FIRST + 4 * h)
                            act.copy(q_hi[:, :], q_raw[:, :]).then_inc(q_hid, 1)
                        for pair in range(2):
                            if t == s + 1 + 3 * pair:
                                act.wait_ge(max_neg, 2 * h + pair + 1)
                                for e in range(2):
                                    b = 2 * pair + e
                                    pr = probs[:, e, 0:BAND[b][1] * P]
                                    act.activation(pr, pr, ACT.Exp, bias=srow[:, 4 + e:5 + e],
                                                   accum_out=srow[:, 8 + e:9 + e]).then_inc(exped, 1)
                                act.wait_ge(sink_diff, 2 * h + pair + 1)
                                act.activation(srow[:, 16:18], srow[:, 12:14], ACT.Exp).then_inc(sink_exp, 1)
                            if t == s + 3 + 3 * pair:
                                for b in (2 * pair, 2 * pair + 1):
                                    nk = BAND[b][1]
                                    act.wait_ge(p_trd, FIRST + 4 * h + b + 1)
                                    act.wait_ge(pv_done, FIRST + h)
                                    act.copy(pt_hi[:, PT_FIRST[b]:PT_FIRST[b] + 2 * nk - 1:2, :],
                                             X[2 + b % 2][:, 0:nk * P].rearrange("p (j q) -> p j q", q=P))\
                                       .then_inc(pt_hid, 1)
                return go
            with act.Fori(B_ATT, B_LRU) as B:
                body(B, attention(B), evacuate=proj_evac)

            with act.Fori(B_LRU, B_MEMATT) as B:
                def lru(t):
                    for i, s in enumerate(TILE_AT):
                        T = 4 * (B - B_LRU) + i
                        if t == s + 2:
                            for n, (o, c) in enumerate(((l_r, C_BA), (l_r, C_BA + 8), (l_i, C_BX), (l_i, C_BX + 8))):
                                act.wait_ge(l_mm, FIRST + 4 * T + n + 1)
                                if n == 2:
                                    act.wait_ge(l_b, FIRST + 2 * T)
                                act.activation(o[:, n % 2, :], X[n][:, :], ACT.Sigmoid,
                                               bias=par[:, bass.ds(T + c, 1)]).then_inc(l_sig, 1)
                        if t == s + 3:
                            act.wait_ge(l_scan, FIRST + 2 * T)
                            act.wait_ge(l_neg, FIRST + 2 * T)
                            act.wait_ge(l_sig, FIRST + 4 * T + 2)
                            for d in range(2):
                                c = cdec[:, bass.ds(T + 8 * d, 1)]
                                act.activation(l_a[:, d, :], l_r[:, d, :], ACT.Exp, scale=c).then_inc(l_exp, 1)
                                act.activation(l_t[:, d, :], l_r[:, d, :], ACT.Tanh, scale=c).then_inc(l_exp, 1)
                        if t == s + 6:
                            for d in range(2):
                                act.wait_ge(l_neg, FIRST + 2 * T + d + 1)
                                act.activation(l_n[:, d, :], l_n[:, d, :], ACT.Sqrt, scale=-1.0).then_inc(l_mult, 1)
                        if t == s + 9:
                            act.wait_ge(l_sum, T + 1)
                            act.wait_ge(y_acc, FIRST + 16 + T)
                            act.activation(sq_tmp[:, :], l_y[:, :], ACT.Square).then_inc(y_sq, 1)
                body(B, lru, evacuate=proj_evac)

            def rms(which, bank, width):
                act.wait_ge(r_sum, which + 1)
                act.activation(r_bc[:, which, :], X[bank][:, :], ACT.Sqrt, bias=eps[:, :],
                               scale=1.0 / width).then_inc(r_sqrt, 1)

            def sigmoids(B):
                for n in range(NT):
                    if n < NT - 1:
                        act.wait_ge(tile_done, 3 * B + n + 1)
                    else:
                        act.wait_ge(unit_done, 32 * B + 32)
                    if n == 0:
                        if isinstance(B, int) and B == B_Z:
                            act.wait_ge(proj_stored, 64 * 14)
                            act.wait_ge(y_stored, 16 * 32)
                        act.wait_ge(g_mul, FIRST + 4 * (B - B_Z))
                    act.activation(stage[:, n, :], G[n][:, :], ACT.Sigmoid).then_inc(sig_done, 1)

            def mem_attention(t):
                if t == 0:
                    rms(0, 2, 2048.0)
                    rms(1, 3, 1024.0)
                for h, s in enumerate(MEMHEAD_AT):
                    if t == s + 9:
                        for d in range(2):
                            act.wait_ge(m_pv, 2 * h + d + 1)
                            act.wait_ge(proj_stored, 64 * 14)
                            act.wait_ge(y_stored, 16 * (24 + 2 * h + d))
                            act.copy(stage[:, 2, :], X[d][:, :]).then_inc(y_out, 1)
                            act.wait_ge(y_acc, FIRST + 24 + 2 * h + d)
                            act.activation(sq_tmp[:, :], X[d][:, :], ACT.Square).then_inc(y_sq, 1)
                for h, s in enumerate(MEMHEAD_AT):
                    if t == s + 1:
                        act.wait_ge(mk_in, 16 * h + 16)
                        act.wait_ge(m_scored, 2 * h)
                        act.copy(mk_hi[:, :], mk_raw[:, :]).then_inc(mk_hid, 1)
                        act.wait_ge(mv_trd, h + 1)
                        act.wait_ge(m_pv, 2 * h)
                        act.copy(mv_hi[:, :], X[2][:, :]).then_inc(mv_hid, 1)
                    for d in range(2):
                        if t == s + 1 + 2 * d:
                            act.wait_ge(mq_in, 16 * (2 * h + d) + 16)
                            act.wait_ge(m_scored, 2 * h)
                            act.copy(mq_hi[:, d, :], mq_raw[:, :]).then_inc(mq_hid, 1)
                    if t == s + 5:
                        for i in range(SB):
                            act.wait_ge(m_neg, 2 * h + i // 2 + 1)
                            act.wait_ge(mp_trd, 2 * h)
                            act.activation(mp[:, i, :], X[i // 2][:, (i % 2) * N_MEM:(i % 2 + 1) * N_MEM], ACT.Exp,
                                           bias=mrow[:, 4 + i:5 + i], scale=MEM_SCALE,
                                           accum_out=mrow[:, 8 + i:9 + i]).then_inc(m_exp, 1)
                    if t == s + 7:
                        for b in range(MB):
                            act.wait_ge(mp_trd, 2 * h + b + 1)
                            act.wait_ge(m_pv, 2 * h)
                            act.copy(mpt_hi[:, b, :], X[2 + b][:, :]).then_inc(mp_hid, 1)
            body(B_MEMATT, mem_attention, evacuate=sigmoids)

            def gates(B, late=None):
                def go(t):
                    if late:
                        late(t)
                    if t >= 6 and t % 2 == 0 and t < 6 + 2 * NT:
                        n = (t - 6) // 2
                        at_g = 4 * (B - 1 - B_Z) + n
                        act.wait_ge(g_mul, FIRST + at_g + 1)
                        if n >= 2:
                            act.wait_ge(g_stored, 128 * (B - 1 - B_Z) + 32 * (n - 1))
                        else:
                            act.wait_ge(g_stored, 128 * (B - 1 - B_Z))
                        act.copy(g_hi[:, n % 2, :], g_y[:, n, :]).then_inc(g_hid, 1)
                return go
            body(B_Z + 1, gates(B_Z + 1, lambda t: rms(2, 2, 1024.0) if t == 2 else None), evacuate=sigmoids)
            with act.Fori(B_Z + 2, B_OUT) as B:
                body(B, gates(B), evacuate=sigmoids)

            def out_evac(B):
                act.wait_ge(g_mul, FIRST + 32)
                act.wait_ge(o_gain, 4 * (B - B_OUT))
                act.wait_ge(o_sq, 4 * (B - B_OUT))
                evac(B)
            body(B_OUT, gates(B_OUT), evacuate=out_evac)

            def row_tiles(B, last=False):
                def go(t):
                    for n in (0, 2):
                        if t == 2 + 2 * n:
                            act.wait_ge(o_trd, FIRST + 4 * (B - 1 - B_OUT) + n + 1)
                            if last:
                                o = o_fin[:, :, 7 * BW + n * P:7 * BW + (n + 1) * P]
                            else:
                                act.wait_ge(o_free, FIRST + B - 1 - B_OUT)
                                o = o_nat[:, :, n * P:(n + 1) * P]
                            act.copy(o, X[n][:, :].rearrange("p (b n) -> p b n", n=P)).then_inc(on_act, 1)
                return go
            with act.Fori(B_OUT + 1, B_END - 1) as B:
                body(B, row_tiles(B), evacuate=out_evac)
            body(B_END - 1, row_tiles(B_END - 1), evacuate=out_evac)
            act.wait_ge(f_sum, 1)
            act.activation(tiny[:, 0:SB], G[0][:, 0:SB], ACT.Sqrt, bias=eps[:, :],
                           scale=1.0 / D_MODEL).then_inc(f_sqrt, 1)
            act.wait_ge(unit_done, 32 * B_END)
            for t in (2, 6):
                row_tiles(B_END, last=True)(t)

        @block.vector
        def _(dve):
            start_counts(dve, conv, g_lod, g_mul, g_norm, k_lod, l_neg, l_scan, on_dve, pt_lod,
                         q_lod, row_max, x_scl)
            def split(B, k):
                dve.wait_ge(hi_ready, 32 * B + k + 1)
                dve.tensor_tensor(w_lo[:, k % RING, :], w_raw[:, k % RAW, :], f32(w_hi[:, k % RING, :]),
                                  ALU.subtract).then_inc(lo_ready, 1)

            def u_part(k):
                dve.wait_ge(u_split, k + 1)
                r = u_raw[:, k * SEQ:(k + 1) * SEQ]
                dve.tensor_tensor(u_lo[:, k, :], r, f32(u_hi[:, k, :]), ALU.subtract)

            def evac(B, width=SEQ):
                for n in (1, 3):
                    if n == 1:
                        dve.wait_ge(tile_done, 3 * B + n + 1)
                    else:
                        dve.wait_ge(unit_done, 32 * B + 32)
                    dve.tensor_copy(stage[:, n, 0:width], G[n][:, 0:width]).then_inc(dve_evac, 1)

            def body(B, side=None, before=None, evacuate=evac):
                for j in range(LEAD, KT + LEAD):
                    b, k = (B, j) if j < KT else (B + 1, j - KT)
                    if before:
                        before(j)
                    if not (isinstance(B, int) and B == B_END - 1 and j >= KT):
                        split(b, k)
                    if side:
                        side(j - LEAD)
                evacuate(B)

            def proj_evac(B, width=SEQ):
                dve.wait_ge(proj_stored, 64 * B)
                evac(B, width)

            dve.memset(ones[:, :], 1.0).then_inc(memset_done, 1)
            dve.memset(eps[:, :], EPS).then_inc(memset_done, 1)
            for b in range(MB):
                dve.wait_ge(mem_in[b], 32)
                for c in range(8):
                    dve.bn_stats(m_bn[:, b, 6 * c:6 * c + 6], mem_rows[:, b, c * 512:(c + 1) * 512])\
                       .then_inc(m_stat, 1)
            dve.wait_ge(m_stat, 16)
            for b in range(MB):
                dve.bn_aggr(m_mv[:, b, :], m_bn[:, b, :]).then_inc(m_stat, 1)
            dve.wait_ge(m_stat, 18)
            dve.tensor_tensor(m_mv[:, :, 0], m_mv[:, :, 0], m_mv[:, :, 0], ALU.mult).then_inc(m_stat, 1)
            dve.wait_ge(m_stat, 19)
            dve.scalar_tensor_tensor(m_mv[:, :, 1], m_mv[:, :, 1], EPS, m_mv[:, :, 0], ALU.add, ALU.add)\
               .then_inc(m_stat, 1)
            dve.wait_ge(m_sqrt, 1)
            dve.reciprocal(m_rstd[:, :], m_rstd[:, :]).then_inc(m_rs, 1)
            dve.wait_ge(m_rs, 1)

            def m_scale(t):
                if t >= KT:
                    return
                if t >= 2:
                    dve.wait_ge(m_trd, t - 1)
                dve.tensor_tensor(m_scaled[:, t % 2, :].rearrange("p (b n) -> p b n", n=P),
                                  mem_rows[:, :, t * P:(t + 1) * P],
                                  m_rstd[:, :].unsqueeze(2).to_broadcast([P, MB, P]), ALU.mult).then_inc(m_scl, 1)

            def m_part(t):
                dve.wait_ge(m_hid, t + 1)
                dve.scalar_tensor_tensor(m_lo[:, t, :], X[t % 4][:, 0:N_MEM], gains[:, G_MEM + t:G_MEM + t + 1],
                                         f32(m_hi[:, t, :]), ALU.mult, ALU.subtract).then_inc(m_lod, 1)
            m_scale(0)
            m_scale(1)
            for k in range(LEAD):
                m_scale(k + 2)
                m_part(k)
                split(0, k)

            def first_parts(j):
                m_scale(j + 2)
                if j < KT:
                    m_part(j)

            def x_stats(t):
                if t == KT - 1:
                    dve.wait_ge(x_sq, 16)
                    dve.reduce_sum(x_rstd[:, :], x_ss[:, :, :], AX.X).then_inc(x_sum, 1)
                    dve.wait_ge(x_sum, 1)
                    dve.tensor_scalar(x_rstd[:, :], x_rstd[:, :], 1.0 / D_MODEL, EPS, ALU.mult, ALU.add)\
                       .then_inc(x_sum, 1)
                    dve.wait_ge(x_sqrt, 1)
                    dve.reciprocal(x_rstd[:, :], x_rstd[:, :]).then_inc(x_rs, 1)
                    dve.wait_ge(x_rs, 1)
            body(0, x_stats, first_parts, lambda B: proj_evac(B, N_MEM))

            with dve.Fori(1, 3) as B:
                def x_scale(t):
                    if t % 2 == 0:
                        e = t // 2
                        kt = 16 * (B - 1) + e
                        c = e // 2
                        dve.wait_ge(chunk_in[c % 2], 64 * B - 64 + 16 * (c // 2) + 16)
                        dve.wait_ge(x_trd, FIRST + 16 * (B - 1) + max(e - 1, 0))
                        dve.tensor_tensor(x_scaled[:, e % 2, :, :], x_chunk[:, c % 2, :, (e % 2) * P:(e % 2 + 1) * P],
                                          x_rstd[:, :].unsqueeze(2).to_broadcast([P, SB, P]), ALU.mult)\
                           .then_inc(x_scl, 1)
                body(B, x_scale, evacuate=lambda B: proj_evac(B, N_MEM))
            body(3, before=lambda j: u_part(j - KT) if j >= KT else None,
                 evacuate=lambda B: proj_evac(B, N_MEM))
            body(B_K, before=lambda j: u_part(j) if j < KT else None, evacuate=proj_evac)

            halves = [(i + ROT // 2) % ROT for i in range(ROT)]

            def rope_swap(B, r, t):
                n = t - 1
                if 0 <= n < NT:
                    dve.wait_ge(act_evac if n % 2 == 0 else dve_evac, 2 * (B - 1) + n // 2 + 1)
                    dve.wait_ge(rope_done, 4 * r + n)
                    dve.sem_inc(passed_dve, 1)
                    dve.stream_shuffle(rot[:, :], stage[0:ROT, n, :], halves).then_inc(swapped, 1)

            cd = [0]

            def step(ins):
                cd[0] += 1
                ins.then_inc(cd_dve, 1)
                dve.wait_ge(cd_dve, cd[0])

            def decay(t):
                lam_c = par[:, C_LAM:C_LAM + 16]
                e, z, z2, s = (tiny[:, 16 * i:16 * i + 16] for i in range(3)) if False else (
                    tiny[:, 0:16], tiny[:, 16:32], tiny[:, 32:48], cdec[:, :])
                if t == 10:
                    dve.wait_ge(par_ready, 2)
                    step(dve.tensor_scalar(s, lam_c, -1.0, None, ALU.mult))
                    step(dve.tensor_tensor(e, lam_c, s, ALU.max))
                if t == 16:
                    dve.wait_ge(cd_act, 1)
                    step(dve.tensor_scalar(z, e, 2.0, None, ALU.add))
                    step(dve.reciprocal(z, z))
                    step(dve.tensor_tensor(z, z, e, ALU.mult))
                    step(dve.tensor_tensor(z2, z, z, ALU.mult))
                    step(dve.tensor_scalar(e, z2, 1.0 / 19, 1.0 / 17, ALU.mult, ALU.add))
                if 17 <= t < 25:
                    n = 15 - 2 * (t - 17)
                    step(dve.tensor_tensor(e, e, z2, ALU.mult))
                    step(dve.tensor_scalar(e, e, 1.0 / n, None, ALU.add))
                if t == 25:
                    step(dve.tensor_tensor(e, e, z, ALU.mult))
                    step(dve.tensor_scalar(s, s, 0.0, None, ALU.max))
                    step(dve.scalar_tensor_tensor(s, e, 2.0, s, ALU.mult, ALU.add))
                    step(dve.tensor_scalar(s, s, -LRU_C, None, ALU.mult))

            def value_side(t):
                rope_swap(B_V, 0, t)
                decay(t)
            body(B_V, value_side, evacuate=proj_evac)
            body(B_Q, evacuate=proj_evac)
            body(B_Q + 1, lambda t: rope_swap(B_Q + 1, 1, t), evacuate=proj_evac)

            def attention(B, rope):
                g = B - B_ATT

                def go(t):
                    if rope:
                        rope_swap(B, g + 2, t)
                    if t == 0:
                        dve.wait_ge(k_hid, g + 1)
                        dve.tensor_tensor(k_lo[:, :], k_raw[:, :], f32(k_hi[:, :]), ALU.subtract).then_inc(k_lod, 1)
                        dve.wait_ge(const_in, 48)
                        dve.tensor_copy(sink4[:, :], sinks[:, bass.ds(4 * g, 4)]).then_inc(sink_set, 1)
                    if t == 2:
                        dve.wait_ge(v_hid, g + 1)
                        dve.tensor_tensor(v_lo[:, :], X[2][:, :], f32(v_hi[:, :]), ALU.subtract).then_inc(v_lod, 1)
                    for i, s in enumerate(HEAD_AT):
                        h = 4 * g + i
                        if t == s:
                            dve.wait_ge(q_hid, h + 1)
                            dve.tensor_tensor(q_lo[:, :], q_raw[:, :], f32(q_hi[:, :]), ALU.subtract)\
                               .then_inc(q_lod, 1)
                        for pair in range(2):
                            if t == s + 3 + 3 * pair:
                                for b in (2 * pair, 2 * pair + 1):
                                    nk = BAND[b][1]
                                    dve.wait_ge(pt_hid, 4 * h + b + 1)
                                    slots = slice(PT_FIRST[b], PT_FIRST[b] + 2 * nk - 1, 2)
                                    dve.tensor_tensor(pt_lo[:, slots, :],
                                                      X[2 + b % 2][:, 0:nk * P].rearrange("p (j q) -> p j q", q=P),
                                                      f32(pt_hi[:, slots, :]), ALU.subtract).then_inc(pt_lod, 1)
                            if t == s + 1 + 3 * pair - pair:
                                sk = sink4[:, i:i + 1]
                                dve.wait_ge(sink_set, g + 1)
                                for e in range(2):
                                    b = 2 * pair + e
                                    k0, nk = BAND[b]
                                    m0 = (k0 - b + 1) * P
                                    dve.wait_ge(scored, FIRST + 4 * h + b + 1)
                                    if pair:
                                        dve.wait_ge(p_trd, FIRST + 4 * h + b - 1)
                                    else:
                                        dve.wait_ge(p_trd, FIRST + 4 * h)
                                    dve.sem_inc(passed_dve, 1)
                                    dve.tensor_tensor_reduce(probs[:, e, 0:nk * P], X[b % 2][:, 0:nk * P],
                                                             mask[:, m0:m0 + nk * P], ATT_SCALE, sk, ALU.add,
                                                             ALU.max, srow[:, e:e + 1]).then_inc(row_max, 1)
                                dve.wait_ge(row_max, FIRST + 4 * h + 2 * pair + 2)
                                dve.tensor_scalar(srow[:, 4:6], srow[:, 0:2], -1.0, None, ALU.mult)\
                                   .then_inc(max_neg, 1)
                                dve.wait_ge(max_neg, 2 * h + pair + 1)
                                dve.tensor_scalar(srow[:, 12:14], srow[:, 4:6], sk, None, ALU.add)\
                                   .then_inc(sink_diff, 1)
                            if t == s + 2 + 3 * pair:
                                dve.wait_ge(exped, 4 * h + 2 * pair + 2)
                                dve.wait_ge(sink_exp, 2 * h + pair + 1)
                                dve.tensor_tensor(srow[:, 18:20], srow[:, 8:10], srow[:, 16:18], ALU.add)\
                                   .then_inc(denom, 1)
                                dve.wait_ge(denom, 2 * h + pair + 1)
                                dve.reciprocal(srow[:, 20:22], srow[:, 18:20]).then_inc(recip, 1)
                                dve.wait_ge(recip, 2 * h + pair + 1)
                                for e in range(2):
                                    pr = probs[:, e, 0:BAND[2 * pair + e][1] * P]
                                    dve.tensor_scalar(pr, pr, srow[:, 20 + e:21 + e], None, ALU.mult)\
                                       .then_inc(normed, 1)
                return go
            with dve.Fori(B_ATT, B_LRU - 1) as B:
                body(B, attention(B, True), evacuate=proj_evac)
            body(B_LRU - 1, attention(B_LRU - 1, False), evacuate=proj_evac)

            with dve.Fori(B_LRU, B_MEMATT) as B:
                def lru(t):
                    for i, s in enumerate(TILE_AT):
                        T = 4 * (B - B_LRU) + i
                        if t == s + 8:
                            for d in range(2):
                                dve.wait_ge(l_b, FIRST + 2 * T + d + 1)
                                o, a, v = l_h[:, d, :], l_a[:, d, :], l_n[:, d, :]
                                if d == 0:
                                    dve.tensor_tensor_scan(o, a, v, 0.0, ALU.mult, ALU.add).then_inc(l_scan, 1)
                                else:
                                    dve.tensor_tensor_scan(o[:, ::-1], a[:, ::-1], v[:, ::-1], 0.0, ALU.mult,
                                                           ALU.add).then_inc(l_scan, 1)
                            dve.wait_ge(l_scan, FIRST + 2 * T + 2)
                            dve.wait_ge(y_stored, 16 * (16 + T))
                            dve.wait_ge(y_sq, FIRST + 16 + T)
                            dve.tensor_tensor(l_y[:, :], l_h[:, 0, :], l_h[:, 1, :], ALU.add).then_inc(l_sum, 1)
                    for i, s in enumerate(TILE_AT):
                        T = 4 * (B - B_LRU) + i
                        if t == s:
                            dve.wait_ge(l_xin, 16 * T + 16)
                            dve.wait_ge(l_mm, FIRST + 4 * T)
                            dve.wait_ge(l_ix, FIRST + 2 * T)
                            dve.tensor_scalar(xc[:, :], l_in[:, 0:SEQ], par[:, bass.ds(T + C_CONVW, 1)],
                                              par[:, bass.ds(T + C_CONVB, 1)], ALU.mult, ALU.add).then_inc(conv, 1)
                            for j in range(1, 4):
                                dve.wait_ge(conv, FIRST + 4 * T + j)
                                dve.scalar_tensor_tensor(xc[:, :], l_in[:, j:j + SEQ],
                                                         par[:, bass.ds(T + (C_CONVW + 8 * j), 1)], xc[:, :],
                                                         ALU.mult, ALU.add).then_inc(conv, 1)
                        if t == s + 5:
                            for d in range(2):
                                dve.wait_ge(l_asq, 2 * T + d + 1)
                                dve.wait_ge(l_exp, 4 * T + 2 * d + 2)
                                dve.scalar_tensor_tensor(l_n[:, d, :], l_n[:, d, :], 1.0, l_t[:, d, :], ALU.add,
                                                         ALU.mult).then_inc(l_neg, 1)
                body(B, lru, evacuate=proj_evac)

            def hold(B):
                for n in range(NT):
                    dve.wait_ge(sig_done, 4 * (B - B_Z) + n + 1)
                    dve.tensor_tensor(stage[:, n, :], stage[:, n, :], G[n][:, :], ALU.mult).then_inc(z_held, 1)

            def rms(which):
                dve.wait_ge(r_sqrt, which + 1)
                dve.reciprocal(r_bc[:, which, :], r_bc[:, which, :]).then_inc(r_ready, 1)

            def mem_attention(t):
                if t == 0:
                    rms(0)
                    rms(1)
                for h, s in enumerate(MEMHEAD_AT):
                    if t == s + 1:
                        dve.wait_ge(mk_hid, h + 1)
                        dve.tensor_tensor(mk_lo[:, :], mk_raw[:, :], f32(mk_hi[:, :]), ALU.subtract)\
                           .then_inc(mk_lod, 1)
                        dve.wait_ge(mv_hid, h + 1)
                        dve.tensor_tensor(mv_lo[:, :], X[2][:, :], f32(mv_hi[:, :]), ALU.subtract)\
                           .then_inc(mv_lod, 1)
                    for d in range(2):
                        if t == s + 1 + 2 * d:
                            dve.wait_ge(mq_hid, 2 * h + d + 1)
                            dve.tensor_tensor(mq_lo[:, d, :], mq_raw[:, :], f32(mq_hi[:, d, :]), ALU.subtract)\
                               .then_inc(mq_lod, 1)
                    if t == s + 4:
                        for i in range(2):
                            dve.wait_ge(m_scored, 2 * h + i + 1)
                            dve.reduce_max(mrow[:, 2 * i:2 * i + 2],
                                           X[i][:, :].rearrange("p (b m) -> p b m", b=2), AX.X).then_inc(m_max, 1)
                            dve.wait_ge(m_max, 2 * h + i + 1)
                            dve.tensor_scalar(mrow[:, 4 + 2 * i:6 + 2 * i], mrow[:, 2 * i:2 * i + 2], -MEM_SCALE,
                                              None, ALU.mult).then_inc(m_neg, 1)
                    if t == s + 6:
                        dve.wait_ge(m_exp, SB * h + SB)
                        dve.reciprocal(mrow[:, 12:16], mrow[:, 8:12]).then_inc(m_rec, 1)
                        dve.wait_ge(m_rec, h + 1)
                        for i in range(SB):
                            dve.tensor_scalar(mp[:, i, :], mp[:, i, :], mrow[:, 12 + i:13 + i], None, ALU.mult)\
                               .then_inc(m_norm, 1)
                    if t == s + 7:
                        for b in range(MB):
                            dve.wait_ge(mp_hid, 2 * h + b + 1)
                            dve.tensor_tensor(mpt_lo[:, b, :], X[2 + b][:, :], f32(mpt_hi[:, b, :]), ALU.subtract)\
                               .then_inc(mp_lod, 1)
            body(B_MEMATT, mem_attention, evacuate=hold)

            def gates(B, which, late=None):
                def go(t):
                    if late:
                        late(t)
                    if t >= 5 and t < 5 + 2 * NT:
                        n = (t - 5) // 2
                        at_g = 4 * (B - 1 - B_Z) + n
                        if t % 2 == 1:
                            dve.wait_ge(gy_in[n], 16 * (B - B_Z))
                            dve.wait_ge(r_ready, which + 1)
                            dve.scalar_tensor_tensor(g_y[:, n, :], g_y[:, n, :],
                                                     gains[:, bass.ds(at_g + G_OUT, 1)] if not isinstance(B, int)
                                                     else gains[:, at_g + G_OUT:at_g + G_OUT + 1],
                                                     r_bc[:, which, :], ALU.mult, ALU.mult).then_inc(g_norm, 1)
                            dve.wait_ge(g_norm, FIRST + at_g + 1)
                            dve.wait_ge(z_held, at_g + 1)
                            dve.tensor_tensor(g_y[:, n, :], g_y[:, n, :], stage[:, n, :], ALU.mult)\
                               .then_inc(g_mul, 1)
                        else:
                            dve.wait_ge(g_hid, at_g + 1)
                            dve.tensor_tensor(g_lo[:, n % 2, :], g_y[:, n, :], f32(g_hi[:, n % 2, :]),
                                              ALU.subtract).then_inc(g_lod, 1)
                return go
            body(B_Z + 1, gates(B_Z + 1, 0, lambda t: rms(2) if t == 2 else None), evacuate=hold)
            with dve.Fori(B_Z + 2, B_Z + 5) as B:
                body(B, gates(B, 0), evacuate=hold)
            with dve.Fori(B_Z + 5, B_Z + 7) as B:
                body(B, gates(B, 1), evacuate=hold)
            body(B_OUT - 1, gates(B_OUT - 1, 2), evacuate=hold)

            def out_evac(B):
                dve.wait_ge(o_gain, 4 * (B - B_OUT))
                dve.wait_ge(o_sq, 4 * (B - B_OUT))
                evac(B)
            body(B_OUT, gates(B_OUT, 2), evacuate=out_evac)

            def out_gain(B, n):
                at_o = 4 * (B - 1 - B_OUT) + n
                if n % 2:
                    dve.wait_ge(dve_evac, 2 * (B - 1 - GATED) + n // 2 + 1)
                else:
                    dve.wait_ge(act_evac, 2 * (B - 1 - GATED) + n // 2 + 1)
                dve.wait_ge(o_trd, FIRST + 4 * (B - 1 - B_OUT) + max(n - 1, 0))
                dve.tensor_scalar(og[:, n % 2, :], stage[:, n, :], gains[:, bass.ds(at_o + G_POST, 1)]
                                  if not isinstance(B, int) else gains[:, at_o + G_POST:at_o + G_POST + 1],
                                  None, ALU.mult).then_inc(o_gain, 1)

            def row_tile(B, n, last=False):
                dve.wait_ge(o_trd, FIRST + 4 * (B - 1 - B_OUT) + n + 1)
                if last:
                    o = o_fin[:, :, 7 * BW + n * P:7 * BW + (n + 1) * P]
                else:
                    dve.wait_ge(o_free, FIRST + B - 1 - B_OUT)
                    o = o_nat[:, :, n * P:(n + 1) * P]
                dve.tensor_copy(o, X[n][:, :].rearrange("p (b n) -> p b n", n=P)).then_inc(on_dve, 1)

            def out_side(B):
                def go(t):
                    for n in range(NT):
                        if t == 1 + 2 * n:
                            out_gain(B, n)
                        if t == 2 + 2 * n and n % 2:
                            row_tile(B, n)
                return go
            with dve.Fori(B_OUT + 1, B_END - 1) as B:
                body(B, out_side(B), evacuate=out_evac)
            body(B_END - 1, out_side(B_END - 1), evacuate=out_evac)
            for n in range(NT):
                out_gain(B_END, n)
                if n == 2:
                    row_tile(B_END, 1, last=True)
            row_tile(B_END, 3, last=True)
            dve.wait_ge(f_sqrt, 1)
            dve.reciprocal(tiny[:, 16:16 + SB], tiny[:, 0:SB]).then_inc(f_rs, 1)
            dve.wait_ge(f_rs, 1)
            half = D_MODEL // 2
            dve.wait_ge(on_act, FIRST + 16)
            dve.wait_ge(on_dve, FIRST + 16)
            for c in range(SB):
                dve.wait_ge(fin_in[c], 32)
                for h in range(2):
                    cols = slice(h * half, (h + 1) * half)
                    dve.scalar_tensor_tensor(o_fin[:, c, cols], o_fin[:, c, cols], tiny[:, 16 + c:17 + c],
                                             x_fin[:, c, cols], ALU.mult, ALU.add).then_inc(f_done, 1)

        @block.gpsimd
        def _(pool):
            start_counts(pool, l_b, l_ix, o_acc, y_acc, y_free, o_free)
            pool.memset(sq_acc[:, :], 0.0).then_inc(acc_zero, 1)

            def copied(B, n):
                pool.wait_ge(dve_evac if n % 2 else act_evac, 2 * B + n // 2 + 1)

            def store(B, dst, width=SEQ, rope=None):
                if not (isinstance(B, int) and B == 0):
                    pool.wait_ge(proj_stored, 64 * B)
                for n in range(NT):
                    copied(B, n)
                    if rope is not None:
                        r = 4 * rope + n
                        pool.wait_ge(swapped, r + 1)
                        pool.tensor_tensor(rot[:, :], rot[:, :], rope_s[:, :], ALU.mult).then_inc(rope_mul, 1)
                        v = stage[0:ROT, n, :]
                        pool.tensor_tensor(v, v, rope_c[:, :], ALU.mult).then_inc(rope_mul, 1)
                        pool.wait_ge(rope_mul, 2 * r + 2)
                        pool.tensor_tensor(v, v, rot[:, :], ALU.add).then_inc(rope_done, 1)
                        pool.wait_ge(rope_done, r + 1)
                    pool.dma_start(dst(n), stage[:, n, 0:width]).then_inc(proj_stored, 16)

            def kv_rows(B):
                return lambda n: kvT[bass.ds(B * BW + n * P, P), :]

            def proj_rows(B):
                return lambda n: projT[bass.ds((B - 4) * BW + n * P, P), :]

            store(0, kv_rows(0), N_MEM)
            with pool.Fori(1, 4) as B:
                store(B, kv_rows(B), N_MEM)
            pool.wait_ge(rope_in, 32)
            store(B_K, proj_rows(B_K), rope=0)
            store(B_V, proj_rows(B_V))
            store(B_Q, proj_rows(B_Q), rope=1)

            def head_out(h):
                pool.wait_ge(y_out, h + 1)
                pool.dma_start(yT[bass.ds(h * P, P), :], y_sb[:, :]).then_inc(y_stored, 16)
                pool.wait_ge(y_sq, FIRST + h + 1)
                pool.wait_ge(y_acc, FIRST + h)
                pool.tensor_tensor(sq_acc[:, :], sq_acc[:, :], sq_tmp[:, :], ALU.add).then_inc(y_acc, 1)
                pool.wait_ge(y_stored, 16 * h + 16)
                pool.sem_inc(y_free, 1)

            pool.wait_ge(acc_zero, 1)
            with pool.Fori(B_ATT, B_LRU - 1) as B:
                store(B - 1, proj_rows(B - 1), rope=B - B_ATT + 2)
                for i in range(4):
                    head_out(4 * (B - B_ATT) + i)
            store(B_LRU - 2, proj_rows(B_LRU - 2))
            for i in range(4):
                head_out(12 + i)
            pool.memset(r_bc[:, 1:3, :], 0.0).then_inc(l_zero, 1)
            pool.wait_ge(y_stored, 16 * 16)
            pool.memset(l_in[:, 0:2], 0.0)
            pool.memset(l_in[:, SEQ + 2:SEQ + 4], 0.0).then_inc(l_zero, 1)
            pool.wait_ge(l_zero, 2)

            with pool.Fori(B_LRU, B_MEMATT) as B:
                store(B - 1, proj_rows(B - 1))
                for i in range(4):
                    T = 4 * (B - B_LRU) + i
                    for d in range(2):
                        pool.wait_ge(l_sig, FIRST + 4 * T + d + 3)
                        pool.wait_ge(conv, FIRST + 4 * T + 4)
                        pool.tensor_tensor(l_i[:, d, :], l_i[:, d, :], xc[:, :], ALU.mult).then_inc(l_ix, 1)
                    for d in range(2):
                        pool.wait_ge(l_exp, 4 * T + 2 * d + 1)
                        pool.wait_ge(l_scan, FIRST + 2 * T)
                        pool.tensor_tensor(l_n[:, d, :], l_a[:, d, :], l_a[:, d, :], ALU.mult).then_inc(l_asq, 1)
                    for d in range(2):
                        pool.wait_ge(l_mult, 2 * T + d + 1)
                        pool.wait_ge(l_ix, FIRST + 2 * T + d + 1)
                        pool.tensor_tensor(l_n[:, d, :], l_n[:, d, :], l_i[:, d, :], ALU.mult).then_inc(l_b, 1)
                    pool.wait_ge(l_sum, T + 1)
                    pool.dma_start(yT[bass.ds(T * P + 16 * P, P), :], l_y[:, :]).then_inc(y_stored, 16)
                    pool.wait_ge(y_sq, FIRST + 16 + T + 1)
                    pool.wait_ge(y_acc, FIRST + 16 + T)
                    pool.tensor_tensor(r_bc[:, 1, :], r_bc[:, 1, :], sq_tmp[:, :], ALU.add).then_inc(y_acc, 1)

            store(B_MEMATT - 1, proj_rows(B_MEMATT - 1))
            for i in range(8):
                pool.wait_ge(y_out, 16 + i + 1)
                pool.dma_start(yT[(24 + i) * P:(25 + i) * P, :], stage[:, 2, :]).then_inc(y_stored, 16)
                pool.wait_ge(y_sq, FIRST + 24 + i + 1)
                pool.wait_ge(y_acc, FIRST + 24 + i)
                pool.tensor_tensor(r_bc[:, 2, :], r_bc[:, 2, :], sq_tmp[:, :], ALU.add).then_inc(y_acc, 1)

            with pool.Fori(0, 8) as z:
                for n in range(NT):
                    for part, made, dst in ((g_hi, g_hid, gT_hi), (g_lo, g_lod, gT_lo)):
                        pool.wait_ge(made, (FIRST if made is g_lod else 0) + 4 * z + n + 1)
                        pool.sem_inc(passed_pool, 1)
                        pool.dma_start(dst[bass.ds(z * BW + n * P, P), :], f32(part[:, n % 2, :]))\
                            .then_inc(g_stored, 16)
                    pool.wait_ge(g_stored, 128 * z + 32 * n + 32)

            pool.wait_ge(r_sum, 1)
            pool.memset(sq_acc[:, :], 0.0).then_inc(acc_zero, 1)
            pool.wait_ge(acc_zero, 2)

            def squares(o, n):
                pool.wait_ge(dve_evac if n % 2 else act_evac, 2 * (o + B_Z) + n // 2 + 1)
                pool.wait_ge(o_acc, FIRST + 4 * o + n)
                pool.tensor_tensor(sq_tmp[:, :], stage[:, n, :], stage[:, n, :], ALU.mult).then_inc(o_sq, 1)
                pool.wait_ge(o_sq, 4 * o + n + 1)
                pool.tensor_tensor(sq_acc[:, :], sq_acc[:, :], sq_tmp[:, :], ALU.add).then_inc(o_acc, 1)

            with pool.Fori(0, 7) as o:
                for n in range(NT):
                    squares(o, n)
                pool.wait_ge(on_act, FIRST + 2 * o + 2)
                pool.wait_ge(on_dve, FIRST + 2 * o + 2)
                pool.dma_start(o_rows[:, bass.ds(o * BW, BW)].rearrange("(b p) n -> p b n", p=P), o_nat[:, :, :])\
                    .then_inc(o_stored, 16)
                pool.wait_ge(o_stored, 16 * o + 16)
                pool.sem_inc(o_free, 1)
            for n in range(NT):
                squares(7, n)


_INS = ["x", "mem", "pre_norm_gain", "w_in", "att_sink", "conv_w", "conv_b", "lru_w_a", "lru_b_a", "lru_w_x",
        "lru_b_x", "lru_lambda", "mem_norm_gain", "w_mem_kv", "att_out_gain", "lru_out_gain", "mem_out_gain",
        "w_out", "post_norm_gain"]


def shape_constants():
    half = ROT // 2
    inv_freq = np.power(np.float32(500000.0), -np.arange(half, dtype=np.float32) * np.float32(2.0) / np.float32(ROT))
    ang = np.arange(SEQ, dtype=np.float32)[None, :] * inv_freq[:, None]
    cos, sin = np.cos(ang).astype(np.float32), np.sin(ang).astype(np.float32)
    q, k = np.arange(P)[:, None], np.arange(3 * P)[None, :] - P
    return {
        "rope_cos": np.concatenate([cos, cos]),
        "rope_sin": np.concatenate([-sin, sin]),
        "band_mask": np.where(np.abs(k - q) <= P, 0.0, MASKED).astype(np.float32),
        "identity": np.eye(P, dtype=np.float32),
    }


def kernel(**inputs):
    import concourse.bacc as bacc
    from concourse.bass_utils import run_bass_kernel_spmd

    nc = bacc.Bacc("TRN2", target_bir_lowering=False, num_devices=1)
    arrays, args = {}, []
    named = {name: np.ascontiguousarray(inputs[name]) for name in _INS}
    named.update(shape_constants())
    for name, a in named.items():
        arrays[f"in_{name}"] = a
        args.append(nc.dram_tensor(f"in_{name}", a.shape, mybir.dt.from_np(a.dtype), kind="ExternalInput").ap())
    out = nc.dram_tensor("out_0", (1, SEQ, D_MODEL), F32, kind="ExternalOutput").ap()
    hymba(nc, *args, out)
    return run_bass_kernel_spmd(nc, [arrays], core_ids=[0]).results[0]["out_0"]
```

```python
from contextlib import ExitStack, contextmanager

import numpy as np
import concourse.bass as bass
from concourse import mybir

F32 = mybir.dt.float32
F32R = mybir.dt.float32r
ALU = mybir.AluOpType
ACT = mybir.ActivationFunctionType
AX = mybir.AxisListType

P = 128
D_MODEL = 4096
SEQ = 512
N_MEM = 256
EPS = 1e-6
KT = D_MODEL // P
NT = 4
BW = NT * P
SB = SEQ // P
MB = N_MEM // P
HEADS = 16
GROUPS = 4
ATT_SCALE = float(P) ** -0.5
MEM_HEADS = 4
MEM_D = 256
MEM_SCALE = float(MEM_D) ** -0.5
LRU_TILES = 8
LRU_C = 8.0
ROT = 32
MASKED = -1.0e30
FIRST = 1

B_XLRU, B_K, B_V, B_Q, B_QMEM, B_Z, B_OUT, B_END = 4, 6, 7, 8, 12, 14, 22, 30
B_LRU, B_ATT, B_MEMATT = 6, 10, 14
RAW = 4
MEM_RAW = 8
B_MEM_END = 4
RING = 4
LEAD = 3
HEAD_AT = (1, 8, 15, 22)
SWAP_AT = (1, 4, 12, 18)
TILE_AT = (0, 16)
MEMHEAD_AT = (1, 8, 15, 22)
BAND = [(max(i - 1, 0), min(i + 1, SB - 1) - max(i - 1, 0) + 1) for i in range(SB)]
PT_FIRST = (0, 1, 4, 7)
PT_AT = (0, 2, 5, 8)
G_MEM, G_PRE, G_OUT, N_GAINS = 0, 32, 64, 96
PAR = 88
C_CONVW, C_CONVB, C_BA, C_BX, C_LAM = 0, 32, 40, 56, 72


def hymba(nc, x, mem, pre_g, w_in, sink, conv_w, conv_b, w_a, b_a, w_x, b_x, lam, mem_g, w_mem,
          g_att, g_lru, g_mem, w_out, post_g, rope_cos, rope_sin, band_mask, identity, out):
    ctx = ExitStack()
    with ctx:
        def sem(name):
            return ctx.enter_context(nc.semaphore(name))

        used = {}

        def at(offset, name, shape, dt=F32):
            used[name] = offset + 32 * ((int(np.prod(shape[1:])) + 7) // 8)
            return nc.alloc_sbuf_tensor_at(name, shape, dt, offset=offset)

        class Region:
            def __init__(self, start, end):
                self.now, self.end = start, end

            def __call__(self, name, shape, dt=F32):
                t = at(self.now, name, shape, dt)
                self.now = used[name]
                assert self.now <= self.end, (name, self.now, self.end)
                return t

        HI = 32 * ((nc.sbuf_base + 31) // 32)
        LO = HI + KT * SEQ * 4
        u_hi = at(HI, "u_hi", [P, KT, SEQ], F32R)
        u_lo = at(LO, "u_lo", [P, SB, D_MODEL], F32R)
        x_rows = at(LO, "x_rows", [P, SB, D_MODEL])
        m_hi = at(HI, "m_hi", [P, KT, N_MEM], F32R)
        m_lo = at(HI + KT * N_MEM * 4, "m_lo", [P, KT, N_MEM], F32R)
        y_hi = at(HI, "y_hi", [P, KT, SEQ], F32R)
        y_lo = at(LO, "y_lo", [P, SB, D_MODEL], F32R)
        mem_rows = at(LO + 2 * D_MODEL * 4, "mem_rows", [P, MB, D_MODEL])
        x_fin = at(HI, "x_fin", [P, SB, D_MODEL])
        o_fin = at(LO, "o_fin", [P, SB, D_MODEL])

        top = nc.sbuf_usable_end
        W = Region(LO + KT * SEQ * 4, top)
        w_raw = W("w_raw", [P, RAW, BW])
        w_hi = W("w_hi", [P, RING, BW], F32R)
        w_lo = W("w_lo", [P, RING, BW], F32R)
        ident = W("ident", [P, P])
        ones = W("ones", [P, P])
        mask = W("mask", [P, 3 * P])
        gains = W("gains", [P, N_GAINS])
        par = W("par", [P, PAR])
        sinks = W("sinks", [P, HEADS])
        eps = W("eps", [P, 1])
        cdec = W("cdec", [P, 2 * LRU_TILES])
        tiny = W("tiny", [P, 48])
        stage = W("stage", [P, NT, SEQ])
        sq_acc = W("sq_acc", [P, SEQ])
        sq_tmp = W("sq_tmp", [P, SEQ])
        at_side = W.now

        R = Region(at_side, top)
        par_rows = R("par_rows", [P, 2, P])
        m_bn = R("m_bn", [P, MB, 8 * 6])
        m_mv = R("m_mv", [P, MB, 2])
        m_rstd = R("m_rstd", [P, MB])
        m_diag = R("m_diag", [P, MB, P])
        x_ss = R("x_ss", [P, SB, 4])
        x_rstd = R("x_rstd", [P, SB])
        x_sqs = R("x_sqs", [P, D_MODEL // 4])
        R.now = at_side + 20480
        m_rms = R("m_rms", [P, N_MEM])
        w_more = R("w_more", [P, MEM_RAW - RAW, BW])

        R = Region(at_side, top)
        r_bc = R("r_bc", [P, 3, SEQ])
        at_late = R.now
        rope_c = R("rope_c", [ROT, SEQ])
        rope_s = R("rope_s", [ROT, SEQ])
        rot = R("rot", [ROT, SEQ])
        at_mixer = R.now

        R = Region(at_mixer, top)
        l_in = R("l_in", [P, SEQ + 4])
        l_w = R("l_w", [P, 2, 2, P])
        xc = R("xc", [P, SEQ])
        l_r = R("l_r", [P, 2, SEQ])
        l_i = R("l_i", [P, 2, SEQ])
        l_a = R("l_a", [P, 2, SEQ])
        l_t = R("l_t", [P, 2, SEQ])
        l_n = R("l_n", [P, 2, SEQ])
        l_h = l_t
        l_y = R("l_y", [P, SEQ])

        R = Region(at_mixer, top)
        q_at, k_at, v_at = R.now, R.now + SEQ * 4, R.now + SEQ * 8
        q_raw = R("q_raw", [P, SEQ])
        k_raw = R("k_raw", [P, SEQ])
        v_raw = R("v_raw", [P, SEQ])
        q_lo = at(q_at, "q_lo", [P, SEQ], F32R)
        k_lo = at(k_at, "k_lo", [P, SEQ], F32R)
        v_lo = at(v_at, "v_lo", [P, SEQ], F32R)
        R.now += 32
        sink4 = R("sink4", [P, 4])
        srow = R("srow", [P, 24])
        q_hi = R("q_hi", [P, SEQ], F32R)
        k_hi = R("k_hi", [P, SEQ], F32R)
        v_hi = R("v_hi", [P, SEQ], F32R)
        probs = R("probs", [P, 2, 3 * P])
        pt_hi = R("pt_hi", [P, 10, P], F32R)
        pt_lo = R("pt_lo", [P, 10, P], F32R)
        y_sb = R("y_sb", [P, SEQ])

        R = Region(at_late, top)
        mq_raw = R("mq_raw", [P, 2, SEQ])
        mk_raw = R("mk_raw", [P, 2 * N_MEM])
        mq_lo = at(at_late, "mq_lo", [P, 2, SEQ], F32R)
        mk_lo = at(at_late + 2 * SEQ * 4, "mk_lo", [P, 2 * N_MEM], F32R)
        assert R.now == at_mixer
        mv_raw = R("mv_raw", [P, 2 * N_MEM])
        mrow = R("mrow", [P, 16])
        mq_hi = R("mq_hi", [P, 2, SEQ], F32R)
        mk_hi = R("mk_hi", [P, 2 * N_MEM], F32R)
        mv_hi = R("mv_hi", [P, MB * MEM_D], F32R)
        mv_lo = R("mv_lo", [P, MB * MEM_D], F32R)
        mp = R("mp", [P, SB, N_MEM])
        mpt_hi = R("mpt_hi", [P, MB, SEQ], F32R)
        m_y = R("m_y", [P, 2, SEQ])
        mpt_lo = R("mpt_lo", [P, MB, SEQ], F32R)

        R = Region(at_late, top)
        g_y = R("g_y", [P, NT, SEQ])
        g_hi = R("g_hi", [P, 2, SEQ], F32R)
        g_lo = R("g_lo", [P, 2, SEQ], F32R)
        o_buf = R("o_buf", [P, 2, SB, BW])
        post_row = R("post_row", [P, BW])
        o_ss = R("o_ss", [P, SB, 8])
        x_end = at(at_late, "x_end", [P, D_MODEL // 2])

        G = [ctx.enter_context(nc.psum_tensor(f"gemm{n}", [P, SEQ], F32)) for n in range(NT)]
        X = [ctx.enter_context(nc.psum_tensor(f"side{n}", [P, SEQ], F32)) for n in range(4)]

        def scratch(name, shape, dt=F32):
            return nc.dram_tensor(name, shape, dt, kind="Internal").ap()

        kvT = scratch("kvT", [4 * BW, N_MEM])
        projT = scratch("projT", [10 * BW, SEQ])
        yT = scratch("yT", [D_MODEL, SEQ])
        gT_hi = scratch("gT_hi", [D_MODEL, SEQ])
        gT_lo = scratch("gT_lo", [D_MODEL, SEQ])
        o_rows = scratch("o_rows", [SEQ, D_MODEL])

        raw_in = [sem(f"raw_in{s}") for s in range(MEM_RAW)]
        hi_ready, lo_ready, unit_done = sem("hi_ready"), sem("lo_ready"), sem("unit_done")
        tile_done, act_evac, dve_evac = sem("tile_done"), sem("act_evac"), sem("dve_evac")
        sig_done, z_held = sem("sig_done"), sem("z_held")
        proj_stored, y_stored, g_stored = sem("proj_stored"), sem("y_stored"), sem("g_stored")
        ident_in, const_in, gain_in, par_in = (sem(n) for n in ("ident_in", "const_in", "gain_in", "par_in"))
        par_tr, par_ready = sem("par_tr"), sem("par_ready")
        memset_done, rope_in, cd_dve, cd_act = (sem(n) for n in ("memset_done", "rope_in", "cd_dve", "cd_act"))
        mem_in = [sem(f"mem_in{i}") for i in range(4)]
        m_stat, m_sqrt, m_rs, m_spread = sem("m_stat"), sem("m_sqrt"), sem("m_rs"), sem("m_spread")
        m_rms_set, kv_scaled = sem("m_rms_set"), sem("kv_scaled")
        m_trd, m_hid, m_lod = (sem(n) for n in ("m_trd", "m_hid", "m_lod"))
        xrow_in = [sem(f"xrow_in{i}") for i in range(SB)]
        x_sq, x_sum, x_sqrt, x_rs = (sem(n) for n in ("x_sq", "x_sum", "x_sqrt", "x_rs"))
        x_scl, x_trd, x_ev, u_split = (sem(n) for n in ("x_scl", "x_trd", "x_ev", "u_split"))
        swapped, rope_mul, rope_done = sem("swapped"), sem("rope_mul"), sem("rope_done")
        q_in, k_in, v_in = sem("q_in"), sem("k_in"), sem("v_in")
        q_hid, q_lod, k_hid, k_lod = (sem(n) for n in ("q_hid", "q_lod", "k_hid", "k_lod"))
        v_trd, v_hid, v_lod = sem("v_trd"), sem("v_hid"), sem("v_lod")
        scored, row_max, max_neg, sink_diff = (sem(n) for n in ("scored", "row_max", "max_neg", "sink_diff"))
        sink_set = sem("sink_set")
        exped, sink_exp, denom, recip, normed = (sem(n) for n in ("exped", "sink_exp", "denom", "recip", "normed"))
        p_trd, pt_hid, pt_lod, pv_done = (sem(n) for n in ("p_trd", "pt_hid", "pt_lod", "pv_done"))
        y_out, y_sq, y_acc, y_free = sem("y_out"), sem("y_sq"), sem("y_acc"), sem("y_free")
        l_zero, l_xin, l_win, conv = (sem(n) for n in ("l_zero", "l_xin", "l_win", "conv"))
        l_mm, l_sig, l_exp, l_asq, l_ix = (sem(n) for n in ("l_mm", "l_sig", "l_exp", "l_asq", "l_ix"))
        l_neg, l_mult, l_b, l_scan, l_sum = (sem(n) for n in ("l_neg", "l_mult", "l_b", "l_scan", "l_sum"))
        mq_in, mk_in, mv_in = sem("mq_in"), sem("mk_in"), sem("mv_in")
        mq_hid, mq_lod, mk_hid, mk_lod = (sem(n) for n in ("mq_hid", "mq_lod", "mk_hid", "mk_lod"))
        mv_trd, mv_hid, mv_lod = sem("mv_trd"), sem("mv_hid"), sem("mv_lod")
        m_scored, m_max, m_neg, m_exp, m_rec, m_norm = (
            sem(n) for n in ("m_scored", "m_max", "m_neg", "m_exp", "m_rec", "m_norm"))
        mp_trd, mp_hid, mp_lod, m_pv, my_sq = (sem(n) for n in ("mp_trd", "mp_hid", "mp_lod", "m_pv", "my_sq"))
        r_sum, r_sqrt, r_ready = sem("r_sum"), sem("r_sqrt"), sem("r_ready")
        gy_in = [sem(f"gy_in{n}") for n in range(NT)]
        g_norm, g_mul, g_hid, g_lod = (sem(n) for n in ("g_norm", "g_mul", "g_hid", "g_lod"))
        y_in = [sem(f"y_in{i}") for i in range(4)]
        acc_zero, post_in, o_sq, o_out = (sem(n) for n in ("acc_zero", "post_in", "o_sq", "o_out"))
        o_stored, o_free = sem("o_stored"), sem("o_free")
        passed = sem("passed")
        fin_in, last_in = sem("fin_in"), sem("last_in")
        f_sum, f_sqrt, f_rs, f_done, stored = (sem(n) for n in ("f_sum", "f_sqrt", "f_rs", "f_done", "stored"))

        block = ctx.enter_context(nc.Block())

        def f32(ap):
            return ap.bitcast(F32)

        def u_lo_tile(k):
            return u_lo[:, :, k * P:(k + 1) * P]

        def y_lo_tile(k):
            return y_lo[:, :, k * P:(k + 1) * P]

        def column(tile, i):
            return tile[:, i:i + 1] if isinstance(i, int) else tile[:, bass.ds(i, 1)]

        def m_lo_tile(k):
            return m_lo[:, k, :]

        def raw_slot(B, k, mem=False):
            if mem or (isinstance(B, int) and B < B_MEM_END):
                i = k % MEM_RAW
                return (w_raw[:, i, :] if i < RAW else w_more[:, i - RAW, :]), raw_in[i], \
                    16 * (KT // MEM_RAW * B + k // MEM_RAW + 1)
            before = B_MEM_END * KT // MEM_RAW
            return w_raw[:, k % RAW, :], raw_in[k % RAW], \
                16 * (KT // RAW * B + (before - B_MEM_END * KT // RAW + k // RAW + 1))

        def start_counts(eng, *sems):
            for s in sems:
                eng.sem_inc(s, FIRST)

        GATED = B_OUT - B_Z

        @block.sync
        def _(sp):
            half = D_MODEL // 2
            rows = lambda v: v.rearrange("a (t p) -> (a t) p", p=P)

            def mem_load(c):
                sp.dma_start(mem_rows[:, :, c * 512:(c + 1) * 512],
                             mem[0, :, c * 512:(c + 1) * 512].rearrange("(b p) n -> p b n", p=P)).then_inc(mem_in[c % 4], 16)

            mem_load(0)
            sp.dma_start(ident[:, :], identity).then_inc(ident_in, 16)
            for at_row, v in ((G_MEM, mem_g), (G_PRE, pre_g), (G_OUT, g_att), (G_OUT + 16, g_lru),
                              (G_OUT + 24, g_mem)):
                n = v.shape[1] // P
                sp.dma_start(par_rows[at_row:at_row + n, 0, :], rows(v)).then_inc(gain_in, 16)

            def x_load(b, h):
                cols = slice(h * half, (h + 1) * half)
                sp.dma_start(x_rows[:, b, cols], x[0, b * P:(b + 1) * P, cols]).then_inc(xrow_in[b], 16)

            def weights(B, k, src, mem=False):
                place, loaded, _ = raw_slot(B, k, mem)
                if mem or (isinstance(B, int) and 32 * B + k < 32 * B_MEM_END + RAW):
                    if not (isinstance(B, int) and 32 * B + k < MEM_RAW):
                        sp.wait_ge(lo_ready, 32 * B + k - MEM_RAW + 1)
                else:
                    sp.wait_ge(lo_ready, 32 * B + k - RAW + 1)
                sp.dma_start(place, src).then_inc(loaded, 16)

            def w_block(B, mat, col, at_unit=None, mem=False):
                for k in range(KT):
                    if at_unit and mem:
                        at_unit(k)
                    weights(B, k, mat[0, k * P:(k + 1) * P, bass.ds(col * BW, BW)], mem)
                    if at_unit and not mem:
                        at_unit(k)

            def first_rows(k):
                for c in range(1, 8):
                    if k == max(4 * c - 5, 1):
                        mem_load(c)
                for i in range(4):
                    if k == 13 + 4 * i:
                        x_load(i // 2, i % 2)
                if k == 30:
                    for at_row, v in ((C_CONVW, conv_w.rearrange("a j c -> (a j) c")), (C_CONVB, conv_b),
                                      (C_BA, b_a.rearrange("a d c -> (a d) c")),
                                      (C_BX, b_x.rearrange("a d c -> (a d) c")),
                                      (C_LAM, lam.rearrange("a d c -> (a d) c"))):
                        n = v.shape[0] * v.shape[1] // P
                        sp.dma_start(par_rows[at_row:at_row + n, 1, :], rows(v)).then_inc(par_in, 16)
            w_block(0, w_mem, 0, first_rows, mem=True)

            def second_rows(k):
                for i in range(4):
                    if k == 8 + 3 * i:
                        if i == 0:
                            sp.wait_ge(m_trd, KT)
                            sp.wait_ge(m_stat, 16)
                        x_load(2 + i // 2, i % 2)
                if k == 24:
                    sp.dma_start(mask[:, :], band_mask).then_inc(const_in, 16)
                    sp.dma_start(sinks[:, :], sink.partition_broadcast(P)).then_inc(const_in, 16)
            w_block(1, w_mem, 1, second_rows, mem=True)
            with sp.Fori(2, B_MEM_END) as B:
                w_block(B, w_mem, B, mem=True)

            def ropes(k):
                if k == 0:
                    sp.dma_start(rope_c[:, :], rope_cos).then_inc(rope_in, 16)
                    sp.dma_start(rope_s[:, :], rope_sin).then_inc(rope_in, 16)
            w_block(B_XLRU, w_in, 6, ropes)
            w_block(B_XLRU + 1, w_in, 7)

            def lru_loads(B):
                def go(k):
                    for i, s in enumerate(TILE_AT):
                        if k == s:
                            t = (B - B_LRU) * 2 + i
                            sp.wait_ge(l_zero, 2)
                            sp.wait_ge(proj_stored, 64 * B - 64)
                            sp.wait_ge(conv, FIRST + 4 * t)
                            sp.dma_start(l_in[:, 2:2 + SEQ], projT[bass.ds(t * P, P), :]).then_inc(l_xin, 16)
                            sp.wait_ge(l_mm, FIRST + 4 * t)
                            for which, w in enumerate((w_a, w_x)):
                                sp.dma_start(l_w[:, which, :, :],
                                             w[0, :, bass.ds(t, 1), :, :].rearrange("d t c e -> c (d t) e"))\
                                  .then_inc(l_win, 16)
                return go
            with sp.Fori(B_LRU, B_Q) as B:
                w_block(B, w_in, B - 2, lru_loads(B))
            with sp.Fori(B_Q, B_ATT) as B:
                w_block(B, w_in, B - B_Q, lru_loads(B))

            def att_loads(B):
                def go(k):
                    g = B - B_ATT
                    if k == 0:
                        sp.wait_ge(proj_stored, 64 * B_Q)
                        sp.wait_ge(conv, FIRST + 4 * LRU_TILES)
                        sp.wait_ge(l_mm, FIRST + 4 * LRU_TILES)
                        sp.wait_ge(l_ix, FIRST + 2 * LRU_TILES)
                        sp.wait_ge(scored, FIRST + 16 * g)
                        sp.dma_start(k_raw[:, :], projT[bass.ds(g * P + 2 * BW, P), :]).then_inc(k_in, 16)
                    for i, s in enumerate(HEAD_AT):
                        if k == (1 if i == 0 else HEAD_AT[i - 1] + 9):
                            if i == 0:
                                sp.wait_ge(proj_stored, 64 * B - 64)
                            sp.wait_ge(scored, FIRST + 16 * g + 4 * i)
                            sp.dma_start(q_raw[:, :], projT[bass.ds(g * BW + (4 * BW + i * P), P), :])\
                              .then_inc(q_in, 16)
                    if k == 3:
                        sp.wait_ge(pv_done, FIRST + 4 * g)
                        sp.dma_start(v_raw[:, :], projT[bass.ds(g * P + 3 * BW, P), :]).then_inc(v_in, 16)
                return go
            with sp.Fori(B_ATT, B_ATT + 2) as B:
                w_block(B, w_in, B - B_Q, att_loads(B))
            with sp.Fori(B_ATT + 2, B_MEMATT) as B:
                w_block(B, w_in, B - 4, att_loads(B))

            def mem_loads(k):
                for h, s in enumerate(MEMHEAD_AT):
                    at0 = s + 4
                    if k == at0:
                        sp.wait_ge(proj_stored, 64 * (13 + min(h, 1)))
                        if h:
                            sp.wait_ge(m_scored, 2 * h)
                        else:
                            sp.wait_ge(scored, FIRST + 4 * HEADS)
                        sp.dma_start(mk_raw[:, :].rearrange("p (t m) -> p t m", t=2),
                                     kvT[h * MEM_D:(h + 1) * MEM_D, :].rearrange("(t p) m -> p t m", p=P))\
                          .then_inc(mk_in, 16)
                        if h:
                            sp.wait_ge(mv_trd, h)
                        sp.dma_start(mv_raw[:, :].rearrange("p (t m) -> p t m", t=2),
                                     kvT[2 * BW + h * MEM_D:2 * BW + (h + 1) * MEM_D, :]
                                     .rearrange("(t p) m -> p t m", p=P)).then_inc(mv_in, 16)
                        sp.dma_start(mq_raw[:, :, :], projT[8 * BW + h * MEM_D:8 * BW + (h + 1) * MEM_D, :]
                                     .rearrange("(t p) n -> p t n", p=P)).then_inc(mq_in, 16)

            w_block(B_MEMATT, w_in, 10, mem_loads)

            def gate_loads(B):
                def go(k):
                    n = k - 9
                    if 0 <= n < NT:
                        if n == 0:
                            sp.wait_ge(y_stored, 16 * 32)
                        sp.wait_ge(g_mul, FIRST + 4 * (B - 15) + n)
                        if not (isinstance(B, int) and B == 15):
                            sp.wait_ge(g_norm, FIRST + 4 * (B - 15))
                        sp.wait_ge(g_lod, FIRST + 4 * (B - 15))
                        sp.dma_start(g_y[:, n, :], yT[bass.ds((B - 15) * BW + n * P, P), :]).then_inc(gy_in[n], 16)
                return go
            with sp.Fori(B_Z + 1, B_OUT - 1) as B:
                w_block(B, w_in, B - 4, gate_loads(B))

            def y_load(t):
                sp.wait_ge(unit_done, 32 * (B_OUT - 1) + t + 1)
                sp.wait_ge(g_stored, 128 * (t // NT + 1))
                sp.dma_start(f32(y_hi[:, t, :]), gT_hi[t * P:(t + 1) * P, :]).then_inc(y_in[t // 8], 16)
                sp.dma_start(f32(y_lo_tile(t)), gT_lo[t * P:(t + 1) * P, :].rearrange("p (b n) -> p b n", b=SB))\
                  .then_inc(y_in[t // 8], 16)

            def first_y_loads(k):
                gate_loads(B_OUT - 1)(k)
                if k >= 9:
                    y_load(k - 9)
            w_block(B_OUT - 1, w_in, B_OUT - 5, first_y_loads)

            def post_load(B, k):
                if k == 16:
                    if not (isinstance(B, int) and B == B_OUT):
                        sp.wait_ge(o_out, 4 * (B - B_OUT))
                    sp.dma_start(post_row[:, :], post_g[0:1, bass.ds((B - B_OUT) * BW, BW)].partition_broadcast(P))\
                      .then_inc(post_in, 16)

            def last_y_loads(k):
                gate_loads(B_OUT)(k)
                if k < 5:
                    y_load(23 + k)
                if k == 22:
                    for t in range(28, KT):
                        y_load(t)
                post_load(B_OUT, k)
            w_block(B_OUT, w_out, 0, last_y_loads)
            with sp.Fori(B_OUT + 1, B_END - 1) as B:
                w_block(B, w_out, B - B_OUT, lambda k: post_load(B, k))

            def fin_load(j, loaded):
                sp.wait_ge(unit_done, 32 * (B_END - 1) + 4 * j + 4)
                sp.wait_ge(o_stored, 16 * 7)
                c, cols = j // 2, slice((j % 2) * half, (j % 2 + 1) * half)
                sp.dma_start(x_fin[:, c, cols], x[0, c * P:(c + 1) * P, cols]).then_inc(loaded, 16)
                sp.dma_start(o_fin[:, :, j * BW:(j + 1) * BW],
                             o_rows[:, j * BW:(j + 1) * BW].rearrange("(b p) n -> p b n", p=P)).then_inc(loaded, 16)

            def last_loads(k):
                post_load(B_END - 1, k)
                if k == 4:
                    sp.wait_ge(g_stored, 128 * 8)
                    sp.dma_start(x_end[:, :], x[0, 3 * P:4 * P, half:2 * half]).then_inc(fin_in, 16)
                if k >= 12 and k % 4 == 0:
                    fin_load((k - 12) // 4, fin_in)
            w_block(B_END - 1, w_out, 7, last_loads)
            fin_load(5, fin_in)
            fin_load(6, last_in)
            for h in range(2):
                for c in range(SB):
                    sp.wait_ge(f_done, SB * h + c + 1)
                    sp.dma_start(out[0, c * P:(c + 1) * P, h * half:(h + 1) * half],
                                 o_fin[:, c, h * half:(h + 1) * half]).then_inc(stored, 16)
            sp.wait_ge(stored, 16 * 2 * SB)

        @block.tensor
        def _(pe):
            start_counts(pe, l_mm, p_trd, pv_done, scored, v_trd, x_trd)
            def unit(B, k, hi, lo, width, bank_free):
                pe.wait_ge(lo_ready, 32 * B + k + 1)
                slot = k % RING
                for n in range(NT):
                    if k == 0:
                        bank_free(n)
                    cols = slice(n * P, (n + 1) * P)
                    acc = G[n][:, 0:width]
                    pe.matmul(acc, w_hi[:, slot, cols], hi[:, k, :], start=(k == 0), stop=False)
                    pe.matmul(acc, w_hi[:, slot, cols], lo(k), start=False, stop=False)
                    mm = pe.matmul(acc, w_lo[:, slot, cols], hi[:, k, :], start=False, stop=(k == KT - 1))
                    if n == NT - 1:
                        mm.then_inc(unit_done, 1)
                    elif k == KT - 1:
                        mm.then_inc(tile_done, 1)

            def after_copy(B, gated=0):
                done = 2 * (B - gated) - 2
                def wait(n):
                    pe.wait_ge(dve_evac if n % 2 else act_evac, done + n // 2 + 1)
                return wait

            def after_gate(B):
                def wait(n):
                    pe.wait_ge(z_held, 4 * (B - 1 - B_Z) + n + 1)
                return wait

            def gemm(B, hi, lo, width=SEQ, bank_free=None, at_unit=None):
                for k in range(KT):
                    if at_unit:
                        at_unit(k)
                    unit(B, k, hi, lo, width, bank_free or after_copy(B))

            pe.wait_ge(ident_in, 16)
            pe.wait_ge(gain_in, 16 * 5)
            pe.transpose(X[2][:, 0:N_GAINS], par_rows[0:N_GAINS, 0, :], ident[0:N_GAINS, 0:N_GAINS]).then_inc(par_tr, 1)

            def mem_transpose(t):
                if t >= KT:
                    return
                if t % 4 == 0:
                    pe.wait_ge(mem_in[t // 4 % 4], 16 * (t // 16 + 1))
                if t >= 4:
                    pe.wait_ge(m_lod, t - 3)
                elif t == 2:
                    pe.wait_ge(par_ready, 1)
                for b in range(MB):
                    tr = pe.transpose(X[t % 4][:, b * P:(b + 1) * P], mem_rows[:, b, t * P:(t + 1) * P],
                                      ident[:, :])
                tr.then_inc(m_trd, 1)

            for t in range(4):
                mem_transpose(t)
            gemm(0, m_hi, m_lo_tile, N_MEM, lambda n: None, lambda k: mem_transpose(k + 4))

            def spread_rms(k):
                if k == 1:
                    pe.wait_ge(memset_done, 2)
                    pe.wait_ge(m_rs, 1 + MB)
                    pe.wait_ge(m_lod, KT)
                    for b in range(MB):
                        mm = pe.matmul(X[0][:, b * P:(b + 1) * P], ones[:, :], m_diag[:, b, :], start=True, stop=True)
                    mm.then_inc(m_spread, 1)
                if k == 6:
                    pe.wait_ge(par_in, 16 * 5)
                    pe.transpose(X[3][:, 0:PAR], par_rows[0:PAR, 1, :], ident[0:PAR, 0:PAR]).then_inc(par_tr, 1)
            gemm(1, m_hi, m_lo_tile, N_MEM, at_unit=spread_rms)

            for B in range(2, B_MEM_END):
                def x_transpose(k):
                    if k % 2:
                        t = 16 * (B - 2) + k // 2
                        pe.wait_ge(x_scl, t + 1)
                        if t >= 4:
                            pe.wait_ge(x_ev, FIRST + t - 3)
                        else:
                            pe.wait_ge(m_rms_set, 1)
                            pe.wait_ge(par_ready, 2)
                        for b in range(SB):
                            tr = pe.transpose(X[t % 4][:, b * P:(b + 1) * P], x_rows[:, b, t * P:(t + 1) * P],
                                              ident[:, :])
                        tr.then_inc(x_trd, 1)
                gemm(B, m_hi, m_lo_tile, N_MEM, at_unit=x_transpose)
            with pe.Fori(B_XLRU, B_LRU) as B:
                gemm(B, u_hi, u_lo_tile)

            with pe.Fori(B_LRU, B_ATT) as B:
                def lru(k):
                    for i, s in enumerate(TILE_AT):
                        for which in range(2):
                            if k == s + 5 + which:
                                t = 2 * (B - B_LRU) + i
                                pe.wait_ge(conv, FIRST + 4 * t + 4)
                                pe.wait_ge(l_win, 32 * t + 32)
                                for d in range(2):
                                    n = 2 * which + d
                                    pe.wait_ge(l_sig, FIRST + 4 * t)
                                    pe.matmul(X[n][:, :], l_w[:, which, d, :], xc[:, :],
                                              start=True, stop=True).then_inc(l_mm, 1)
                gemm(B, u_hi, u_lo_tile, at_unit=lru)

            def attention(B):
                g = B - B_ATT

                def scores(h, i):
                    if i < 2:
                        pe.wait_ge(row_max, FIRST + 4 * h)
                    else:
                        pe.wait_ge(row_max, FIRST + 4 * h + i - 1)
                    k0, nk = BAND[i]
                    q, kk = slice(i * P, (i + 1) * P), slice(k0 * P, (k0 + nk) * P)
                    s = X[i % 2][:, 0:nk * P]
                    pe.matmul(s, q_hi[:, q], k_hi[:, kk], start=True, stop=False)
                    pe.matmul(s, q_hi[:, q], k_lo[:, kk], start=False, stop=False)
                    pe.matmul(s, q_lo[:, q], k_hi[:, kk], start=False, stop=True).then_inc(scored, 1)

                def turn(h, i):
                    pe.wait_ge(normed, 4 * h + i + 1)
                    if i < 2:
                        pe.wait_ge(pt_lod, FIRST + 4 * h)
                        pe.wait_ge(y_sq, FIRST + LRU_TILES + h)
                    else:
                        pe.wait_ge(pt_lod, FIRST + 4 * h + i - 1)
                    for j in range(BAND[i][1]):
                        tr = pe.transpose(X[2 + i % 2][:, j * P:(j + 1) * P], probs[:, i % 2, j * P:(j + 1) * P],
                                          ident[:, :])
                    tr.then_inc(p_trd, 1)

                def values(h):
                    pe.wait_ge(pt_lod, FIRST + 4 * h + 4)
                    pe.wait_ge(v_lod, g + 1)
                    for kb in range(SB):
                        q0, nq = BAND[kb]
                        o = X[2][:, q0 * P:(q0 + nq) * P]
                        v = slice(kb * P, (kb + 1) * P)
                        ph = pt_hi[:, PT_AT[kb]:PT_AT[kb] + nq, :]
                        pl = pt_lo[:, PT_AT[kb]:PT_AT[kb] + nq, :]
                        pe.matmul(o, v_hi[:, v], ph, start=(kb == 0), stop=False, skip_group_check=True)
                        pe.matmul(o, v_hi[:, v], pl, start=False, stop=False, skip_group_check=True)
                        mm = pe.matmul(o, v_lo[:, v], ph, start=False, stop=(kb == SB - 1), skip_group_check=True)
                    mm.then_inc(pv_done, 1)

                def go(k):
                    if k == 1:
                        pe.wait_ge(l_sig, FIRST + 4 * LRU_TILES)
                        pe.wait_ge(v_in, 16 * g + 16)
                        pe.wait_ge(pt_lod, FIRST + 16 * g)
                        pe.wait_ge(y_sq, FIRST + LRU_TILES + 4 * g)
                        for kb in range(SB):
                            tr = pe.transpose(X[2][:, kb * P:(kb + 1) * P], v_raw[:, kb * P:(kb + 1) * P],
                                              ident[:, :])
                        tr.then_inc(v_trd, 1)
                    for i, s in enumerate(HEAD_AT):
                        h = 4 * g + i
                        if k == s + 8:
                            values(h)
                    for i, s in enumerate(HEAD_AT):
                        h = 4 * g + i
                        if k == s + 1:
                            pe.wait_ge(q_lod, FIRST + h + 1)
                            if i == 0:
                                pe.wait_ge(k_lod, FIRST + g + 1)
                            scores(h, 0)
                            scores(h, 1)
                        if k == s + 3:
                            if i == 0:
                                pe.wait_ge(v_lod, g + 1)
                            turn(h, 0)
                            turn(h, 1)
                            scores(h, 2)
                            scores(h, 3)
                        if k == s + 6:
                            turn(h, 2)
                            turn(h, 3)
                return go
            with pe.Fori(B_ATT, B_MEMATT) as B:
                gemm(B, u_hi, u_lo_tile, at_unit=attention(B))

            def out_norm(which, squares, bank):
                pe.matmul(X[bank][:, :], ones[:, :], squares, start=True, stop=True).then_inc(r_sum, 1)

            def mem_attention(k):
                if k == 0:
                    pe.wait_ge(y_acc, FIRST + 24)
                    pe.wait_ge(memset_done, 2)
                    out_norm(0, sq_acc[:, :], 2)
                    out_norm(1, r_bc[:, 1, :], 3)
                for h, s in enumerate(MEMHEAD_AT):
                    if k == s + 9:
                        mem_values(h)
                for h, s in enumerate(MEMHEAD_AT):
                    if k == s + 1:
                        pe.wait_ge(mv_in, 16 * h + 16)
                        if h:
                            pe.wait_ge(mp_lod, 2 * h)
                        else:
                            pe.wait_ge(r_sqrt, 2)
                        for b in range(MB):
                            for t in range(2):
                                tr = pe.transpose(X[2][:, (2 * b + t) * P:(2 * b + t + 1) * P],
                                                  mv_raw[:, t * N_MEM + b * P:t * N_MEM + (b + 1) * P], ident[:, :])
                        tr.then_inc(mv_trd, 1)
                    if k == s + 4:
                        pe.wait_ge(mk_lod, h + 1)
                        pe.wait_ge(mq_lod, 2 * h + 2)
                        pe.wait_ge(y_out, HEADS + 2 * h)
                        for i in range(SB):
                            o = X[i // 2][:, (i % 2) * N_MEM:(i % 2 + 1) * N_MEM]
                            q = slice(i * P, (i + 1) * P)
                            for t in range(2):
                                kk = slice(t * N_MEM, (t + 1) * N_MEM)
                                pe.matmul(o, mq_hi[:, t, q], mk_hi[:, kk], start=(i % 2 == 0 and t == 0), stop=False,
                                          skip_group_check=True)
                                pe.matmul(o, mq_hi[:, t, q], mk_lo[:, kk], start=False, stop=False,
                                          skip_group_check=True)
                                mm = pe.matmul(o, mq_lo[:, t, q], mk_hi[:, kk], start=False,
                                               stop=(t == 1), skip_group_check=True)
                            if i % 2:
                                mm.then_inc(m_scored, 1)
                    if k == s + 7:
                        pe.wait_ge(m_norm, SB * h + SB)
                        pe.wait_ge(mv_lod, h + 1)
                        for b in range(MB):
                            for i in range(SB):
                                tr = pe.transpose(X[2 + b][:, i * P:(i + 1) * P], mp[:, i, b * P:(b + 1) * P],
                                                  ident[:, :])
                            tr.then_inc(mp_trd, 1)

            def mem_values(h):
                pe.wait_ge(mp_lod, 2 * h + 2)
                pe.wait_ge(m_exp, SB * h + SB)
                for t in range(2):
                    for b in range(MB):
                        v = slice(b * MEM_D + t * P, b * MEM_D + (t + 1) * P)
                        pe.matmul(X[t][:, :], mv_hi[:, v], mpt_hi[:, b, :], start=(b == 0), stop=False)
                        pe.matmul(X[t][:, :], mv_hi[:, v], mpt_lo[:, b, :], start=False, stop=False)
                        mm = pe.matmul(X[t][:, :], mv_lo[:, v], mpt_hi[:, b, :], start=False, stop=(b == MB - 1))
                    mm.then_inc(m_pv, 1)
            gemm(B_MEMATT, u_hi, u_lo_tile, at_unit=mem_attention)

            def mem_norm(k):
                if k == 8:
                    pe.wait_ge(y_acc, FIRST + 32)
                    out_norm(2, r_bc[:, 2, :], 2)
            gemm(B_Z + 1, u_hi, u_lo_tile, bank_free=after_gate(B_Z + 1), at_unit=mem_norm)
            with pe.Fori(B_Z + 2, B_OUT) as B:
                gemm(B, u_hi, u_lo_tile, bank_free=after_gate(B))

            def y_ready(k):
                if k % 8 == 0:
                    pe.wait_ge(y_in[k // 8], 256)

            def out_gemm(B, bank_free, at_unit=None):
                for k in range(KT):
                    if at_unit:
                        at_unit(k)
                    pe.wait_ge(lo_ready, 32 * B + k + 1)
                    slot = k % RING
                    for n in range(SB):
                        if k == 0:
                            bank_free(n)
                        hi, lo = y_hi[:, k, n * P:(n + 1) * P], y_lo[:, n, k * P:(k + 1) * P]
                        acc = G[n][:, :]
                        pe.matmul(acc, hi, w_hi[:, slot, :], start=(k == 0), stop=False)
                        pe.matmul(acc, hi, w_lo[:, slot, :], start=False, stop=False)
                        mm = pe.matmul(acc, lo, w_hi[:, slot, :], start=False, stop=(k == KT - 1))
                        if n == SB - 1:
                            mm.then_inc(unit_done, 1)
                        elif k == KT - 1:
                            mm.then_inc(tile_done, 1)

            def after_out(B):
                def wait(n):
                    pe.wait_ge(o_sq, 4 * (B - 1 - B_OUT) + n + 1)
                return wait
            out_gemm(B_OUT, after_gate(B_OUT), y_ready)
            with pe.Fori(B_OUT + 1, B_END) as B:
                out_gemm(B, after_out(B))

        @block.scalar
        def _(act):
            start_counts(act, l_sig, x_ev, y_sq)
            def split(B, k):
                raw, loaded, count = raw_slot(B, k)
                act.wait_ge(loaded, count)
                if not (isinstance(B, int) and 32 * B + k < RING):
                    act.wait_ge(unit_done, 32 * B + k - RING + 1)
                act.copy(w_hi[:, k % RING, :], raw).then_inc(hi_ready, 1)

            def u_part(k):
                act.wait_ge(x_ev, FIRST + k + 1)
                act.copy(u_hi[:, k, :].rearrange("p (b n) -> p b n", b=SB), x_rows[:, :, k * P:(k + 1) * P])\
                   .then_inc(u_split, 1)

            def evac(B, width=SEQ):
                for n in (0, 2):
                    act.wait_ge(tile_done, 3 * B + n + 1)
                    act.copy(stage[:, n, 0:width], G[n][:, 0:width]).then_inc(act_evac, 1)

            def body(B, side=None, before=None, evacuate=evac):
                for j in range(LEAD, KT + LEAD):
                    b, k = (B, j) if j < KT else (B + 1, j - KT)
                    if before:
                        before(j)
                    if not (isinstance(B, int) and B == B_END - 1 and j >= KT):
                        split(b, k)
                    if side:
                        side(j - LEAD)
                evacuate(B)

            def proj_evac(B, width=SEQ):
                act.wait_ge(proj_stored, 64 * B)
                evac(B, width)

            def m_part(t):
                act.wait_ge(m_trd, t + 1)
                act.activation(m_hi[:, t, :], X[t % 4][:, 0:N_MEM], ACT.Copy,
                               scale=gains[:, G_MEM + t:G_MEM + t + 1]).then_inc(m_hid, 1)

            act.wait_ge(par_tr, 1)
            act.copy(gains[:, :], X[2][:, 0:N_GAINS]).then_inc(par_ready, 1)
            act.wait_ge(par_ready, 1)
            for k in range(LEAD):
                m_part(k)
                split(0, k)

            def x_square(q):
                b, c = q // 4, q % 4
                act.wait_ge(xrow_in[b], 32)
                if q:
                    act.wait_ge(x_sq, q)
                act.activation(x_sqs[:, :], x_rows[:, b, c * 1024:(c + 1) * 1024], ACT.Square,
                               accum_out=x_ss[:, b, c:c + 1]).then_inc(x_sq, 1)

            def first_side(t):
                if t == 30:
                    act.wait_ge(m_stat, 20)
                    act.activation(m_rstd[:, :], m_mv[:, :, 1], ACT.Sqrt).then_inc(m_sqrt, 1)
                if t >= 24 and t % 2 == 0:
                    x_square((t - 24) // 2)
            body(0, first_side, lambda j: m_part(j) if j < KT else None, lambda B: proj_evac(B, N_MEM))

            def second_side(t):
                if t < 8 and t % 2 == 0:
                    x_square(4 + t // 2)
                if t == 9:
                    act.wait_ge(par_tr, 2)
                    act.copy(par[:, :], X[3][:, 0:PAR]).then_inc(par_ready, 1)
                if t >= 15 and t % 2 and t < 31:
                    x_square(8 + (t - 15) // 2)
                if t == 31:
                    act.wait_ge(x_sum, 2)
                    act.activation(x_rstd[:, :], x_rstd[:, :], ACT.Sqrt).then_inc(x_sqrt, 1)
            body(1, second_side, evacuate=lambda B: proj_evac(B, N_MEM))

            def x_out(B):
                def go(t):
                    if t % 2 == 1:
                        kt = 16 * (B - 2) + t // 2
                        act.wait_ge(x_trd, FIRST + kt + 1)
                        act.activation(x_rows[:, :, kt * P:(kt + 1) * P],
                                       X[(t // 2) % 4][:, :].rearrange("p (b n) -> p b n", b=SB), ACT.Copy,
                                       scale=gains[:, G_PRE + kt:G_PRE + kt + 1]).then_inc(x_ev, 1)
                return go
            body(2, x_out(2), evacuate=lambda B: proj_evac(B, N_MEM))
            body(3, x_out(3), before=lambda j: u_part(j - KT) if j >= KT else None,
                 evacuate=lambda B: proj_evac(B, N_MEM))
            body(B_XLRU, before=lambda j: u_part(j) if j < KT else None, evacuate=proj_evac)

            def decay(t):
                if t == 12:
                    act.wait_ge(cd_dve, 2)
                    act.activation(tiny[:, 0:16], tiny[:, 0:16], ACT.Exp, scale=-1.0).then_inc(cd_act, 1)
            body(B_XLRU + 1, decay, evacuate=proj_evac)

            with act.Fori(B_LRU, B_ATT) as B:
                def lru(t):
                    for i, s in enumerate(TILE_AT):
                        T = 2 * (B - B_LRU) + i
                        for which, (o, c) in enumerate(((l_r, C_BA), (l_i, C_BX))):
                            if t == s + 5 + which:
                                for d in range(2):
                                    act.wait_ge(l_mm, FIRST + 4 * T + 2 * which + d + 1)
                                    act.wait_ge(l_b, FIRST + 2 * T)
                                    act.activation(o[:, d, :], X[2 * which + d][:, :], ACT.Sigmoid,
                                                   bias=par[:, bass.ds(T + c + 8 * d, 1)]).then_inc(l_sig, 1)
                        for d in range(2):
                            if t == s + 7 + d:
                                act.wait_ge(l_scan, FIRST + 2 * T)
                                act.wait_ge(y_sq, FIRST + T)
                                act.wait_ge(l_sig, FIRST + 4 * T + 2)
                                c = cdec[:, bass.ds(T + 8 * d, 1)]
                                act.activation(l_a[:, d, :], l_r[:, d, :], ACT.Exp, scale=c).then_inc(l_exp, 1)
                                act.activation(l_t[:, d, :], l_r[:, d, :], ACT.Tanh, scale=c).then_inc(l_exp, 1)
                        if t == s + 10:
                            for d in range(2):
                                act.wait_ge(l_neg, FIRST + 2 * T + d + 1)
                                act.activation(l_n[:, d, :], l_n[:, d, :], ACT.Sqrt, scale=-1.0).then_inc(l_mult, 1)
                        if t == s + 15:
                            act.wait_ge(l_sum, T + 1)
                            act.wait_ge(y_acc, FIRST + T)
                            act.activation(sq_tmp[:, :], l_y[:, :], ACT.Square).then_inc(y_sq, 1)
                body(B, lru, evacuate=proj_evac)

            def attention(B):
                g = B - B_ATT

                def go(t):
                    if t == 0:
                        act.wait_ge(k_in, 16 * g + 16)
                        act.wait_ge(l_sum, LRU_TILES)
                        act.wait_ge(scored, FIRST + 16 * g)
                        act.copy(k_hi[:, :], k_raw[:, :]).then_inc(k_hid, 1)
                    if t == 2:
                        act.wait_ge(v_trd, FIRST + g + 1)
                        act.wait_ge(pv_done, FIRST + 4 * g)
                        act.copy(v_hi[:, :], X[2][:, :]).then_inc(v_hid, 1)
                    for i, s in enumerate(HEAD_AT):
                        h = 4 * g + i
                        if t == s + 8:
                            act.wait_ge(pv_done, FIRST + h + 1)
                            act.wait_ge(y_free, FIRST + LRU_TILES + h)
                            act.copy(y_sb[:, :], X[2][:, :]).then_inc(y_out, 1)
                            act.wait_ge(y_acc, FIRST + LRU_TILES + h)
                            act.activation(sq_tmp[:, :], X[2][:, :], ACT.Square).then_inc(y_sq, 1)
                    for i, s in enumerate(HEAD_AT):
                        h = 4 * g + i
                        if t == s:
                            act.wait_ge(q_in, 16 * h + 16)
                            act.wait_ge(scored, FIRST + 4 * h)
                            act.copy(q_hi[:, :], q_raw[:, :]).then_inc(q_hid, 1)
                        for pair in range(2):
                            if t == s + 1 + 3 * pair:
                                act.wait_ge(max_neg, 2 * h + pair + 1)
                                for e in range(2):
                                    b = 2 * pair + e
                                    pr = probs[:, e, 0:BAND[b][1] * P]
                                    act.activation(pr, pr, ACT.Exp, bias=srow[:, 4 + e:5 + e],
                                                   accum_out=srow[:, 8 + e:9 + e]).then_inc(exped, 1)
                                act.wait_ge(sink_diff, 2 * h + pair + 1)
                                act.activation(srow[:, 16:18], srow[:, 12:14], ACT.Exp).then_inc(sink_exp, 1)
                            if t == s + 3 + 3 * pair:
                                for b in (2 * pair, 2 * pair + 1):
                                    nk = BAND[b][1]
                                    act.wait_ge(p_trd, FIRST + 4 * h + b + 1)
                                    act.wait_ge(pv_done, FIRST + h)
                                    act.copy(pt_hi[:, PT_FIRST[b]:PT_FIRST[b] + 2 * nk - 1:2, :],
                                             X[2 + b % 2][:, 0:nk * P].rearrange("p (j q) -> p j q", q=P))\
                                       .then_inc(pt_hid, 1)
                return go
            with act.Fori(B_ATT, B_MEMATT) as B:
                body(B, attention(B), evacuate=proj_evac)

            def rms(which, bank, width):
                act.wait_ge(r_sum, which + 1)
                act.activation(r_bc[:, which, :], X[bank][:, :], ACT.Sqrt, bias=eps[:, :],
                               scale=1.0 / width).then_inc(r_sqrt, 1)

            def sigmoids(B):
                for n in range(NT):
                    if n < NT - 1:
                        act.wait_ge(tile_done, 3 * B + n + 1)
                    else:
                        act.wait_ge(unit_done, 32 * B + 32)
                    if n == 0:
                        if isinstance(B, int) and B == B_Z:
                            act.wait_ge(proj_stored, 64 * 14)
                        act.wait_ge(g_mul, FIRST + 4 * (B - B_Z))
                    act.activation(stage[:, n, :], G[n][:, :], ACT.Sigmoid).then_inc(sig_done, 1)

            def mem_attention(t):
                if t == 0:
                    rms(0, 2, 2048.0)
                    rms(1, 3, 1024.0)
                for h, s in enumerate(MEMHEAD_AT):
                    if t == s + 9:
                        for d in range(2):
                            act.wait_ge(m_pv, 2 * h + d + 1)
                            if h and d == 0:
                                act.wait_ge(y_stored, 16 * (24 + 2 * h))
                                act.wait_ge(y_acc, FIRST + 24 + 2 * h)
                            act.copy(m_y[:, d, :], X[d][:, :]).then_inc(y_out, 1)
                for h, s in enumerate(MEMHEAD_AT):
                    if t == s + 1:
                        act.wait_ge(mk_in, 16 * h + 16)
                        act.wait_ge(m_scored, 2 * h)
                        act.copy(mk_hi[:, :], mk_raw[:, :]).then_inc(mk_hid, 1)
                        act.wait_ge(mv_trd, h + 1)
                        act.wait_ge(m_pv, 2 * h)
                        act.copy(mv_hi[:, :], X[2][:, :]).then_inc(mv_hid, 1)
                    for d in range(2):
                        if t == s + 1 + 2 * d:
                            act.wait_ge(mq_in, 16 * h + 16)
                            act.wait_ge(m_scored, 2 * h)
                            act.copy(mq_hi[:, d, :], mq_raw[:, d, :]).then_inc(mq_hid, 1)
                    if t == s + 5:
                        for i in range(SB):
                            act.wait_ge(m_neg, 2 * h + i // 2 + 1)
                            act.wait_ge(mp_trd, 2 * h)
                            act.activation(mp[:, i, :], X[i // 2][:, (i % 2) * N_MEM:(i % 2 + 1) * N_MEM], ACT.Exp,
                                           bias=mrow[:, 4 + i:5 + i], scale=MEM_SCALE,
                                           accum_out=mrow[:, 8 + i:9 + i]).then_inc(m_exp, 1)
                    if t == s + 7:
                        for b in range(MB):
                            act.wait_ge(mp_trd, 2 * h + b + 1)
                            act.wait_ge(m_pv, 2 * h)
                            act.copy(mpt_hi[:, b, :], X[2 + b][:, :]).then_inc(mp_hid, 1)
            body(B_MEMATT, mem_attention, evacuate=sigmoids)

            def gates(B, late=None):
                def go(t):
                    if late:
                        late(t)
                    if t >= 6 and t % 2 == 0 and t < 6 + 2 * NT:
                        n = (t - 6) // 2
                        at_g = 4 * (B - 1 - B_Z) + n
                        act.wait_ge(g_mul, FIRST + at_g + 1)
                        if n >= 2:
                            act.wait_ge(g_stored, 128 * (B - 1 - B_Z) + 32 * (n - 1))
                        else:
                            act.wait_ge(g_stored, 128 * (B - 1 - B_Z))
                        act.copy(g_hi[:, n % 2, :], g_y[:, n, :]).then_inc(g_hid, 1)
                return go
            body(B_Z + 1, gates(B_Z + 1, lambda t: rms(2, 2, 1024.0) if t == 8 else None), evacuate=sigmoids)
            with act.Fori(B_Z + 2, B_OUT) as B:
                body(B, gates(B), evacuate=sigmoids)

            def out_squares(B):
                o = B - B_OUT
                for n in range(SB):
                    act.wait_ge(o_out, 4 * o + n + 1)
                    act.wait_ge(g_mul, FIRST + 32)
                    if not (isinstance(B, int) and B == B_OUT):
                        act.wait_ge(o_sq, 4 * o)
                    act.activation(stage[:, n, :], G[n][:, :], ACT.Square,
                                   accum_out=column(o_ss[:, n, :], o)).then_inc(o_sq, 1)
            body(B_OUT, gates(B_OUT), evacuate=out_squares)
            with act.Fori(B_OUT + 1, B_END - 1) as B:
                body(B, evacuate=out_squares)
            body(B_END - 1, evacuate=out_squares)
            act.wait_ge(f_sum, 1)
            act.activation(tiny[:, 0:SB], tiny[:, 0:SB], ACT.Sqrt, bias=eps[:, :],
                           scale=1.0 / D_MODEL).then_inc(f_sqrt, 1)

        @block.vector
        def _(dve):
            start_counts(dve, conv, g_lod, g_mul, g_norm, k_lod, l_neg, l_scan, pt_lod,
                         q_lod, row_max)
            def split(B, k):
                dve.wait_ge(hi_ready, 32 * B + k + 1)
                dve.tensor_tensor(w_lo[:, k % RING, :], raw_slot(B, k)[0], f32(w_hi[:, k % RING, :]),
                                  ALU.subtract).then_inc(lo_ready, 1)

            def u_part(k):
                dve.wait_ge(u_split, k + 1)
                dve.tensor_tensor(u_lo_tile(k), x_rows[:, :, k * P:(k + 1) * P],
                                  f32(u_hi[:, k, :]).rearrange("p (b n) -> p b n", b=SB), ALU.subtract)

            def evac(B, width=SEQ):
                for n in (1, 3):
                    if n == 1:
                        dve.wait_ge(tile_done, 3 * B + n + 1)
                    else:
                        dve.wait_ge(unit_done, 32 * B + 32)
                    dve.tensor_copy(stage[:, n, 0:width], G[n][:, 0:width]).then_inc(dve_evac, 1)

            def body(B, side=None, before=None, evacuate=evac):
                for j in range(LEAD, KT + LEAD):
                    b, k = (B, j) if j < KT else (B + 1, j - KT)
                    if before:
                        before(j)
                    if not (isinstance(B, int) and B == B_END - 1 and j >= KT):
                        split(b, k)
                    if side:
                        side(j - LEAD)
                evacuate(B)

            def proj_evac(B, width=SEQ):
                dve.wait_ge(proj_stored, 64 * B)
                evac(B, width)

            dve.memset(ones[:, :], 1.0).then_inc(memset_done, 1)
            dve.memset(eps[:, :], EPS).then_inc(memset_done, 1)

            def m_part(t):
                dve.wait_ge(m_hid, t + 1)
                dve.scalar_tensor_tensor(m_lo[:, t, :], X[t % 4][:, 0:N_MEM], gains[:, G_MEM + t:G_MEM + t + 1],
                                         f32(m_hi[:, t, :]), ALU.mult, ALU.subtract).then_inc(m_lod, 1)
            for k in range(LEAD):
                m_part(k)
                split(0, k)

            def mem_stats(t):
                for c in range(8):
                    for b in range(MB):
                        if t == max(4 * c - 2, 0) + (2 if c else 1) * b:
                            dve.wait_ge(mem_in[c % 4], 16 * (c // 4 + 1))
                            dve.bn_stats(m_bn[:, b, 6 * c:6 * c + 6], mem_rows[:, b, c * 512:(c + 1) * 512])\
                               .then_inc(m_stat, 1)
                if t == 29:
                    dve.wait_ge(m_stat, 16)
                    for b in range(MB):
                        dve.bn_aggr(m_mv[:, b, :], m_bn[:, b, :]).then_inc(m_stat, 1)
                    dve.wait_ge(m_stat, 18)
                    dve.tensor_tensor(m_mv[:, :, 0], m_mv[:, :, 0], m_mv[:, :, 0], ALU.mult).then_inc(m_stat, 1)
                    dve.wait_ge(m_stat, 19)
                    dve.scalar_tensor_tensor(m_mv[:, :, 1], m_mv[:, :, 1], EPS, m_mv[:, :, 0], ALU.add, ALU.add)\
                       .then_inc(m_stat, 1)
                if t == 31:
                    dve.wait_ge(ident_in, 16)
                    dve.wait_ge(m_sqrt, 1)
                    dve.reciprocal(m_rstd[:, :], m_rstd[:, :]).then_inc(m_rs, 1)
                    dve.wait_ge(m_rs, 1)
                    for b in range(MB):
                        dve.tensor_scalar(m_diag[:, b, :], ident[:, :], m_rstd[:, b:b + 1], None, ALU.mult)\
                           .then_inc(m_rs, 1)
            body(0, mem_stats, lambda j: m_part(j) if j < KT else None, lambda B: proj_evac(B, N_MEM))

            def x_stats(t):
                if t == 3:
                    dve.wait_ge(m_spread, 1)
                    dve.tensor_copy(m_rms[:, :], X[0][:, 0:N_MEM]).then_inc(m_rms_set, 1)
                if t == 30:
                    dve.wait_ge(x_sq, 16)
                    dve.reduce_sum(x_rstd[:, :], x_ss[:, :, :], AX.X).then_inc(x_sum, 1)
                    dve.wait_ge(x_sum, 1)
                    dve.tensor_scalar(x_rstd[:, :], x_rstd[:, :], 1.0 / D_MODEL, EPS, ALU.mult, ALU.add)\
                       .then_inc(x_sum, 1)
                if t == 31:
                    dve.wait_ge(x_sqrt, 1)
                    dve.reciprocal(x_rstd[:, :], x_rstd[:, :]).then_inc(x_rs, 1)
            body(1, x_stats, evacuate=lambda B: proj_evac(B, N_MEM))
            body(2, evacuate=lambda B: proj_evac(B, N_MEM))
            body(3, before=lambda j: u_part(j - KT) if j >= KT else None,
                 evacuate=lambda B: proj_evac(B, N_MEM))
            body(B_XLRU, before=lambda j: u_part(j) if j < KT else None, evacuate=proj_evac)

            halves = [(i + ROT // 2) % ROT for i in range(ROT)]

            def rope_swap(B, r, t):
                for n in range(NT):
                    if t != SWAP_AT[n]:
                        continue
                    dve.wait_ge(act_evac if n % 2 == 0 else dve_evac, 2 * (B - 1) + n // 2 + 1)
                    dve.wait_ge(rope_done, FIRST + 4 * r + n)
                    dve.sem_inc(passed, 1)
                    dve.stream_shuffle(rot[:, :], stage[0:ROT, n, :], halves).then_inc(swapped, 1)

            cd = [0]

            def step(ins):
                cd[0] += 1
                ins.then_inc(cd_dve, 1)
                dve.wait_ge(cd_dve, cd[0])

            def decay(t):
                lam_c = par[:, C_LAM:C_LAM + 16]
                e, z, z2, s = tiny[:, 0:16], tiny[:, 16:32], tiny[:, 32:48], cdec[:, :]
                if t == 10:
                    dve.wait_ge(par_ready, 2)
                    step(dve.tensor_scalar(s, lam_c, -1.0, None, ALU.mult))
                    step(dve.tensor_tensor(e, lam_c, s, ALU.max))
                if t == 16:
                    dve.wait_ge(cd_act, 1)
                    step(dve.tensor_scalar(z, e, 2.0, None, ALU.add))
                    step(dve.reciprocal(z, z))
                    step(dve.tensor_tensor(z, z, e, ALU.mult))
                    step(dve.tensor_tensor(z2, z, z, ALU.mult))
                    step(dve.tensor_scalar(e, z2, 1.0 / 19, 1.0 / 17, ALU.mult, ALU.add))
                if 17 <= t < 25:
                    n = 15 - 2 * (t - 17)
                    step(dve.tensor_tensor(e, e, z2, ALU.mult))
                    step(dve.tensor_scalar(e, e, 1.0 / n, None, ALU.add))
                if t == 25:
                    step(dve.tensor_tensor(e, e, z, ALU.mult))
                    step(dve.tensor_scalar(s, s, 0.0, None, ALU.max))
                    step(dve.scalar_tensor_tensor(s, e, 2.0, s, ALU.mult, ALU.add))
                    step(dve.tensor_scalar(s, s, -LRU_C, None, ALU.mult))

            body(B_XLRU + 1, decay, evacuate=proj_evac)

            def lru(B, rope=None):
                def go(t):
                    if rope is not None:
                        rope_swap(B, rope, t)
                    for i, s in enumerate(TILE_AT):
                        T = 2 * (B - B_LRU) + i
                        for d in range(2):
                            if t == s + 12 + d:
                                dve.wait_ge(l_b, FIRST + 2 * T + d + 1)
                                o, a, v = l_h[:, d, :], l_a[:, d, :], l_n[:, d, :]
                                if d == 0:
                                    dve.tensor_tensor_scan(o, a, v, 0.0, ALU.mult, ALU.add).then_inc(l_scan, 1)
                                else:
                                    dve.tensor_tensor_scan(o[:, ::-1], a[:, ::-1], v[:, ::-1], 0.0, ALU.mult,
                                                           ALU.add).then_inc(l_scan, 1)
                        if t == s + 14:
                            dve.wait_ge(l_scan, FIRST + 2 * T + 2)
                            dve.wait_ge(y_free, FIRST + T)
                            dve.wait_ge(y_sq, FIRST + T)
                            dve.tensor_tensor(l_y[:, :], l_h[:, 0, :], l_h[:, 1, :], ALU.add).then_inc(l_sum, 1)
                        if t == s:
                            dve.wait_ge(l_xin, 16 * T + 16)
                            dve.wait_ge(l_mm, FIRST + 4 * T)
                            dve.wait_ge(l_ix, FIRST + 2 * T)
                            dve.tensor_scalar(xc[:, :], l_in[:, 0:SEQ], par[:, bass.ds(T + C_CONVW, 1)],
                                              par[:, bass.ds(T + C_CONVB, 1)], ALU.mult, ALU.add).then_inc(conv, 1)
                        for j in range(1, 4):
                            if t == s + j:
                                dve.wait_ge(conv, FIRST + 4 * T + j)
                                dve.scalar_tensor_tensor(xc[:, :], l_in[:, j:j + SEQ],
                                                         par[:, bass.ds(T + (C_CONVW + 8 * j), 1)], xc[:, :],
                                                         ALU.mult, ALU.add).then_inc(conv, 1)
                        if t == s + 9:
                            for d in range(2):
                                dve.wait_ge(l_asq, 2 * T + d + 1)
                                dve.wait_ge(l_exp, 4 * T + 2 * d + 2)
                                dve.scalar_tensor_tensor(l_n[:, d, :], l_n[:, d, :], 1.0, l_t[:, d, :], ALU.add,
                                                         ALU.mult).then_inc(l_neg, 1)
                return go
            with dve.Fori(0, 2) as pair:
                body(2 * pair + B_LRU, lru(2 * pair + B_LRU), evacuate=proj_evac)
                body(2 * pair + (B_LRU + 1), lru(2 * pair + (B_LRU + 1), pair), evacuate=proj_evac)

            def attention(B, rope):
                g = B - B_ATT

                def go(t):
                    if rope:
                        rope_swap(B, g + 2, t)
                    if t == 0:
                        dve.wait_ge(k_hid, g + 1)
                        dve.tensor_tensor(k_lo[:, :], k_raw[:, :], f32(k_hi[:, :]), ALU.subtract).then_inc(k_lod, 1)
                        dve.wait_ge(const_in, 32)
                        dve.tensor_copy(sink4[:, :], sinks[:, bass.ds(4 * g, 4)]).then_inc(sink_set, 1)
                    if t == 2:
                        dve.wait_ge(v_hid, g + 1)
                        dve.tensor_tensor(v_lo[:, :], X[2][:, :], f32(v_hi[:, :]), ALU.subtract).then_inc(v_lod, 1)
                    for i, s in enumerate(HEAD_AT):
                        h = 4 * g + i
                        if t == s:
                            dve.wait_ge(q_hid, h + 1)
                            dve.tensor_tensor(q_lo[:, :], q_raw[:, :], f32(q_hi[:, :]), ALU.subtract)\
                               .then_inc(q_lod, 1)
                        for pair in range(2):
                            if t == s + 3 + 3 * pair:
                                for b in (2 * pair, 2 * pair + 1):
                                    nk = BAND[b][1]
                                    dve.wait_ge(pt_hid, 4 * h + b + 1)
                                    slots = slice(PT_FIRST[b], PT_FIRST[b] + 2 * nk - 1, 2)
                                    dve.tensor_tensor(pt_lo[:, slots, :],
                                                      X[2 + b % 2][:, 0:nk * P].rearrange("p (j q) -> p j q", q=P),
                                                      f32(pt_hi[:, slots, :]), ALU.subtract).then_inc(pt_lod, 1)
                            if t == s + 1 + 3 * pair - pair:
                                sk = sink4[:, i:i + 1]
                                dve.wait_ge(sink_set, g + 1)
                                for e in range(2):
                                    b = 2 * pair + e
                                    k0, nk = BAND[b]
                                    m0 = (k0 - b + 1) * P
                                    dve.wait_ge(scored, FIRST + 4 * h + b + 1)
                                    if pair:
                                        dve.wait_ge(p_trd, FIRST + 4 * h + b - 1)
                                    else:
                                        dve.wait_ge(p_trd, FIRST + 4 * h)
                                    dve.sem_inc(passed, 1)
                                    dve.tensor_tensor_reduce(probs[:, e, 0:nk * P], X[b % 2][:, 0:nk * P],
                                                             mask[:, m0:m0 + nk * P], ATT_SCALE, sk, ALU.add,
                                                             ALU.max, srow[:, e:e + 1]).then_inc(row_max, 1)
                                dve.wait_ge(row_max, FIRST + 4 * h + 2 * pair + 2)
                                dve.tensor_scalar(srow[:, 4:6], srow[:, 0:2], -1.0, None, ALU.mult)\
                                   .then_inc(max_neg, 1)
                                dve.wait_ge(max_neg, 2 * h + pair + 1)
                                dve.tensor_scalar(srow[:, 12:14], srow[:, 4:6], sk, None, ALU.add)\
                                   .then_inc(sink_diff, 1)
                            if t == s + 2 + 3 * pair:
                                dve.wait_ge(exped, 4 * h + 2 * pair + 2)
                                dve.wait_ge(sink_exp, 2 * h + pair + 1)
                                dve.tensor_tensor(srow[:, 18:20], srow[:, 8:10], srow[:, 16:18], ALU.add)\
                                   .then_inc(denom, 1)
                                dve.wait_ge(denom, 2 * h + pair + 1)
                                dve.reciprocal(srow[:, 20:22], srow[:, 18:20]).then_inc(recip, 1)
                                dve.wait_ge(recip, 2 * h + pair + 1)
                                for e in range(2):
                                    pr = probs[:, e, 0:BAND[2 * pair + e][1] * P]
                                    dve.tensor_scalar(pr, pr, srow[:, 20 + e:21 + e], None, ALU.mult)\
                                       .then_inc(normed, 1)
                return go
            with dve.Fori(B_ATT, B_MEMATT - 1) as B:
                body(B, attention(B, True), evacuate=proj_evac)
            body(B_MEMATT - 1, attention(B_MEMATT - 1, False), evacuate=proj_evac)

            def hold(B):
                for n in range(NT):
                    dve.wait_ge(sig_done, 4 * (B - B_Z) + n + 1)
                    dve.tensor_tensor(stage[:, n, :], stage[:, n, :], G[n][:, :], ALU.mult).then_inc(z_held, 1)

            def rms(which):
                dve.wait_ge(r_sqrt, which + 1)
                dve.reciprocal(r_bc[:, which, :], r_bc[:, which, :]).then_inc(r_ready, 1)

            def mem_attention(t):
                if t == 0:
                    rms(0)
                    rms(1)
                for h, s in enumerate(MEMHEAD_AT):
                    if t == s + 1:
                        dve.wait_ge(mk_hid, h + 1)
                        dve.tensor_tensor(mk_lo[:, :], mk_raw[:, :], f32(mk_hi[:, :]), ALU.subtract)\
                           .then_inc(mk_lod, 1)
                        dve.wait_ge(mv_hid, h + 1)
                        dve.tensor_tensor(mv_lo[:, :], X[2][:, :], f32(mv_hi[:, :]), ALU.subtract)\
                           .then_inc(mv_lod, 1)
                    for d in range(2):
                        if t == s + 1 + 2 * d:
                            dve.wait_ge(mq_hid, 2 * h + d + 1)
                            dve.tensor_tensor(mq_lo[:, d, :], mq_raw[:, d, :], f32(mq_hi[:, d, :]), ALU.subtract)\
                               .then_inc(mq_lod, 1)
                    if t == s + 4:
                        for i in range(2):
                            dve.wait_ge(m_scored, 2 * h + i + 1)
                            dve.reduce_max(mrow[:, 2 * i:2 * i + 2],
                                           X[i][:, :].rearrange("p (b m) -> p b m", b=2), AX.X).then_inc(m_max, 1)
                            dve.wait_ge(m_max, 2 * h + i + 1)
                            dve.tensor_scalar(mrow[:, 4 + 2 * i:6 + 2 * i], mrow[:, 2 * i:2 * i + 2], -MEM_SCALE,
                                              None, ALU.mult).then_inc(m_neg, 1)
                    if t == s + 6:
                        dve.wait_ge(m_exp, SB * h + SB)
                        dve.reciprocal(mrow[:, 12:16], mrow[:, 8:12]).then_inc(m_rec, 1)
                        dve.wait_ge(m_rec, h + 1)
                        for i in range(SB):
                            dve.tensor_scalar(mp[:, i, :], mp[:, i, :], mrow[:, 12 + i:13 + i], None, ALU.mult)\
                               .then_inc(m_norm, 1)
                    if t == s + 7:
                        dve.wait_ge(y_stored, 16 * 24)
                        for b in range(MB):
                            dve.wait_ge(mp_hid, 2 * h + b + 1)
                            dve.tensor_tensor(mpt_lo[:, b, :], X[2 + b][:, :], f32(mpt_hi[:, b, :]), ALU.subtract)\
                               .then_inc(mp_lod, 1)
            body(B_MEMATT, mem_attention, evacuate=hold)

            def gates(B, which, late=None):
                def go(t):
                    if late:
                        late(t)
                    if t >= 5 and t < 5 + 2 * NT:
                        n = (t - 5) // 2
                        at_g = 4 * (B - 1 - B_Z) + n
                        if t % 2 == 1:
                            dve.wait_ge(gy_in[n], 16 * (B - B_Z))
                            dve.wait_ge(r_ready, which + 1)
                            dve.scalar_tensor_tensor(g_y[:, n, :], g_y[:, n, :],
                                                     gains[:, bass.ds(at_g + G_OUT, 1)] if not isinstance(B, int)
                                                     else gains[:, at_g + G_OUT:at_g + G_OUT + 1],
                                                     r_bc[:, which, :], ALU.mult, ALU.mult).then_inc(g_norm, 1)
                            dve.wait_ge(g_norm, FIRST + at_g + 1)
                            dve.wait_ge(z_held, at_g + 1)
                            dve.tensor_tensor(g_y[:, n, :], g_y[:, n, :], stage[:, n, :], ALU.mult)\
                               .then_inc(g_mul, 1)
                        else:
                            dve.wait_ge(g_hid, at_g + 1)
                            dve.tensor_tensor(g_lo[:, n % 2, :], g_y[:, n, :], f32(g_hi[:, n % 2, :]),
                                              ALU.subtract).then_inc(g_lod, 1)
                return go
            body(B_Z + 1, gates(B_Z + 1, 0, lambda t: rms(2) if t == 8 else None), evacuate=hold)
            with dve.Fori(B_Z + 2, B_Z + 5) as B:
                body(B, gates(B, 0), evacuate=hold)
            with dve.Fori(B_Z + 5, B_Z + 7) as B:
                body(B, gates(B, 1), evacuate=hold)
            body(B_OUT - 1, gates(B_OUT - 1, 2), evacuate=hold)

            def out_rows(B, buffer=None):
                def go(_):
                    o = B - B_OUT
                    for n in range(SB):
                        if n < SB - 1:
                            dve.wait_ge(tile_done, 3 * B + n + 1)
                        else:
                            dve.wait_ge(unit_done, 32 * B + 32)
                        if n == 0:
                            dve.wait_ge(post_in, 16 * o + 16)
                            if buffer is not None and not (isinstance(B, int) and B == B_OUT):
                                dve.wait_ge(o_free, o)
                        dst = o_fin[:, n, 7 * BW:8 * BW] if buffer is None else o_buf[:, buffer, n, :]
                        dve.tensor_tensor(dst, G[n][:, :], post_row[:, :], ALU.mult).then_inc(o_out, 1)
                return go
            body(B_OUT, gates(B_OUT, 2), evacuate=out_rows(B_OUT, 0))
            with dve.Fori(0, 3) as pair:
                body(2 * pair + (B_OUT + 1), evacuate=out_rows(2 * pair + (B_OUT + 1), 1))
                body(2 * pair + (B_OUT + 2), evacuate=out_rows(2 * pair + (B_OUT + 2), 0))
            body(B_END - 1, evacuate=out_rows(B_END - 1))
            dve.wait_ge(o_sq, 32)
            dve.reduce_sum(tiny[:, 0:SB], o_ss[:, :, :], AX.X).then_inc(f_sum, 1)
            dve.wait_ge(f_sqrt, 1)
            dve.reciprocal(tiny[:, 16:16 + SB], tiny[:, 0:SB]).then_inc(f_rs, 1)
            dve.wait_ge(f_rs, 1)
            half = D_MODEL // 2
            dve.wait_ge(o_out, 32)
            dve.wait_ge(fin_in, 16 * 13)
            for h in range(2):
                for c in range(SB):
                    if h == 0 and c == 3:
                        dve.wait_ge(last_in, 32)
                    cols = slice(h * half, (h + 1) * half)
                    x_part = x_end[:, :] if h == 1 and c == 3 else x_fin[:, c, cols]
                    dve.scalar_tensor_tensor(o_fin[:, c, cols], o_fin[:, c, cols], tiny[:, 16 + c:17 + c],
                                             x_part, ALU.mult, ALU.add).then_inc(f_done, 1)

        @block.gpsimd
        def _(pool):
            start_counts(pool, l_b, l_ix, y_acc, y_free, o_free, rope_done)
            pool.memset(sq_acc[:, :], 0.0).then_inc(acc_zero, 1)

            def copied(B, n):
                pool.wait_ge(dve_evac if n % 2 else act_evac, 2 * B + n // 2 + 1)

            def store(B, dst, width=SEQ, rope=None, tiles=range(NT)):
                if 0 in tiles and not (isinstance(B, int) and B == 0):
                    pool.wait_ge(proj_stored, 64 * B)
                for n in tiles:
                    copied(B, n)
                    if width == N_MEM:
                        v = stage[:, n, 0:width]
                        pool.tensor_tensor(v, v, m_rms[:, :], ALU.mult).then_inc(kv_scaled, 1)
                        pool.wait_ge(kv_scaled, 4 * B + n + 1)
                    if rope is not None:
                        r = 4 * rope + n
                        pool.wait_ge(swapped, r + 1)
                        pool.tensor_tensor(rot[:, :], rot[:, :], rope_s[:, :], ALU.mult).then_inc(rope_mul, 1)
                        v = stage[0:ROT, n, :]
                        pool.tensor_tensor(v, v, rope_c[:, :], ALU.mult).then_inc(rope_mul, 1)
                        pool.wait_ge(rope_mul, 2 * r + 2)
                        pool.tensor_tensor(v, v, rot[:, :], ALU.add).then_inc(rope_done, 1)
                        pool.wait_ge(rope_done, FIRST + r + 1)
                    pool.dma_start(dst(n), stage[:, n, 0:width]).then_inc(proj_stored, 16)

            def kv_rows(B):
                return lambda n: kvT[bass.ds(B * BW + n * P, P), :]

            def proj_rows(B):
                return lambda n: projT[bass.ds((B - 4) * BW + n * P, P), :]

            pool.wait_ge(m_rms_set, 1)
            store(0, kv_rows(0), N_MEM)

            def x_scale(e):
                v = x_rows[:, :, bass.ds(e * P, P)]
                pool.tensor_tensor(v, v, x_rstd[:, :].unsqueeze(2).to_broadcast([P, SB, P]), ALU.mult)\
                    .then_inc(x_scl, 1)

            pool.wait_ge(x_rs, 1)
            with pool.Fori(0, 4) as e:
                x_scale(e)
            store(1, kv_rows(1), N_MEM)
            with pool.Fori(4, KT) as e:
                x_scale(e)
            with pool.Fori(2, B_MEM_END) as B:
                store(B, kv_rows(B), N_MEM)
            store(B_XLRU, proj_rows(B_XLRU))
            pool.memset(r_bc[:, 1:3, :], 0.0).then_inc(l_zero, 1)
            pool.memset(l_in[:, 0:2], 0.0)
            pool.memset(l_in[:, SEQ + 2:SEQ + 4], 0.0).then_inc(l_zero, 1)
            pool.wait_ge(l_zero, 2)
            pool.wait_ge(acc_zero, 1)
            pool.wait_ge(rope_in, 32)

            def lru_tile(T):
                for d in range(2):
                    pool.wait_ge(l_sig, FIRST + 4 * T + d + 3)
                    pool.wait_ge(conv, FIRST + 4 * T + 4)
                    pool.tensor_tensor(l_i[:, d, :], l_i[:, d, :], xc[:, :], ALU.mult).then_inc(l_ix, 1)
                for d in range(2):
                    pool.wait_ge(l_exp, 4 * T + 2 * d + 1)
                    pool.wait_ge(l_scan, FIRST + 2 * T)
                    pool.tensor_tensor(l_n[:, d, :], l_a[:, d, :], l_a[:, d, :], ALU.mult).then_inc(l_asq, 1)
                for d in range(2):
                    pool.wait_ge(l_mult, 2 * T + d + 1)
                    pool.wait_ge(l_ix, FIRST + 2 * T + d + 1)
                    pool.tensor_tensor(l_n[:, d, :], l_n[:, d, :], l_i[:, d, :], ALU.mult).then_inc(l_b, 1)
                pool.wait_ge(l_sum, T + 1)
                pool.dma_start(yT[bass.ds(T * P + 16 * P, P), :], l_y[:, :]).then_inc(y_stored, 16)
                pool.wait_ge(y_sq, FIRST + T + 1)
                pool.wait_ge(y_acc, FIRST + T)
                pool.tensor_tensor(r_bc[:, 1, :], r_bc[:, 1, :], sq_tmp[:, :], ALU.add).then_inc(y_acc, 1)
                pool.wait_ge(y_stored, 16 * T + 16)
                pool.sem_inc(y_free, 1)

            with pool.Fori(0, 2) as pair:
                store(2 * pair + (B_LRU - 1), proj_rows(2 * pair + (B_LRU - 1)))
                lru_tile(4 * pair)
                lru_tile(4 * pair + 1)
                store(2 * pair + B_LRU, proj_rows(2 * pair + B_LRU), rope=pair, tiles=(0, 1))
                lru_tile(4 * pair + 2)
                store(2 * pair + B_LRU, proj_rows(2 * pair + B_LRU), rope=pair, tiles=(2, 3))
                lru_tile(4 * pair + 3)

            def head_out(h):
                pool.wait_ge(y_out, h + 1)
                pool.dma_start(yT[bass.ds(h * P, P), :], y_sb[:, :]).then_inc(y_stored, 16)
                pool.wait_ge(y_sq, FIRST + LRU_TILES + h + 1)
                pool.wait_ge(y_acc, FIRST + LRU_TILES + h)
                pool.tensor_tensor(sq_acc[:, :], sq_acc[:, :], sq_tmp[:, :], ALU.add).then_inc(y_acc, 1)
                pool.wait_ge(y_stored, 16 * (LRU_TILES + 1) + 16 * h)
                pool.sem_inc(y_free, 1)

            with pool.Fori(B_ATT, B_MEMATT - 1) as B:
                for i, tiles in enumerate(((0, 1), (2,), (3,), ())):
                    store(B - 1, proj_rows(B - 1), rope=B - B_ATT + 2, tiles=tiles)
                    head_out(4 * (B - B_ATT) + i)
            store(B_MEMATT - 2, proj_rows(B_MEMATT - 2))
            for i in range(4):
                head_out(12 + i)

            store(B_MEMATT - 1, proj_rows(B_MEMATT - 1))
            for i in range(8):
                pool.wait_ge(y_out, HEADS + i + 1)
                v = m_y[:, i % 2, :]
                pool.dma_start(yT[(24 + i) * P:(25 + i) * P, :], v).then_inc(y_stored, 16)
                pool.wait_ge(y_acc, FIRST + 24 + i)
                pool.tensor_tensor(sq_tmp[:, :], v, v, ALU.mult).then_inc(my_sq, 1)
                pool.wait_ge(my_sq, i + 1)
                pool.tensor_tensor(r_bc[:, 2, :], r_bc[:, 2, :], sq_tmp[:, :], ALU.add).then_inc(y_acc, 1)

            with pool.Fori(0, 8) as z:
                for n in range(NT):
                    for part, made, dst in ((g_hi, g_hid, gT_hi), (g_lo, g_lod, gT_lo)):
                        pool.wait_ge(made, (FIRST if made is g_lod else 0) + 4 * z + n + 1)
                        pool.sem_inc(passed, 1)
                        pool.dma_start(dst[bass.ds(z * BW + n * P, P), :], f32(part[:, n % 2, :]))\
                            .then_inc(g_stored, 16)
                    pool.wait_ge(g_stored, 128 * z + 32 * n + 32)

            def out_store(o, buffer):
                pool.wait_ge(o_out, 4 * o + 4)
                pool.sem_inc(passed, 1)
                pool.dma_start(o_rows[:, bass.ds(o * BW, BW)].rearrange("(b p) n -> p b n", p=P),
                               o_buf[:, buffer, :, :]).then_inc(o_stored, 16)
                pool.wait_ge(o_stored, 16 * o + 16)
                pool.sem_inc(o_free, 1)

            with pool.Fori(0, 3) as pair:
                out_store(2 * pair, 0)
                out_store(2 * pair + 1, 1)
            out_store(6, 0)


_INS = ["x", "mem", "pre_norm_gain", "w_in", "att_sink", "conv_w", "conv_b", "lru_w_a", "lru_b_a", "lru_w_x",
        "lru_b_x", "lru_lambda", "mem_norm_gain", "w_mem_kv", "att_out_gain", "lru_out_gain", "mem_out_gain",
        "w_out", "post_norm_gain"]


def shape_constants():
    half = ROT // 2
    inv_freq = np.power(np.float32(500000.0), -np.arange(half, dtype=np.float32) * np.float32(2.0) / np.float32(ROT))
    ang = np.arange(SEQ, dtype=np.float32)[None, :] * inv_freq[:, None]
    cos, sin = np.cos(ang).astype(np.float32), np.sin(ang).astype(np.float32)
    q, k = np.arange(P)[:, None], np.arange(3 * P)[None, :] - P
    return {
        "rope_cos": np.concatenate([cos, cos]),
        "rope_sin": np.concatenate([-sin, sin]),
        "band_mask": np.where(np.abs(k - q) <= P, 0.0, MASKED).astype(np.float32),
        "identity": np.eye(P, dtype=np.float32),
    }


def kernel(**inputs):
    import concourse.bacc as bacc
    from concourse.bass_utils import run_bass_kernel_spmd

    nc = bacc.Bacc("TRN2", target_bir_lowering=False, num_devices=1)
    arrays, args = {}, []
    named = {name: np.ascontiguousarray(inputs[name]) for name in _INS}
    named.update(shape_constants())
    for name, a in named.items():
        arrays[f"in_{name}"] = a
        args.append(nc.dram_tensor(f"in_{name}", a.shape, mybir.dt.from_np(a.dtype), kind="ExternalInput").ap())
    out = nc.dram_tensor("out_0", (1, SEQ, D_MODEL), F32, kind="ExternalOutput").ap()
    hymba(nc, *args, out)
    return run_bass_kernel_spmd(nc, [arrays], core_ids=[0]).results[0]["out_0"]
```

```python
from contextlib import ExitStack

import numpy as np
import concourse.bass as bass
from concourse import mybir

F32 = mybir.dt.float32
F32R = mybir.dt.float32r
ALU = mybir.AluOpType
ACT = mybir.ActivationFunctionType
AX = mybir.AxisListType

P = 128
D_MODEL = 4096
SEQ = 512
N_MEM = 256
EPS = 1e-6
KT = D_MODEL // P
NT = 4
BW = NT * P
SB = SEQ // P
MB = N_MEM // P
HEADS = 16
ATT_SCALE = float(P) ** -0.5
MEM_HEADS = 4
MEM_D = 256
MEM_SCALE = float(MEM_D) ** -0.5
LRU_TILES = 8
LRU_C = 8.0
ROT = 32
MASKED = -1.0e30
FIRST = 1

B_XLRU, B_K, B_V, B_Q, B_QMEM, B_Z, B_OUT, B_END = 4, 6, 7, 8, 12, 14, 22, 30
B_LRU, B_ATT, B_MEMATT = 6, 10, 14
RAW = 4
MEM_RAW = 8
B_MEM_END = 4
RING = 4
SKEW = 7
LEAD = 3
HEAD_AT = (1, 8, 15, 22)
SWAP_AT = (1, 4, 12, 18)
TILE_AT = (0, 16)
MEMHEAD_AT = (1, 8, 15, 22)
BAND = [(max(i - 1, 0), min(i + 1, SB - 1) - max(i - 1, 0) + 1) for i in range(SB)]
PT_FIRST = (0, 1, 4, 7)
PT_AT = (0, 2, 5, 8)
G_PRE, G_OUT, G_MEM, N_GAINS = 0, 32, 64, 96
PAR = 88
FINAL = [(c, q) for c in range(SB) for q in range(4)]
C_CONVW, C_CONVB, C_BA, C_BX, C_LAM = 0, 32, 40, 56, 72


def hymba(nc, x, mem, pre_g, w_in, sink, conv_w, conv_b, w_a, b_a, w_x, b_x, lam, mem_g, w_mem,
          g_att, g_lru, g_mem, w_out, post_g, rope_cos, rope_sin, band_mask, identity, out):
    ctx = ExitStack()
    with ctx:
        def sem(name):
            return ctx.enter_context(nc.semaphore(name))

        used = {}

        def at(offset, name, shape, dt=F32):
            used[name] = offset + 32 * ((int(np.prod(shape[1:])) + 7) // 8)
            return nc.alloc_sbuf_tensor_at(name, shape, dt, offset=offset)

        class Region:
            def __init__(self, start, end):
                self.now, self.end = start, end

            def __call__(self, name, shape, dt=F32):
                t = at(self.now, name, shape, dt)
                self.now = used[name]
                assert self.now <= self.end, (name, self.now, self.end)
                return t

        HI = 32 * ((nc.sbuf_base + 31) // 32)
        LO = HI + KT * SEQ * 4
        u_hi = at(HI, "u_hi", [P, KT, SEQ], F32R)
        u_lo = at(LO, "u_lo", [P, SB, D_MODEL], F32R)
        x_rows = at(LO, "x_rows", [P, SB, D_MODEL])
        m_hi = at(HI, "m_hi", [P, KT, N_MEM], F32R)
        m_lo = at(HI + KT * N_MEM * 4, "m_lo", [P, KT, N_MEM], F32R)
        y_hi = at(HI, "y_hi", [P, KT, SEQ], F32R)
        y_lo = at(LO, "y_lo", [P, SB, D_MODEL], F32R)
        mem_rows = at(LO + 2 * D_MODEL * 4, "mem_rows", [P, MB, D_MODEL])
        x_fin = at(HI, "x_fin", [P, SB, D_MODEL])
        o_fin = at(LO, "o_fin", [P, SB, D_MODEL])

        top = nc.sbuf_usable_end
        W = Region(LO + KT * SEQ * 4, top)
        w_raw = W("w_raw", [P, RAW, BW])
        w_hi = W("w_hi", [P, RING, BW], F32R)
        w_lo = W("w_lo", [P, RING, BW], F32R)
        ident = W("ident", [P, P])
        ones = W("ones", [P, P])
        mask = W("mask", [P, 3 * P])
        gains = W("gains", [P, N_GAINS])
        par = W("par", [P, PAR])
        sinks = W("sinks", [P, HEADS])
        eps = W("eps", [P, 1])
        cdec = W("cdec", [P, 2 * LRU_TILES])
        tiny = W("tiny", [P, 48])
        stage = W("stage", [P, NT, SEQ])
        sq_acc = W("sq_acc", [P, SEQ])
        sq_tmp = W("sq_tmp", [P, SEQ])
        at_side = W.now

        R = Region(at_side, top)
        par_rows = R("par_rows", [P, 3, P])
        m_bn = R("m_bn", [P, MB, 8 * 6])
        m_mv = R("m_mv", [P, MB, 2])
        m_rstd = R("m_rstd", [P, MB])
        m_diag = R("m_diag", [P, MB, P])
        x_ss = R("x_ss", [P, SB, 4])
        x_rstd = R("x_rstd", [P, SB])
        x_sqs = R("x_sqs", [P, D_MODEL // 4])
        R.now = at_side + 20480
        m_rms = R("m_rms", [P, N_MEM])
        w_more = R("w_more", [P, MEM_RAW - RAW, BW])

        R = Region(at_side, top)
        r_bc = R("r_bc", [P, 3, SEQ])
        at_late = R.now
        rope_c = R("rope_c", [ROT, SEQ])
        rope_s = R("rope_s", [ROT, SEQ])
        rot = R("rot", [ROT, SEQ])
        at_mixer = R.now

        R = Region(at_mixer, top)
        l_in = R("l_in", [P, SEQ + 4])
        l_w_at = R.now
        l_w = R("l_w", [P, 2, 2, P])
        l_wlo = at(l_w_at, "l_wlo", [P, 2, 2, P], F32R)
        xc_lo = at(at_mixer, "xc_lo", [P, SEQ + 4], F32R)
        xc = R("xc", [P, SEQ])
        l_r = R("l_r", [P, 2, SEQ])
        l_i = R("l_i", [P, 2, SEQ])
        l_a = R("l_a", [P, 2, SEQ])
        l_whi = at(R.now, "l_whi", [P, 2, 2, P], F32R)
        l_t = R("l_t", [P, 2, SEQ])
        l_n = R("l_n", [P, 2, SEQ])
        l_h = l_t
        xc_hi = at(R.now, "xc_hi", [P, SEQ], F32R)
        l_y = R("l_y", [P, SEQ])

        R = Region(at_mixer, top)
        q_at, k_at, v_at = R.now, R.now + SEQ * 4, R.now + SEQ * 8
        q_raw = R("q_raw", [P, SEQ])
        k_raw = R("k_raw", [P, SEQ])
        v_raw = R("v_raw", [P, SEQ])
        q_lo = at(q_at, "q_lo", [P, SEQ], F32R)
        k_lo = at(k_at, "k_lo", [P, SEQ], F32R)
        v_lo = at(v_at, "v_lo", [P, SEQ], F32R)
        R.now += 32
        sink4 = R("sink4", [P, 4])
        srow = R("srow", [P, 24])
        q_hi = R("q_hi", [P, SEQ], F32R)
        k_hi = R("k_hi", [P, SEQ], F32R)
        v_hi = R("v_hi", [P, SEQ], F32R)
        probs = R("probs", [P, 2, 3 * P])
        pt_hi = R("pt_hi", [P, 10, P], F32R)
        pt_lo = R("pt_lo", [P, 10, P], F32R)
        y_sb = R("y_sb", [P, SEQ])

        R = Region(at_late, top)
        mq_raw = R("mq_raw", [P, 2, SEQ])
        mk_raw = R("mk_raw", [P, 2 * N_MEM])
        mq_lo = at(at_late, "mq_lo", [P, 2, SEQ], F32R)
        mk_lo = at(at_late + 2 * SEQ * 4, "mk_lo", [P, 2 * N_MEM], F32R)
        assert R.now == at_mixer
        mv_raw = R("mv_raw", [P, 2 * N_MEM])
        mrow = R("mrow", [P, 16])
        mq_hi = R("mq_hi", [P, 2, SEQ], F32R)
        mk_hi = R("mk_hi", [P, 2 * N_MEM], F32R)
        mv_hi = R("mv_hi", [P, MB * MEM_D], F32R)
        mv_lo = R("mv_lo", [P, MB * MEM_D], F32R)
        mp = R("mp", [P, SB, N_MEM])
        mpt_hi = R("mpt_hi", [P, MB, SEQ], F32R)
        m_y = R("m_y", [P, 2, SEQ])
        mpt_lo = R("mpt_lo", [P, MB, SEQ], F32R)

        R = Region(at_late, top)
        g_y = R("g_y", [P, NT, SEQ])
        g_hi = R("g_hi", [P, 2, SEQ], F32R)
        g_lo = R("g_lo", [P, 2, SEQ], F32R)
        o_buf = R("o_buf", [P, 2, SB, BW])
        post_row = R("post_row", [P, BW])
        o_ss = R("o_ss", [P, SB, 8])
        x_end = at(at_late, "x_end", [P, D_MODEL // 2])
        x_mid = at(used["g_lo"] + SB * BW * 4, "x_mid", [P, D_MODEL // 2])
        w_hi_more = at(at_side, "w_hi_more", [P, SKEW - RING, BW], F32R)
        w_lo_more = at(used["g_y"], "w_lo_more", [P, SKEW - RING, BW], F32R)

        G = [ctx.enter_context(nc.psum_tensor(f"gemm{n}", [P, SEQ], F32)) for n in range(NT)]
        X = [ctx.enter_context(nc.psum_tensor(f"side{n}", [P, SEQ], F32)) for n in range(4)]

        def scratch(name, shape, dt=F32):
            return nc.dram_tensor(name, shape, dt, kind="Internal").ap()

        kvT = scratch("kvT", [4 * BW, N_MEM])
        projT = scratch("projT", [10 * BW, SEQ])
        yT = scratch("yT", [D_MODEL, SEQ])
        gT_hi = scratch("gT_hi", [D_MODEL, SEQ])
        gT_lo = scratch("gT_lo", [D_MODEL, SEQ])
        o_rows = scratch("o_rows", [SEQ, D_MODEL])

        raw_in = [sem(f"raw_in{s}") for s in range(MEM_RAW)]
        hi_ready, lo_ready, unit_done = sem("hi_ready"), sem("lo_ready"), sem("unit_done")
        tile_done, act_evac, dve_evac = sem("tile_done"), sem("act_evac"), sem("dve_evac")
        sig_done, z_held = sem("sig_done"), sem("z_held")
        proj_stored, y_stored, g_stored = sem("proj_stored"), sem("y_stored"), sem("g_stored")
        ident_in, const_in, gain_in, par_in = (sem(n) for n in ("ident_in", "const_in", "gain_in", "par_in"))
        par_tr, par_ready = sem("par_tr"), sem("par_ready")
        memset_done, rope_in, cd_dve, cd_act = (sem(n) for n in ("memset_done", "rope_in", "cd_dve", "cd_act"))
        mem_in = [sem(f"mem_in{i}") for i in range(4)]
        m_stat, m_sqrt, m_rs, m_spread = sem("m_stat"), sem("m_sqrt"), sem("m_rs"), sem("m_spread")
        m_rms_set, kv_scaled = sem("m_rms_set"), sem("kv_scaled")
        m_trd, m_hid, m_lod = (sem(n) for n in ("m_trd", "m_hid", "m_lod"))
        xrow_in = [sem(f"xrow_in{i}") for i in range(SB)]
        x_sq, x_sum, x_sqrt, x_rs = (sem(n) for n in ("x_sq", "x_sum", "x_sqrt", "x_rs"))
        x_scl, x_trd, x_ev, u_split = (sem(n) for n in ("x_scl", "x_trd", "x_ev", "u_split"))
        swapped, rope_mul, rope_done = sem("swapped"), sem("rope_mul"), sem("rope_done")
        q_in, k_in, v_in = sem("q_in"), sem("k_in"), sem("v_in")
        q_hid, q_lod, k_hid, k_lod = (sem(n) for n in ("q_hid", "q_lod", "k_hid", "k_lod"))
        v_hid, v_lod = sem("v_hid"), sem("v_lod")
        scored, row_max, max_neg, sink_diff = (sem(n) for n in ("scored", "row_max", "max_neg", "sink_diff"))
        sink_set = sem("sink_set")
        exped, sink_exp, denom, recip, normed = (sem(n) for n in ("exped", "sink_exp", "denom", "recip", "normed"))
        p_trd, pt_hid, pt_lod, pv_done = (sem(n) for n in ("p_trd", "pt_hid", "pt_lod", "pv_done"))
        y_out, y_sq, y_acc, y_free = sem("y_out"), sem("y_sq"), sem("y_acc"), sem("y_free")
        l_zero, l_xin, l_win, conv = (sem(n) for n in ("l_zero", "l_xin", "l_win", "conv"))
        xc_hid, xc_lod, l_whid, l_wlod = (sem(n) for n in ("xc_hid", "xc_lod", "l_whid", "l_wlod"))
        l_mm, l_sig, l_exp, l_asq, l_ix = (sem(n) for n in ("l_mm", "l_sig", "l_exp", "l_asq", "l_ix"))
        l_neg, l_mult, l_b, l_scan, l_sum = (sem(n) for n in ("l_neg", "l_mult", "l_b", "l_scan", "l_sum"))
        mq_in, mk_in, mv_in = sem("mq_in"), sem("mk_in"), sem("mv_in")
        mq_hid, mq_lod, mk_hid, mk_lod = (sem(n) for n in ("mq_hid", "mq_lod", "mk_hid", "mk_lod"))
        mv_trd, mv_hid, mv_lod = sem("mv_trd"), sem("mv_hid"), sem("mv_lod")
        m_scored, m_max, m_neg, m_exp, m_rec, m_norm = (
            sem(n) for n in ("m_scored", "m_max", "m_neg", "m_exp", "m_rec", "m_norm"))
        mp_trd, mp_hid, mp_lod, m_pv, my_sq = (sem(n) for n in ("mp_trd", "mp_hid", "mp_lod", "m_pv", "my_sq"))
        r_sum, r_sqrt, r_ready = sem("r_sum"), sem("r_sqrt"), sem("r_ready")
        gy_in = [sem(f"gy_in{n}") for n in range(NT)]
        g_norm, g_mul, g_hid, g_lod = (sem(n) for n in ("g_norm", "g_mul", "g_hid", "g_lod"))
        y_in = [sem(f"y_in{i}") for i in range(4)]
        acc_zero, post_in, post_mul, o_sq, o_out = (
            sem(n) for n in ("acc_zero", "post_in", "post_mul", "o_sq", "o_out"))
        o_stored, o_free = sem("o_stored"), sem("o_free")
        passed = sem("passed")
        fin_in, last_in = sem("fin_in"), sem("last_in")
        f_sum, f_sqrt, f_rs, f_done, stored = (sem(n) for n in ("f_sum", "f_sqrt", "f_rs", "f_done", "stored"))

        block = ctx.enter_context(nc.Block())

        def f32(ap):
            return ap.bitcast(F32)

        def u_lo_tile(k):
            return u_lo[:, :, k * P:(k + 1) * P]

        def y_lo_tile(k):
            return y_lo[:, :, k * P:(k + 1) * P]

        def column(tile, i):
            return tile[:, i:i + 1] if isinstance(i, int) else tile[:, bass.ds(i, 1)]

        def m_lo_tile(k):
            return m_lo[:, k, :]

        def split_slot(B, k):
            if isinstance(B, int) and B == B_END - 1 and k >= KT - SKEW + RING:
                i = k - (KT - SKEW + RING)
                return w_hi_more[:, i, :], w_lo_more[:, i, :]
            return w_hi[:, k % RING, :], w_lo[:, k % RING, :]

        def raw_slot(B, k, mem=False):
            if mem or (isinstance(B, int) and B < B_MEM_END):
                i = k % MEM_RAW
                return (w_raw[:, i, :] if i < RAW else w_more[:, i - RAW, :]), raw_in[i], \
                    16 * (KT // MEM_RAW * B + k // MEM_RAW + 1)
            before = B_MEM_END * KT // MEM_RAW
            return w_raw[:, k % RAW, :], raw_in[k % RAW], \
                16 * (KT // RAW * B + (before - B_MEM_END * KT // RAW + k // RAW + 1))

        def start_counts(eng, *sems):
            for s in sems:
                eng.sem_inc(s, FIRST)

        @block.sync
        def _(sp):
            half = D_MODEL // 2
            rows = lambda v: v.rearrange("a (t p) -> (a t) p", p=P)

            def mem_load(c):
                sp.dma_start(mem_rows[:, :, c * 512:(c + 1) * 512],
                             mem[0, :, c * 512:(c + 1) * 512].rearrange("(b p) n -> p b n", p=P))\
                  .then_inc(mem_in[c % 4], 16)

            mem_load(0)
            sp.dma_start(ident[:, :], identity).then_inc(ident_in, 16)
            sp.dma_start(par_rows[0:KT, 1, :], rows(mem_g)).then_inc(gain_in, 16)

            def x_load(b, h):
                cols = slice(h * half, (h + 1) * half)
                sp.dma_start(x_rows[:, b, cols], x[0, b * P:(b + 1) * P, cols]).then_inc(xrow_in[b], 16)

            def weights(B, k, src, mem=False):
                place, loaded, _ = raw_slot(B, k, mem)
                if mem or (isinstance(B, int) and 32 * B + k < 32 * B_MEM_END + RAW):
                    if not (isinstance(B, int) and 32 * B + k < MEM_RAW):
                        sp.wait_ge(lo_ready, 32 * B + k - MEM_RAW + 1)
                else:
                    sp.wait_ge(lo_ready, 32 * B + k - RAW + 1)
                sp.dma_start(place, src).then_inc(loaded, 16)

            def w_block(B, mat, col, at_unit=None, mem=False):
                for k in range(KT):
                    if at_unit and mem:
                        at_unit(k)
                    weights(B, k, mat[0, k * P:(k + 1) * P, bass.ds(col * BW, BW)], mem)
                    if at_unit and not mem:
                        at_unit(k)

            def first_rows(k):
                for c in range(1, 8):
                    if k == max(4 * c - 5, 1):
                        mem_load(c)
                for i in range(3):
                    if k == 13 + 5 * i:
                        x_load(i // 2, i % 2)
                vectors = ((0, C_CONVW, conv_w.rearrange("a j c -> (a j) c")), (0, C_CONVB, conv_b),
                           (0, C_BA, b_a.rearrange("a d c -> (a d) c")),
                           (0, C_BX, b_x.rearrange("a d c -> (a d) c")),
                           (0, C_LAM, lam.rearrange("a d c -> (a d) c")),
                           (2, G_PRE, pre_g), (2, G_OUT, g_att), (2, G_OUT + 16, g_lru), (2, G_OUT + 24, g_mem))
                if 10 <= k < 10 + 2 * len(vectors) and k % 2 == 0:
                    group, at_row, v = vectors[(k - 10) // 2]
                    n = v.shape[0] * v.shape[1] // P
                    sp.dma_start(par_rows[at_row:at_row + n, group, :], rows(v)).then_inc(par_in, 16)
            w_block(0, w_mem, 0, first_rows, mem=True)

            def second_rows(k):
                if k == 1:
                    x_load(1, 1)
                for i in range(4):
                    if k == 8 + 4 * i:
                        if i == 0:
                            sp.wait_ge(m_trd, KT)
                            sp.wait_ge(m_stat, 16)
                        x_load(2 + i // 2, i % 2)
                if k == 24:
                    sp.dma_start(mask[:, :], band_mask).then_inc(const_in, 16)
                    sp.dma_start(sinks[:, :], sink.partition_broadcast(P)).then_inc(const_in, 16)
            w_block(1, w_mem, 1, second_rows, mem=True)
            with sp.Fori(2, B_MEM_END) as B:
                w_block(B, w_mem, B, mem=True)

            def ropes(k):
                if k == 0:
                    sp.dma_start(rope_c[:, :], rope_cos).then_inc(rope_in, 16)
                    sp.dma_start(rope_s[:, :], rope_sin).then_inc(rope_in, 16)
            w_block(B_XLRU, w_in, 6, ropes)
            w_block(B_XLRU + 1, w_in, 7)

            def lru_loads(B):
                def go(k):
                    for i, s in enumerate(TILE_AT):
                        if k == s:
                            t = (B - B_LRU) * 2 + i
                            sp.wait_ge(l_zero, 2)
                            sp.wait_ge(proj_stored, 64 * B - 64)
                            sp.wait_ge(l_mm, FIRST + 4 * t)
                            sp.dma_start(l_in[:, 2:2 + SEQ], projT[bass.ds(t * P, P), :]).then_inc(l_xin, 16)
                            for which, w in enumerate((w_a, w_x)):
                                sp.dma_start(l_w[:, which, :, :],
                                             w[0, :, bass.ds(t, 1), :, :].rearrange("d t c e -> c (d t) e"))\
                                  .then_inc(l_win, 16)
                return go
            with sp.Fori(B_LRU, B_Q) as B:
                w_block(B, w_in, B - 2, lru_loads(B))
            with sp.Fori(B_Q, B_ATT) as B:
                w_block(B, w_in, B - B_Q, lru_loads(B))

            def att_loads(B):
                def go(k):
                    g = B - B_ATT
                    if k == 0:
                        sp.wait_ge(proj_stored, 64 * B_Q)
                        sp.wait_ge(conv, FIRST + 4 * LRU_TILES)
                        sp.wait_ge(l_mm, FIRST + 4 * LRU_TILES)
                        sp.wait_ge(l_ix, FIRST + 2 * LRU_TILES)
                        sp.wait_ge(scored, FIRST + 16 * g)
                        sp.dma_start(k_raw[:, :], projT[bass.ds(g * P + 2 * BW, P), :]).then_inc(k_in, 16)
                    for i, s in enumerate(HEAD_AT):
                        if k == (1 if i == 0 else HEAD_AT[i - 1] + 9):
                            if i == 0:
                                sp.wait_ge(proj_stored, 64 * B - 64)
                            sp.wait_ge(scored, FIRST + 16 * g + 4 * i)
                            sp.dma_start(q_raw[:, :], projT[bass.ds(g * BW + (4 * BW + i * P), P), :])\
                              .then_inc(q_in, 16)
                    if k == 3:
                        sp.wait_ge(pv_done, FIRST + 4 * g)
                        sp.dma_start(v_raw[:, :].rearrange("p (b d) -> p b d", b=SB),
                                     projT[3 * BW:4 * BW, bass.ds(g * P, P)].rearrange("(b p) d -> p b d", p=P))\
                          .then_inc(v_in, 16)
                return go
            with sp.Fori(B_ATT, B_ATT + 2) as B:
                w_block(B, w_in, B - B_Q, att_loads(B))
            with sp.Fori(B_ATT + 2, B_MEMATT) as B:
                w_block(B, w_in, B - 4, att_loads(B))

            def mem_loads(k):
                for h, s in enumerate(MEMHEAD_AT):
                    at0 = s + 4
                    if k == at0:
                        sp.wait_ge(proj_stored, 64 * (13 + min(h, 1)))
                        if h:
                            sp.wait_ge(m_scored, 2 * h)
                        else:
                            sp.wait_ge(scored, FIRST + 4 * HEADS)
                        sp.dma_start(mk_raw[:, :].rearrange("p (t m) -> p t m", t=2),
                                     kvT[h * MEM_D:(h + 1) * MEM_D, :].rearrange("(t p) m -> p t m", p=P))\
                          .then_inc(mk_in, 16)
                        if h:
                            sp.wait_ge(mv_trd, h)
                        sp.dma_start(mv_raw[:, :].rearrange("p (t m) -> p t m", t=2),
                                     kvT[2 * BW + h * MEM_D:2 * BW + (h + 1) * MEM_D, :]
                                     .rearrange("(t p) m -> p t m", p=P)).then_inc(mv_in, 16)
                        sp.dma_start(mq_raw[:, :, :], projT[8 * BW + h * MEM_D:8 * BW + (h + 1) * MEM_D, :]
                                     .rearrange("(t p) n -> p t n", p=P)).then_inc(mq_in, 16)

            w_block(B_MEMATT, w_in, 10, mem_loads)

            def gate_loads(B):
                def go(k):
                    n = k - 9
                    if 0 <= n < NT:
                        if n == 0:
                            sp.wait_ge(y_stored, 16 * 32)
                        sp.wait_ge(g_mul, FIRST + 4 * (B - B_Z - 1) + n)
                        if not (isinstance(B, int) and B == B_Z + 1):
                            sp.wait_ge(g_norm, FIRST + 4 * (B - B_Z - 1))
                        sp.wait_ge(g_lod, FIRST + 4 * (B - B_Z - 1))
                        sp.dma_start(g_y[:, n, :], yT[bass.ds((B - (B_Z + 1)) * BW + n * P, P), :]).then_inc(gy_in[n], 16)
                return go
            with sp.Fori(B_Z + 1, B_OUT - 1) as B:
                w_block(B, w_in, B - 4, gate_loads(B))

            def y_load(t):
                sp.wait_ge(unit_done, 32 * (B_OUT - 1) + t + 1)
                sp.wait_ge(g_stored, 128 * (t // NT + 1))
                sp.dma_start(f32(y_hi[:, t, :]), gT_hi[t * P:(t + 1) * P, :]).then_inc(y_in[t // 8], 16)
                sp.dma_start(f32(y_lo_tile(t)), gT_lo[t * P:(t + 1) * P, :].rearrange("p (b n) -> p b n", b=SB))\
                  .then_inc(y_in[t // 8], 16)

            def first_y_loads(k):
                gate_loads(B_OUT - 1)(k)
                if k >= 13:
                    y_load(k - 13)
            w_block(B_OUT - 1, w_in, B_OUT - 5, first_y_loads)

            def post_load(B, k):
                if k == 16:
                    if not (isinstance(B, int) and B == B_OUT):
                        sp.wait_ge(post_mul, 4 * (B - B_OUT))
                    sp.dma_start(post_row[:, :], post_g[0:1, bass.ds((B - B_OUT) * BW, BW)].partition_broadcast(P))\
                      .then_inc(post_in, 16)

            def last_y_loads(k):
                gate_loads(B_OUT)(k)
                if k < 9:
                    y_load(KT - 13 + k)
                if k == 22:
                    for t in range(28, KT):
                        y_load(t)
                post_load(B_OUT, k)
            w_block(B_OUT, w_out, 0, last_y_loads)
            with sp.Fori(B_OUT + 1, B_END - 1) as B:
                w_block(B, w_out, B - B_OUT, lambda k: post_load(B, k))

            def fin_load(j, loaded):
                sp.wait_ge(unit_done, 32 * (B_END - 1) + 4 * j + 4)
                sp.wait_ge(o_stored, 16 * 6)
                c, cols = j // 2, slice((j % 2) * half, (j % 2 + 1) * half)
                sp.dma_start(x_fin[:, c, cols], x[0, c * P:(c + 1) * P, cols]).then_inc(loaded, 16)
                sp.dma_start(o_fin[:, :, j * BW:(j + 1) * BW],
                             o_rows[:, j * BW:(j + 1) * BW].rearrange("(b p) n -> p b n", p=P)).then_inc(loaded, 16)

            def last_loads(k):
                post_load(B_END - 1, k)
                if k == 4:
                    sp.wait_ge(g_stored, 128 * 8)
                    sp.dma_start(x_end[:, :], x[0, 3 * P:4 * P, half:2 * half]).then_inc(fin_in, 16)
                if k == 6:
                    sp.wait_ge(o_stored, 16 * 6)
                    sp.dma_start(x_mid[:, :], x[0, 3 * P:4 * P, 0:half]).then_inc(fin_in, 16)
                if k >= 12 and k % 4 == 0:
                    fin_load((k - 12) // 4, fin_in)
            w_block(B_END - 1, w_out, 7, last_loads)
            fin_load(5, last_in)
            for i, (c, q) in enumerate(FINAL):
                cols = slice(q * 1024, (q + 1) * 1024)
                sp.wait_ge(f_done, i + 1)
                sp.dma_start(out[0, c * P:(c + 1) * P, cols], o_fin[:, c, cols]).then_inc(stored, 16)
            sp.wait_ge(stored, 16 * len(FINAL))

        @block.tensor
        def _(pe):
            start_counts(pe, l_mm, p_trd, pv_done, scored, x_trd)
            def unit(B, k, hi, lo, width, bank_free):
                pe.wait_ge(lo_ready, 32 * B + k + 1)
                slot = k % RING
                for n in range(NT):
                    if k == 0:
                        bank_free(n)
                    cols = slice(n * P, (n + 1) * P)
                    acc = G[n][:, 0:width]
                    pe.matmul(acc, w_hi[:, slot, cols], hi[:, k, :], start=(k == 0), stop=False)
                    pe.matmul(acc, w_hi[:, slot, cols], lo(k), start=False, stop=False)
                    mm = pe.matmul(acc, w_lo[:, slot, cols], hi[:, k, :], start=False, stop=(k == KT - 1))
                    if n == NT - 1:
                        mm.then_inc(unit_done, 1)
                    elif k == KT - 1:
                        mm.then_inc(tile_done, 1)

            def after_copy(B):
                done = 2 * B - 2

                def wait(n):
                    pe.wait_ge(dve_evac if n % 2 else act_evac, done + n // 2 + 1)
                return wait

            def after_gate(B):
                def wait(n):
                    pe.wait_ge(z_held, 4 * (B - 1 - B_Z) + n + 1)
                return wait

            def gemm(B, hi, lo, width=SEQ, bank_free=None, at_unit=None):
                for k in range(KT):
                    if at_unit:
                        at_unit(k)
                    unit(B, k, hi, lo, width, bank_free or after_copy(B))

            def rows_tile(B, k, n, hi, lo):
                wh, wl = split_slot(B, k)
                hi_n, lo_n = hi[:, k, n * P:(n + 1) * P], lo[:, n, k * P:(k + 1) * P]
                acc = G[n][:, :]
                pe.matmul(acc, hi_n, wh, start=(k == 0), stop=False)
                pe.matmul(acc, hi_n, wl, start=False, stop=False)
                return pe.matmul(acc, lo_n, wh, start=False, stop=(k == KT - 1))

            def rows_gemm(B, hi, lo, bank_free, at_unit=None, units=KT):
                for k in range(units):
                    if at_unit:
                        at_unit(k)
                    pe.wait_ge(lo_ready, 32 * B + k + 1)
                    for n in range(SB):
                        if k == 0:
                            bank_free(n)
                        mm = rows_tile(B, k, n, hi, lo)
                        if n == SB - 1:
                            mm.then_inc(unit_done, 1)
                        elif k == KT - 1:
                            mm.then_inc(tile_done, 1)

            pe.wait_ge(ident_in, 16)
            pe.wait_ge(gain_in, 16)
            pe.transpose(X[2][:, 0:KT], par_rows[0:KT, 1, :], ident[0:KT, 0:KT]).then_inc(par_tr, 1)

            def mem_transpose(t):
                if t >= KT:
                    return
                if t % 4 == 0:
                    pe.wait_ge(mem_in[t // 4 % 4], 16 * (t // 16 + 1))
                if t >= 4:
                    pe.wait_ge(m_lod, t - 3)
                elif t == 2:
                    pe.wait_ge(par_ready, 1)
                for b in range(MB):
                    tr = pe.transpose(X[t % 4][:, b * P:(b + 1) * P], mem_rows[:, b, t * P:(t + 1) * P],
                                      ident[:, :])
                tr.then_inc(m_trd, 1)

            for t in range(4):
                mem_transpose(t)
            gemm(0, m_hi, m_lo_tile, N_MEM, lambda n: None, lambda k: mem_transpose(k + 4))

            def spread_rms(k):
                if k == 1:
                    pe.wait_ge(memset_done, 2)
                    pe.wait_ge(m_rs, 1 + MB)
                    pe.wait_ge(m_lod, KT)
                    for b in range(MB):
                        mm = pe.matmul(X[0][:, b * P:(b + 1) * P], ones[:, :], m_diag[:, b, :], start=True, stop=True)
                    mm.then_inc(m_spread, 1)
                if k == 8:
                    pe.wait_ge(par_in, 16 * 9)
                    pe.transpose(X[3][:, 0:PAR], par_rows[0:PAR, 0, :], ident[0:PAR, 0:PAR]).then_inc(par_tr, 1)
                    pe.transpose(X[2][:, 0:G_MEM], par_rows[0:G_MEM, 2, :], ident[0:G_MEM, 0:G_MEM])\
                      .then_inc(par_tr, 1)
            gemm(1, m_hi, m_lo_tile, N_MEM, at_unit=spread_rms)

            for B in range(2, B_MEM_END):
                def x_transpose(k):
                    if k % 2:
                        t = 16 * (B - 2) + k // 2
                        pe.wait_ge(x_scl, t + 1)
                        if t >= 4:
                            pe.wait_ge(x_ev, FIRST + t - 3)
                        else:
                            pe.wait_ge(m_rms_set, 1)
                            pe.wait_ge(par_ready, 3)
                        for b in range(SB):
                            tr = pe.transpose(X[t % 4][:, b * P:(b + 1) * P], x_rows[:, b, t * P:(t + 1) * P],
                                              ident[:, :])
                        tr.then_inc(x_trd, 1)
                gemm(B, m_hi, m_lo_tile, N_MEM, at_unit=x_transpose)
            with pe.Fori(B_XLRU, B_LRU) as B:
                gemm(B, u_hi, u_lo_tile)

            def lru(B):
                def go(k):
                    for i, s in enumerate(TILE_AT):
                        for which in range(2):
                            if k == s + 5 + which:
                                t = 2 * (B - B_LRU) + i
                                pe.wait_ge(xc_lod, t + 1)
                                pe.wait_ge(l_wlod, t + 1)
                                for d in range(2):
                                    n = 2 * which + d
                                    pe.wait_ge(l_sig, FIRST + 4 * t)
                                    lo = xc_lo[:, 2:2 + SEQ]
                                    pe.matmul(X[n][:, :], l_whi[:, which, d, :], xc_hi[:, :], start=True, stop=False)
                                    pe.matmul(X[n][:, :], l_whi[:, which, d, :], lo, start=False, stop=False)
                                    pe.matmul(X[n][:, :], l_wlo[:, which, d, :], xc_hi[:, :],
                                              start=False, stop=True).then_inc(l_mm, 1)
                return go
            gemm(B_K, u_hi, u_lo_tile, at_unit=lru(B_K))
            rows_gemm(B_V, u_hi, u_lo, after_copy(B_V), lru(B_V))
            with pe.Fori(B_Q, B_ATT) as B:
                gemm(B, u_hi, u_lo_tile, at_unit=lru(B))

            def attention(B):
                g = B - B_ATT

                def scores(h, i):
                    if i < 2:
                        pe.wait_ge(row_max, FIRST + 4 * h)
                    else:
                        pe.wait_ge(row_max, FIRST + 4 * h + i - 1)
                    k0, nk = BAND[i]
                    q, kk = slice(i * P, (i + 1) * P), slice(k0 * P, (k0 + nk) * P)
                    s = X[i % 2][:, 0:nk * P]
                    pe.matmul(s, q_hi[:, q], k_hi[:, kk], start=True, stop=False)
                    pe.matmul(s, q_hi[:, q], k_lo[:, kk], start=False, stop=False)
                    pe.matmul(s, q_lo[:, q], k_hi[:, kk], start=False, stop=True).then_inc(scored, 1)

                def turn(h, i):
                    pe.wait_ge(normed, 4 * h + i + 1)
                    if i < 2:
                        pe.wait_ge(pt_lod, FIRST + 4 * h)
                        pe.wait_ge(y_sq, FIRST + LRU_TILES + h)
                    else:
                        pe.wait_ge(pt_lod, FIRST + 4 * h + i - 1)
                    for j in range(BAND[i][1]):
                        tr = pe.transpose(X[2 + i % 2][:, j * P:(j + 1) * P], probs[:, i % 2, j * P:(j + 1) * P],
                                          ident[:, :])
                    tr.then_inc(p_trd, 1)

                def values(h):
                    pe.wait_ge(pt_lod, FIRST + 4 * h + 4)
                    pe.wait_ge(v_lod, g + 1)
                    for kb in range(SB):
                        q0, nq = BAND[kb]
                        o = X[2][:, q0 * P:(q0 + nq) * P]
                        v = slice(kb * P, (kb + 1) * P)
                        ph = pt_hi[:, PT_AT[kb]:PT_AT[kb] + nq, :]
                        pl = pt_lo[:, PT_AT[kb]:PT_AT[kb] + nq, :]
                        pe.matmul(o, v_hi[:, v], ph, start=(kb == 0), stop=False, skip_group_check=True)
                        pe.matmul(o, v_hi[:, v], pl, start=False, stop=False, skip_group_check=True)
                        mm = pe.matmul(o, v_lo[:, v], ph, start=False, stop=(kb == SB - 1), skip_group_check=True)
                    mm.then_inc(pv_done, 1)

                def go(k):
                    for i, s in enumerate(HEAD_AT):
                        h = 4 * g + i
                        if k == s + 8:
                            values(h)
                    for i, s in enumerate(HEAD_AT):
                        h = 4 * g + i
                        if k == s + 1:
                            pe.wait_ge(q_lod, FIRST + h + 1)
                            if i == 0:
                                pe.wait_ge(k_lod, FIRST + g + 1)
                                pe.wait_ge(l_sig, FIRST + 4 * LRU_TILES)
                            scores(h, 0)
                            scores(h, 1)
                        if k == s + 3:
                            turn(h, 0)
                            turn(h, 1)
                            scores(h, 2)
                            scores(h, 3)
                        if k == s + 6:
                            turn(h, 2)
                            turn(h, 3)
                return go
            with pe.Fori(B_ATT, B_MEMATT) as B:
                gemm(B, u_hi, u_lo_tile, at_unit=attention(B))

            def out_norm(squares, bank):
                pe.matmul(X[bank][:, :], ones[:, :], squares, start=True, stop=True).then_inc(r_sum, 1)

            def mem_attention(k):
                if k == 3:
                    pe.wait_ge(y_acc, FIRST + 24)
                    pe.wait_ge(memset_done, 2)
                    out_norm(sq_acc[:, :], 0)
                    out_norm(r_bc[:, 1, :], 1)
                for h, s in enumerate(MEMHEAD_AT):
                    if k == s + 9:
                        mem_values(h)
                for h, s in enumerate(MEMHEAD_AT):
                    if k == s + 1:
                        pe.wait_ge(mv_in, 16 * h + 16)
                        if h:
                            pe.wait_ge(mp_lod, 2 * h)
                        for b in range(MB):
                            for t in range(2):
                                tr = pe.transpose(X[2][:, (2 * b + t) * P:(2 * b + t + 1) * P],
                                                  mv_raw[:, t * N_MEM + b * P:t * N_MEM + (b + 1) * P], ident[:, :])
                        tr.then_inc(mv_trd, 1)
                    if k == s + 4:
                        pe.wait_ge(mk_lod, h + 1)
                        pe.wait_ge(mq_lod, 2 * h + 2)
                        pe.wait_ge(r_sqrt, 2)
                        pe.wait_ge(y_out, HEADS + 2 * h)
                        for i in range(SB):
                            o = X[i // 2][:, (i % 2) * N_MEM:(i % 2 + 1) * N_MEM]
                            q = slice(i * P, (i + 1) * P)
                            for t in range(2):
                                kk = slice(t * N_MEM, (t + 1) * N_MEM)
                                pe.matmul(o, mq_hi[:, t, q], mk_hi[:, kk], start=(i % 2 == 0 and t == 0), stop=False,
                                          skip_group_check=True)
                                pe.matmul(o, mq_hi[:, t, q], mk_lo[:, kk], start=False, stop=False,
                                          skip_group_check=True)
                                mm = pe.matmul(o, mq_lo[:, t, q], mk_hi[:, kk], start=False,
                                               stop=(t == 1), skip_group_check=True)
                            if i % 2:
                                mm.then_inc(m_scored, 1)
                    if k == s + 7:
                        pe.wait_ge(m_norm, SB * h + SB)
                        pe.wait_ge(mv_lod, h + 1)
                        for b in range(MB):
                            for i in range(SB):
                                tr = pe.transpose(X[2 + b][:, i * P:(i + 1) * P], mp[:, i, b * P:(b + 1) * P],
                                                  ident[:, :])
                            tr.then_inc(mp_trd, 1)

            def mem_values(h):
                pe.wait_ge(mp_lod, 2 * h + 2)
                pe.wait_ge(m_exp, SB * h + SB)
                for t in range(2):
                    for b in range(MB):
                        v = slice(b * MEM_D + t * P, b * MEM_D + (t + 1) * P)
                        pe.matmul(X[t][:, :], mv_hi[:, v], mpt_hi[:, b, :], start=(b == 0), stop=False)
                        pe.matmul(X[t][:, :], mv_hi[:, v], mpt_lo[:, b, :], start=False, stop=False)
                        mm = pe.matmul(X[t][:, :], mv_lo[:, v], mpt_hi[:, b, :], start=False, stop=(b == MB - 1))
                    mm.then_inc(m_pv, 1)
            gemm(B_MEMATT, u_hi, u_lo_tile, at_unit=mem_attention)

            def mem_norm(k):
                if k == 8:
                    pe.wait_ge(y_acc, FIRST + 32)
                    out_norm(r_bc[:, 2, :], 2)
            gemm(B_Z + 1, u_hi, u_lo_tile, bank_free=after_gate(B_Z + 1), at_unit=mem_norm)
            with pe.Fori(B_Z + 2, B_OUT) as B:
                gemm(B, u_hi, u_lo_tile, bank_free=after_gate(B))

            def y_ready(k):
                if k % 8 == 0:
                    pe.wait_ge(y_in[k // 8], 256)

            def after_out(B):
                def wait(n):
                    pe.wait_ge(o_out, 4 * (B - 1 - B_OUT) + n + 1)
                return wait
            rows_gemm(B_OUT, y_hi, y_lo, after_gate(B_OUT), y_ready)
            with pe.Fori(B_OUT + 1, B_END - 1) as B:
                rows_gemm(B, y_hi, y_lo, after_out(B))
            rows_gemm(B_END - 1, y_hi, y_lo, after_out(B_END - 1), units=KT - SKEW)
            for n in range(SB):
                for k in range(KT - SKEW, KT):
                    if n == 0:
                        pe.wait_ge(lo_ready, 32 * (B_END - 1) + k + 1)
                    mm = rows_tile(B_END - 1, k, n, y_hi, y_lo)
                if n < SB - 1:
                    mm.then_inc(tile_done, 1)
                else:
                    mm.then_inc(unit_done, SKEW)

        @block.scalar
        def _(act):
            start_counts(act, l_sig, x_ev, y_sq)
            def split(B, k):
                raw, loaded, count = raw_slot(B, k)
                act.wait_ge(loaded, count)
                if isinstance(B, int) and (32 * B + k < RING or B == B_END - 1 and k >= KT - SKEW + RING):
                    pass
                else:
                    act.wait_ge(unit_done, 32 * B + k - RING + 1)
                act.copy(split_slot(B, k)[0], raw).then_inc(hi_ready, 1)

            def u_part(k):
                act.wait_ge(x_ev, FIRST + k + 1)
                act.copy(u_hi[:, k, :].rearrange("p (b n) -> p b n", b=SB), x_rows[:, :, k * P:(k + 1) * P])\
                   .then_inc(u_split, 1)

            def evac(B, width=SEQ):
                for n in (0, 2):
                    act.wait_ge(tile_done, 3 * B + n + 1)
                    act.copy(stage[:, n, 0:width], G[n][:, 0:width]).then_inc(act_evac, 1)

            def body(B, side=None, before=None, evacuate=evac):
                for j in range(LEAD, KT + LEAD):
                    b, k = (B, j) if j < KT else (B + 1, j - KT)
                    if before:
                        before(j)
                    if not (isinstance(B, int) and B == B_END - 1 and j >= KT):
                        split(b, k)
                    if side:
                        side(j - LEAD)
                evacuate(B)

            def proj_evac(B, width=SEQ):
                act.wait_ge(proj_stored, 64 * B)
                evac(B, width)

            def m_part(t):
                act.wait_ge(m_trd, t + 1)
                act.activation(m_hi[:, t, :], X[t % 4][:, 0:N_MEM], ACT.Copy,
                               scale=gains[:, G_MEM + t:G_MEM + t + 1]).then_inc(m_hid, 1)

            act.wait_ge(par_tr, 1)
            act.copy(gains[:, G_MEM:N_GAINS], X[2][:, 0:KT]).then_inc(par_ready, 1)
            act.wait_ge(par_ready, 1)
            for k in range(LEAD):
                m_part(k)
                split(0, k)

            def x_square(q):
                b, c = q // 4, q % 4
                act.wait_ge(xrow_in[b], 32)
                if q:
                    act.wait_ge(x_sq, q)
                act.activation(x_sqs[:, :], x_rows[:, b, c * 1024:(c + 1) * 1024], ACT.Square,
                               accum_out=x_ss[:, b, c:c + 1]).then_inc(x_sq, 1)

            def first_side(t):
                if t == 30:
                    act.wait_ge(m_stat, 20)
                    act.activation(m_rstd[:, :], m_mv[:, :, 1], ACT.Sqrt).then_inc(m_sqrt, 1)
                if 20 <= t < 28 and t % 2 == 0:
                    x_square((t - 20) // 2)
            body(0, first_side, lambda j: m_part(j) if j < KT else None, lambda B: proj_evac(B, N_MEM))

            def second_side(t):
                if 3 <= t < 11 and t % 2:
                    x_square(4 + (t - 3) // 2)
                if t == 10:
                    act.wait_ge(par_tr, 2)
                    act.copy(par[:, :], X[3][:, 0:PAR]).then_inc(par_ready, 1)
                    act.wait_ge(par_tr, 3)
                    act.copy(gains[:, 0:G_MEM], X[2][:, 0:G_MEM]).then_inc(par_ready, 1)
                if t >= 15 and t % 2 and t < 31:
                    x_square(8 + (t - 15) // 2)
                if t == 31:
                    act.wait_ge(x_sum, 2)
                    act.activation(x_rstd[:, :], x_rstd[:, :], ACT.Sqrt).then_inc(x_sqrt, 1)
            body(1, second_side, evacuate=lambda B: proj_evac(B, N_MEM))

            def x_out(B):
                def go(t):
                    if t % 2 == 1:
                        kt = 16 * (B - 2) + t // 2
                        act.wait_ge(x_trd, FIRST + kt + 1)
                        act.activation(x_rows[:, :, kt * P:(kt + 1) * P],
                                       X[(t // 2) % 4][:, :].rearrange("p (b n) -> p b n", b=SB), ACT.Copy,
                                       scale=gains[:, G_PRE + kt:G_PRE + kt + 1]).then_inc(x_ev, 1)
                return go
            body(2, x_out(2), evacuate=lambda B: proj_evac(B, N_MEM))
            body(3, x_out(3), before=lambda j: u_part(j - KT) if j >= KT else None,
                 evacuate=lambda B: proj_evac(B, N_MEM))
            body(B_XLRU, before=lambda j: u_part(j) if j < KT else None, evacuate=proj_evac)

            def decay(t):
                if t == 12:
                    act.wait_ge(cd_dve, 2)
                    act.activation(tiny[:, 0:16], tiny[:, 0:16], ACT.Exp, scale=-1.0).then_inc(cd_act, 1)
            body(B_XLRU + 1, decay, evacuate=proj_evac)

            with act.Fori(B_LRU, B_ATT) as B:
                def lru(t):
                    for i, s in enumerate(TILE_AT):
                        T = 2 * (B - B_LRU) + i
                        if t == s + 2:
                            act.wait_ge(l_win, 32 * T + 32)
                            act.wait_ge(y_sq, FIRST + T)
                            act.copy(l_whi[:, :, :, :], l_w[:, :, :, :]).then_inc(l_whid, 1)
                        if t == s + 4:
                            act.wait_ge(conv, FIRST + 4 * T + 4)
                            act.wait_ge(y_free, FIRST + T)
                            act.copy(xc_hi[:, :], xc[:, :]).then_inc(xc_hid, 1)
                        for which, (o, c) in enumerate(((l_r, C_BA), (l_i, C_BX))):
                            if t == s + 5 + which:
                                for d in range(2):
                                    act.wait_ge(l_mm, FIRST + 4 * T + 2 * which + d + 1)
                                    act.wait_ge(l_b, FIRST + 2 * T)
                                    act.activation(o[:, d, :], X[2 * which + d][:, :], ACT.Sigmoid,
                                                   bias=par[:, bass.ds(T + c + 8 * d, 1)]).then_inc(l_sig, 1)
                        for d in range(2):
                            if t == s + 7 + d:
                                act.wait_ge(l_scan, FIRST + 2 * T)
                                act.wait_ge(y_sq, FIRST + T)
                                act.wait_ge(l_sig, FIRST + 4 * T + 2)
                                c = cdec[:, bass.ds(T + 8 * d, 1)]
                                act.activation(l_a[:, d, :], l_r[:, d, :], ACT.Exp, scale=c).then_inc(l_exp, 1)
                                act.activation(l_t[:, d, :], l_r[:, d, :], ACT.Tanh, scale=c).then_inc(l_exp, 1)
                        if t == s + 10:
                            for d in range(2):
                                act.wait_ge(l_neg, FIRST + 2 * T + d + 1)
                                act.activation(l_n[:, d, :], l_n[:, d, :], ACT.Sqrt, scale=-1.0).then_inc(l_mult, 1)
                        if t == s + 15:
                            act.wait_ge(l_sum, T + 1)
                            act.wait_ge(y_acc, FIRST + T)
                            act.activation(sq_tmp[:, :], l_y[:, :], ACT.Square).then_inc(y_sq, 1)
                body(B, lru, evacuate=proj_evac)

            def attention(B):
                g = B - B_ATT

                def go(t):
                    if t == 0:
                        act.wait_ge(k_in, 16 * g + 16)
                        act.wait_ge(l_sum, LRU_TILES)
                        act.wait_ge(scored, FIRST + 16 * g)
                        act.copy(k_hi[:, :], k_raw[:, :]).then_inc(k_hid, 1)
                    if t == 2:
                        act.wait_ge(v_in, 16 * g + 16)
                        act.wait_ge(pv_done, FIRST + 4 * g)
                        act.copy(v_hi[:, :], v_raw[:, :]).then_inc(v_hid, 1)
                    for i, s in enumerate(HEAD_AT):
                        h = 4 * g + i
                        if t == s + 8:
                            act.wait_ge(pv_done, FIRST + h + 1)
                            act.wait_ge(y_free, FIRST + LRU_TILES + h)
                            act.copy(y_sb[:, :], X[2][:, :]).then_inc(y_out, 1)
                            act.wait_ge(y_acc, FIRST + LRU_TILES + h)
                            act.activation(sq_tmp[:, :], X[2][:, :], ACT.Square).then_inc(y_sq, 1)
                    for i, s in enumerate(HEAD_AT):
                        h = 4 * g + i
                        if t == s:
                            act.wait_ge(q_in, 16 * h + 16)
                            act.wait_ge(scored, FIRST + 4 * h)
                            act.copy(q_hi[:, :], q_raw[:, :]).then_inc(q_hid, 1)
                        for pair in range(2):
                            if t == s + 1 + 3 * pair:
                                act.wait_ge(max_neg, 2 * h + pair + 1)
                                for e in range(2):
                                    b = 2 * pair + e
                                    pr = probs[:, e, 0:BAND[b][1] * P]
                                    act.activation(pr, pr, ACT.Exp, bias=srow[:, 4 + e:5 + e],
                                                   accum_out=srow[:, 8 + e:9 + e]).then_inc(exped, 1)
                                act.wait_ge(sink_diff, 2 * h + pair + 1)
                                act.activation(srow[:, 16:18], srow[:, 12:14], ACT.Exp).then_inc(sink_exp, 1)
                            if t == s + 3 + 3 * pair:
                                for b in (2 * pair, 2 * pair + 1):
                                    nk = BAND[b][1]
                                    act.wait_ge(p_trd, FIRST + 4 * h + b + 1)
                                    act.wait_ge(pv_done, FIRST + h)
                                    act.copy(pt_hi[:, PT_FIRST[b]:PT_FIRST[b] + 2 * nk - 1:2, :],
                                             X[2 + b % 2][:, 0:nk * P].rearrange("p (j q) -> p j q", q=P))\
                                       .then_inc(pt_hid, 1)
                return go
            with act.Fori(B_ATT, B_MEMATT) as B:
                body(B, attention(B), evacuate=proj_evac)

            def bring_sigmoid():
                act.activation(tiny[:, 32:33], eps[:, :], ACT.Sigmoid)

            def rms(which, bank, width):
                act.wait_ge(r_sum, which + 1)
                act.activation(r_bc[:, which, :], X[bank][:, :], ACT.Sqrt, bias=eps[:, :],
                               scale=1.0 / width).then_inc(r_sqrt, 1)

            def sigmoids(B):
                for n in range(NT):
                    if n < NT - 1:
                        act.wait_ge(tile_done, 3 * B + n + 1)
                    else:
                        act.wait_ge(unit_done, 32 * B + 32)
                    if n == 0:
                        if isinstance(B, int) and B == B_Z:
                            act.wait_ge(proj_stored, 64 * 14)
                        act.wait_ge(g_mul, FIRST + 4 * (B - B_Z))
                    act.activation(stage[:, n, :], G[n][:, :], ACT.Sigmoid).then_inc(sig_done, 1)

            def mem_attention(t):
                if t == 30:
                    bring_sigmoid()
                if t == 3:
                    rms(0, 0, 2048.0)
                    rms(1, 1, 1024.0)
                for h, s in enumerate(MEMHEAD_AT):
                    if t == s + 9:
                        for d in range(2):
                            act.wait_ge(m_pv, 2 * h + d + 1)
                            if h and d == 0:
                                act.wait_ge(y_stored, 16 * (24 + 2 * h))
                                act.wait_ge(y_acc, FIRST + 24 + 2 * h)
                            act.copy(m_y[:, d, :], X[d][:, :]).then_inc(y_out, 1)
                for h, s in enumerate(MEMHEAD_AT):
                    if t == s + 1:
                        act.wait_ge(mk_in, 16 * h + 16)
                        act.wait_ge(m_scored, 2 * h)
                        act.copy(mk_hi[:, :], mk_raw[:, :]).then_inc(mk_hid, 1)
                        act.wait_ge(mv_trd, h + 1)
                        act.wait_ge(m_pv, 2 * h)
                        act.copy(mv_hi[:, :], X[2][:, :]).then_inc(mv_hid, 1)
                    for d in range(2):
                        if t == s + 1 + 2 * d:
                            act.wait_ge(mq_in, 16 * h + 16)
                            act.wait_ge(m_scored, 2 * h)
                            act.copy(mq_hi[:, d, :], mq_raw[:, d, :]).then_inc(mq_hid, 1)
                    if t == s + 4:
                        for i in range(SB):
                            act.wait_ge(m_neg, 2 * h + i // 2 + 1)
                            act.wait_ge(mp_trd, 2 * h)
                            act.activation(mp[:, i, :], X[i // 2][:, (i % 2) * N_MEM:(i % 2 + 1) * N_MEM], ACT.Exp,
                                           bias=mrow[:, 4 + i:5 + i], scale=MEM_SCALE,
                                           accum_out=mrow[:, 8 + i:9 + i]).then_inc(m_exp, 1)
                    if t == s + 7:
                        for b in range(MB):
                            act.wait_ge(mp_trd, 2 * h + b + 1)
                            act.wait_ge(m_pv, 2 * h)
                            act.copy(mpt_hi[:, b, :], X[2 + b][:, :]).then_inc(mp_hid, 1)
            body(B_MEMATT, mem_attention, evacuate=sigmoids)

            def gates(B, late=None):
                def go(t):
                    if late:
                        late(t)
                    if t >= 6 and t % 2 == 0 and t < 6 + 2 * NT:
                        n = (t - 6) // 2
                        at_g = 4 * (B - 1 - B_Z) + n
                        act.wait_ge(g_mul, FIRST + at_g + 1)
                        if n >= 2:
                            act.wait_ge(g_stored, 128 * (B - 1 - B_Z) + 32 * (n - 1))
                        else:
                            act.wait_ge(g_stored, 128 * (B - 1 - B_Z))
                        act.copy(g_hi[:, n % 2, :], g_y[:, n, :]).then_inc(g_hid, 1)
                return go

            def last_norm(t):
                if t == 8:
                    rms(2, 2, 1024.0)
                if t == 10:
                    bring_sigmoid()
            body(B_Z + 1, gates(B_Z + 1, last_norm), evacuate=sigmoids)
            with act.Fori(B_Z + 2, B_OUT) as B:
                body(B, gates(B), evacuate=sigmoids)

            def out_square(B, n, src):
                o = B - B_OUT
                act.wait_ge(o_out, 4 * o + n + 1)
                act.wait_ge(g_mul, FIRST + 32)
                if not (isinstance(B, int) and B == B_OUT):
                    act.wait_ge(o_sq, 4 * o)
                act.activation(stage[:, n, :], src[:, n, :], ACT.Square,
                               accum_out=column(o_ss[:, n, :], o)).then_inc(o_sq, 1)

            def out_squares(B, buffer):
                def go(_):
                    for n in range(SB):
                        out_square(B, n, o_buf[:, buffer])
                return go
            body(B_OUT, gates(B_OUT), evacuate=out_squares(B_OUT, 0))
            with act.Fori(0, 3) as pair:
                body(2 * pair + (B_OUT + 1), evacuate=out_squares(2 * pair + (B_OUT + 1), 1))
                body(2 * pair + (B_OUT + 2), evacuate=out_squares(2 * pair + (B_OUT + 2), 0))

            def last_rms(n):
                act.wait_ge(f_sum, n + 1)
                act.activation(tiny[:, n:n + 1], tiny[:, n:n + 1], ACT.Sqrt, bias=eps[:, :],
                               scale=1.0 / D_MODEL).then_inc(f_sqrt, 1)

            def last_squares(B):
                act.activation(tiny[:, 32:33], eps[:, :], ACT.Sqrt)
                for n in range(SB):
                    out_square(B, n, o_fin[:, :, 7 * BW:8 * BW])
                    last_rms(n)
            body(B_END - 1, evacuate=last_squares)

        @block.vector
        def _(dve):
            start_counts(dve, conv, g_lod, g_mul, g_norm, k_lod, l_neg, l_scan, pt_lod,
                         q_lod, row_max)
            def split(B, k):
                dve.wait_ge(hi_ready, 32 * B + k + 1)
                hi, lo = split_slot(B, k)
                if isinstance(B, int) and B == B_END - 1 and k == KT - SKEW + RING:
                    dve.wait_ge(g_stored, 128 * 8)
                dve.tensor_tensor(lo, raw_slot(B, k)[0], f32(hi), ALU.subtract).then_inc(lo_ready, 1)

            def u_part(k):
                dve.wait_ge(u_split, k + 1)
                dve.tensor_tensor(u_lo_tile(k), x_rows[:, :, k * P:(k + 1) * P],
                                  f32(u_hi[:, k, :]).rearrange("p (b n) -> p b n", b=SB), ALU.subtract)

            def evac(B, width=SEQ):
                for n in (1, 3):
                    if n == 1:
                        dve.wait_ge(tile_done, 3 * B + n + 1)
                    else:
                        dve.wait_ge(unit_done, 32 * B + 32)
                    dve.tensor_copy(stage[:, n, 0:width], G[n][:, 0:width]).then_inc(dve_evac, 1)

            def body(B, side=None, before=None, evacuate=evac):
                for j in range(LEAD, KT + LEAD):
                    b, k = (B, j) if j < KT else (B + 1, j - KT)
                    if before:
                        before(j)
                    if not (isinstance(B, int) and B == B_END - 1 and j >= KT):
                        split(b, k)
                    if side:
                        side(j - LEAD)
                evacuate(B)

            def proj_evac(B, width=SEQ):
                dve.wait_ge(proj_stored, 64 * B)
                evac(B, width)

            dve.memset(ones[:, :], 1.0).then_inc(memset_done, 1)
            dve.memset(eps[:, :], EPS).then_inc(memset_done, 1)

            def m_part(t):
                dve.wait_ge(m_hid, t + 1)
                dve.scalar_tensor_tensor(m_lo[:, t, :], X[t % 4][:, 0:N_MEM], gains[:, G_MEM + t:G_MEM + t + 1],
                                         f32(m_hi[:, t, :]), ALU.mult, ALU.subtract).then_inc(m_lod, 1)
            for k in range(LEAD):
                m_part(k)
                split(0, k)

            def mem_stats(t):
                for c in range(8):
                    for b in range(MB):
                        if t == max(4 * c - 2, 0) + (2 if c else 1) * b:
                            dve.wait_ge(mem_in[c % 4], 16 * (c // 4 + 1))
                            dve.bn_stats(m_bn[:, b, 6 * c:6 * c + 6], mem_rows[:, b, c * 512:(c + 1) * 512])\
                               .then_inc(m_stat, 1)
                if t == 29:
                    dve.wait_ge(m_stat, 16)
                    for b in range(MB):
                        dve.bn_aggr(m_mv[:, b, :], m_bn[:, b, :]).then_inc(m_stat, 1)
                    dve.wait_ge(m_stat, 18)
                    dve.tensor_tensor(m_mv[:, :, 0], m_mv[:, :, 0], m_mv[:, :, 0], ALU.mult).then_inc(m_stat, 1)
                    dve.wait_ge(m_stat, 19)
                    dve.scalar_tensor_tensor(m_mv[:, :, 1], m_mv[:, :, 1], EPS, m_mv[:, :, 0], ALU.add, ALU.add)\
                       .then_inc(m_stat, 1)
                if t == 31:
                    dve.wait_ge(ident_in, 16)
                    dve.wait_ge(m_sqrt, 1)
                    dve.reciprocal(m_rstd[:, :], m_rstd[:, :]).then_inc(m_rs, 1)
                    dve.wait_ge(m_rs, 1)
                    for b in range(MB):
                        dve.tensor_scalar(m_diag[:, b, :], ident[:, :], m_rstd[:, b:b + 1], None, ALU.mult)\
                           .then_inc(m_rs, 1)
            body(0, mem_stats, lambda j: m_part(j) if j < KT else None, lambda B: proj_evac(B, N_MEM))

            def x_stats(t):
                if t == 3:
                    dve.wait_ge(m_spread, 1)
                    dve.tensor_copy(m_rms[:, :], X[0][:, 0:N_MEM]).then_inc(m_rms_set, 1)
                if t == 30:
                    dve.wait_ge(x_sq, 16)
                    dve.reduce_sum(x_rstd[:, :], x_ss[:, :, :], AX.X).then_inc(x_sum, 1)
                    dve.wait_ge(x_sum, 1)
                    dve.tensor_scalar(x_rstd[:, :], x_rstd[:, :], 1.0 / D_MODEL, EPS, ALU.mult, ALU.add)\
                       .then_inc(x_sum, 1)
                if t == 31:
                    dve.wait_ge(x_sqrt, 1)
                    dve.reciprocal(x_rstd[:, :], x_rstd[:, :]).then_inc(x_rs, 1)
            body(1, x_stats, evacuate=lambda B: proj_evac(B, N_MEM))
            body(2, evacuate=lambda B: proj_evac(B, N_MEM))
            body(3, before=lambda j: u_part(j - KT) if j >= KT else None,
                 evacuate=lambda B: proj_evac(B, N_MEM))
            body(B_XLRU, before=lambda j: u_part(j) if j < KT else None, evacuate=proj_evac)

            halves = [(i + ROT // 2) % ROT for i in range(ROT)]

            def rope_swap(B, r, t):
                for n in range(NT):
                    if t != SWAP_AT[n]:
                        continue
                    dve.wait_ge(act_evac if n % 2 == 0 else dve_evac, 2 * (B - 1) + n // 2 + 1)
                    dve.wait_ge(rope_done, FIRST + 4 * r + n)
                    dve.sem_inc(passed, 1)
                    dve.stream_shuffle(rot[:, :], stage[0:ROT, n, :], halves).then_inc(swapped, 1)

            cd = [0]

            def step(ins):
                cd[0] += 1
                ins.then_inc(cd_dve, 1)
                dve.wait_ge(cd_dve, cd[0])

            def decay(t):
                lam_c = par[:, C_LAM:C_LAM + 16]
                e, z, z2, s = tiny[:, 0:16], tiny[:, 16:32], tiny[:, 32:48], cdec[:, :]
                if t == 10:
                    dve.wait_ge(par_ready, 2)
                    step(dve.tensor_scalar(s, lam_c, -1.0, None, ALU.mult))
                    step(dve.tensor_tensor(e, lam_c, s, ALU.max))
                if t == 16:
                    dve.wait_ge(cd_act, 1)
                    step(dve.tensor_scalar(z, e, 2.0, None, ALU.add))
                    step(dve.reciprocal(z, z))
                    step(dve.tensor_tensor(z, z, e, ALU.mult))
                    step(dve.tensor_tensor(z2, z, z, ALU.mult))
                    step(dve.tensor_scalar(e, z2, 1.0 / 19, 1.0 / 17, ALU.mult, ALU.add))
                if 17 <= t < 25:
                    n = 15 - 2 * (t - 17)
                    step(dve.tensor_tensor(e, e, z2, ALU.mult))
                    step(dve.tensor_scalar(e, e, 1.0 / n, None, ALU.add))
                if t == 25:
                    step(dve.tensor_tensor(e, e, z, ALU.mult))
                    step(dve.tensor_scalar(s, s, 0.0, None, ALU.max))
                    step(dve.scalar_tensor_tensor(s, e, 2.0, s, ALU.mult, ALU.add))
                    step(dve.tensor_scalar(s, s, -LRU_C, None, ALU.mult))

            body(B_XLRU + 1, decay, evacuate=proj_evac)

            def lru(B, rope=None):
                def go(t):
                    if rope is not None:
                        rope_swap(B, rope, t)
                    for i, s in enumerate(TILE_AT):
                        T = 2 * (B - B_LRU) + i
                        for d in range(2):
                            if t == s + 12 + d:
                                dve.wait_ge(l_b, FIRST + 2 * T + d + 1)
                                o, a, v = l_h[:, d, :], l_a[:, d, :], l_n[:, d, :]
                                if d == 0:
                                    dve.tensor_tensor_scan(o, a, v, 0.0, ALU.mult, ALU.add).then_inc(l_scan, 1)
                                else:
                                    dve.tensor_tensor_scan(o[:, ::-1], a[:, ::-1], v[:, ::-1], 0.0, ALU.mult,
                                                           ALU.add).then_inc(l_scan, 1)
                        if t == s + 14:
                            dve.wait_ge(l_scan, FIRST + 2 * T + 2)
                            dve.wait_ge(y_free, FIRST + T)
                            dve.wait_ge(y_sq, FIRST + T)
                            dve.tensor_tensor(l_y[:, :], l_h[:, 0, :], l_h[:, 1, :], ALU.add).then_inc(l_sum, 1)
                        if t == s:
                            dve.wait_ge(l_xin, 16 * T + 16)
                            dve.wait_ge(l_mm, FIRST + 4 * T)
                            dve.wait_ge(l_ix, FIRST + 2 * T)
                            dve.tensor_scalar(xc[:, :], l_in[:, 0:SEQ], par[:, bass.ds(T + C_CONVW, 1)],
                                              par[:, bass.ds(T + C_CONVB, 1)], ALU.mult, ALU.add).then_inc(conv, 1)
                        for j in range(1, 4):
                            if t == s + j:
                                dve.wait_ge(conv, FIRST + 4 * T + j)
                                dve.scalar_tensor_tensor(xc[:, :], l_in[:, j:j + SEQ],
                                                         par[:, bass.ds(T + (C_CONVW + 8 * j), 1)], xc[:, :],
                                                         ALU.mult, ALU.add).then_inc(conv, 1)
                        if t == s + 3:
                            dve.wait_ge(l_whid, T + 1)
                            dve.tensor_tensor(l_wlo[:, :, :, :], l_w[:, :, :, :], f32(l_whi[:, :, :, :]),
                                              ALU.subtract).then_inc(l_wlod, 1)
                        if t == s + 4:
                            dve.wait_ge(xc_hid, T + 1)
                            dve.tensor_tensor(xc_lo[:, 2:2 + SEQ], xc[:, :], f32(xc_hi[:, :]), ALU.subtract)\
                               .then_inc(xc_lod, 1)
                        if t == s + 9:
                            for d in range(2):
                                dve.wait_ge(l_asq, 2 * T + d + 1)
                                dve.wait_ge(l_exp, 4 * T + 2 * d + 2)
                                dve.scalar_tensor_tensor(l_n[:, d, :], l_n[:, d, :], 1.0, l_t[:, d, :], ALU.add,
                                                         ALU.mult).then_inc(l_neg, 1)
                return go
            with dve.Fori(0, 2) as pair:
                body(2 * pair + B_LRU, lru(2 * pair + B_LRU), evacuate=proj_evac)
                body(2 * pair + (B_LRU + 1), lru(2 * pair + (B_LRU + 1), pair), evacuate=proj_evac)

            def attention(B, rope):
                g = B - B_ATT

                def go(t):
                    if t == 0:
                        dve.wait_ge(k_hid, g + 1)
                        dve.tensor_tensor(k_lo[:, :], k_raw[:, :], f32(k_hi[:, :]), ALU.subtract).then_inc(k_lod, 1)
                        dve.wait_ge(const_in, 32)
                        dve.tensor_copy(sink4[:, :], sinks[:, bass.ds(4 * g, 4)]).then_inc(sink_set, 1)
                    if t == 2:
                        dve.wait_ge(v_hid, g + 1)
                        dve.tensor_tensor(v_lo[:, :], v_raw[:, :], f32(v_hi[:, :]), ALU.subtract).then_inc(v_lod, 1)
                    for i, s in enumerate(HEAD_AT):
                        h = 4 * g + i
                        if t == s:
                            dve.wait_ge(q_hid, h + 1)
                            dve.tensor_tensor(q_lo[:, :], q_raw[:, :], f32(q_hi[:, :]), ALU.subtract)\
                               .then_inc(q_lod, 1)
                        for pair in range(2):
                            if t == s + 3 + 3 * pair:
                                for b in (2 * pair, 2 * pair + 1):
                                    nk = BAND[b][1]
                                    dve.wait_ge(pt_hid, 4 * h + b + 1)
                                    slots = slice(PT_FIRST[b], PT_FIRST[b] + 2 * nk - 1, 2)
                                    dve.tensor_tensor(pt_lo[:, slots, :],
                                                      X[2 + b % 2][:, 0:nk * P].rearrange("p (j q) -> p j q", q=P),
                                                      f32(pt_hi[:, slots, :]), ALU.subtract).then_inc(pt_lod, 1)
                            if t == s + 1 + 3 * pair - pair:
                                sk = sink4[:, i:i + 1]
                                dve.wait_ge(sink_set, g + 1)
                                for e in range(2):
                                    b = 2 * pair + e
                                    k0, nk = BAND[b]
                                    m0 = (k0 - b + 1) * P
                                    dve.wait_ge(scored, FIRST + 4 * h + b + 1)
                                    if pair:
                                        dve.wait_ge(p_trd, FIRST + 4 * h + b - 1)
                                    else:
                                        dve.wait_ge(p_trd, FIRST + 4 * h)
                                    dve.sem_inc(passed, 1)
                                    dve.tensor_tensor_reduce(probs[:, e, 0:nk * P], X[b % 2][:, 0:nk * P],
                                                             mask[:, m0:m0 + nk * P], ATT_SCALE, sk, ALU.add,
                                                             ALU.max, srow[:, e:e + 1]).then_inc(row_max, 1)
                                dve.wait_ge(row_max, FIRST + 4 * h + 2 * pair + 2)
                                dve.tensor_scalar(srow[:, 4:6], srow[:, 0:2], -1.0, None, ALU.mult)\
                                   .then_inc(max_neg, 1)
                                dve.wait_ge(max_neg, 2 * h + pair + 1)
                                dve.tensor_scalar(srow[:, 12:14], srow[:, 4:6], sk, None, ALU.add)\
                                   .then_inc(sink_diff, 1)
                            if t == s + 2 + 3 * pair:
                                dve.wait_ge(exped, 4 * h + 2 * pair + 2)
                                dve.wait_ge(sink_exp, 2 * h + pair + 1)
                                dve.tensor_tensor(srow[:, 18:20], srow[:, 8:10], srow[:, 16:18], ALU.add)\
                                   .then_inc(denom, 1)
                                dve.wait_ge(denom, 2 * h + pair + 1)
                                dve.reciprocal(srow[:, 20:22], srow[:, 18:20]).then_inc(recip, 1)
                                dve.wait_ge(recip, 2 * h + pair + 1)
                                for e in range(2):
                                    pr = probs[:, e, 0:BAND[2 * pair + e][1] * P]
                                    dve.tensor_scalar(pr, pr, srow[:, 20 + e:21 + e], None, ALU.mult)\
                                       .then_inc(normed, 1)
                    if rope:
                        rope_swap(B, g + 2, t)
                return go
            with dve.Fori(B_ATT, B_MEMATT - 1) as B:
                body(B, attention(B, True), evacuate=proj_evac)
            body(B_MEMATT - 1, attention(B_MEMATT - 1, False), evacuate=proj_evac)

            def hold(B):
                for n in range(NT):
                    dve.wait_ge(sig_done, 4 * (B - B_Z) + n + 1)
                    dve.tensor_tensor(stage[:, n, :], stage[:, n, :], G[n][:, :], ALU.mult).then_inc(z_held, 1)

            def rms(which):
                dve.wait_ge(r_sqrt, which + 1)
                dve.reciprocal(r_bc[:, which, :], r_bc[:, which, :]).then_inc(r_ready, 1)

            def mem_attention(t):
                if t == 12:
                    rms(0)
                if t == 19:
                    rms(1)
                for h, s in enumerate(MEMHEAD_AT):
                    if t == s + 1:
                        dve.wait_ge(mk_hid, h + 1)
                        dve.tensor_tensor(mk_lo[:, :], mk_raw[:, :], f32(mk_hi[:, :]), ALU.subtract)\
                           .then_inc(mk_lod, 1)
                        dve.wait_ge(mv_hid, h + 1)
                        dve.tensor_tensor(mv_lo[:, :], X[2][:, :], f32(mv_hi[:, :]), ALU.subtract)\
                           .then_inc(mv_lod, 1)
                    for d in range(2):
                        if t == s + 1 + 2 * d:
                            dve.wait_ge(mq_hid, 2 * h + d + 1)
                            dve.tensor_tensor(mq_lo[:, d, :], mq_raw[:, d, :], f32(mq_hi[:, d, :]), ALU.subtract)\
                               .then_inc(mq_lod, 1)
                    if t == s + 4:
                        for i in range(2):
                            dve.wait_ge(m_scored, 2 * h + i + 1)
                            dve.reduce_max(mrow[:, 2 * i:2 * i + 2],
                                           X[i][:, :].rearrange("p (b m) -> p b m", b=2), AX.X).then_inc(m_max, 1)
                            dve.wait_ge(m_max, 2 * h + i + 1)
                            dve.tensor_scalar(mrow[:, 4 + 2 * i:6 + 2 * i], mrow[:, 2 * i:2 * i + 2], -MEM_SCALE,
                                              None, ALU.mult).then_inc(m_neg, 1)
                    if t == s + 5:
                        dve.wait_ge(m_exp, SB * h + SB)
                        dve.reciprocal(mrow[:, 12:16], mrow[:, 8:12]).then_inc(m_rec, 1)
                        dve.wait_ge(m_rec, h + 1)
                        for i in range(SB):
                            dve.tensor_scalar(mp[:, i, :], mp[:, i, :], mrow[:, 12 + i:13 + i], None, ALU.mult)\
                               .then_inc(m_norm, 1)
                    if t == s + 7:
                        dve.wait_ge(y_stored, 16 * 24)
                        for b in range(MB):
                            dve.wait_ge(mp_hid, 2 * h + b + 1)
                            dve.tensor_tensor(mpt_lo[:, b, :], X[2 + b][:, :], f32(mpt_hi[:, b, :]), ALU.subtract)\
                               .then_inc(mp_lod, 1)
            body(B_MEMATT, mem_attention, evacuate=hold)

            def gates(B, which, late=None):
                def go(t):
                    if late:
                        late(t)
                    if t >= 5 and t < 5 + 2 * NT:
                        n = (t - 5) // 2
                        at_g = 4 * (B - 1 - B_Z) + n
                        if t % 2 == 1:
                            dve.wait_ge(gy_in[n], 16 * (B - B_Z))
                            dve.wait_ge(r_ready, which + 1)
                            dve.scalar_tensor_tensor(g_y[:, n, :], g_y[:, n, :],
                                                     gains[:, bass.ds(at_g + G_OUT, 1)] if not isinstance(B, int)
                                                     else gains[:, at_g + G_OUT:at_g + G_OUT + 1],
                                                     r_bc[:, which, :], ALU.mult, ALU.mult).then_inc(g_norm, 1)
                            dve.wait_ge(g_norm, FIRST + at_g + 1)
                            dve.wait_ge(z_held, at_g + 1)
                            dve.tensor_tensor(g_y[:, n, :], g_y[:, n, :], stage[:, n, :], ALU.mult)\
                               .then_inc(g_mul, 1)
                        else:
                            dve.wait_ge(g_hid, at_g + 1)
                            dve.tensor_tensor(g_lo[:, n % 2, :], g_y[:, n, :], f32(g_hi[:, n % 2, :]),
                                              ALU.subtract).then_inc(g_lod, 1)
                return go
            body(B_Z + 1, gates(B_Z + 1, 0, lambda t: rms(2) if t == 8 else None), evacuate=hold)
            with dve.Fori(B_Z + 2, B_Z + 5) as B:
                body(B, gates(B, 0), evacuate=hold)
            with dve.Fori(B_Z + 5, B_Z + 7) as B:
                body(B, gates(B, 1), evacuate=hold)
            body(B_OUT - 1, gates(B_OUT - 1, 2), evacuate=hold)

            def out_row(B, n, dst):
                if n < SB - 1:
                    dve.wait_ge(tile_done, 3 * B + n + 1)
                else:
                    dve.wait_ge(unit_done, 32 * B + 32)
                dve.tensor_copy(dst[:, n, :], G[n][:, :]).then_inc(o_out, 1)

            def out_rows(B, buffer):
                def go(_):
                    if not (isinstance(B, int) and B == B_OUT):
                        dve.wait_ge(o_free, B - B_OUT)
                    for n in range(SB):
                        out_row(B, n, o_buf[:, buffer])
                return go
            body(B_OUT, gates(B_OUT, 2), evacuate=out_rows(B_OUT, 0))
            with dve.Fori(0, 3) as pair:
                body(2 * pair + (B_OUT + 1), evacuate=out_rows(2 * pair + (B_OUT + 1), 1))
                body(2 * pair + (B_OUT + 2), evacuate=out_rows(2 * pair + (B_OUT + 2), 0))

            def row_sum(n):
                dve.wait_ge(o_sq, 28 + n + 1)
                dve.reduce_sum(tiny[:, n:n + 1], o_ss[:, n, :], AX.X).then_inc(f_sum, 1)

            def row_rms(n):
                dve.wait_ge(f_sqrt, n + 1)
                dve.reciprocal(tiny[:, 16 + n:17 + n], tiny[:, n:n + 1]).then_inc(f_rs, 1)

            def final(i):
                c, q = FINAL[i]
                first = q * 1024
                if (c, q) == (0, 0):
                    dve.wait_ge(fin_in, 16 * 12)
                if (c, q) == (0, 2):
                    dve.wait_ge(last_in, 32)
                if q == 0:
                    dve.wait_ge(f_rs, c + 1)
                if q == 3:
                    dve.wait_ge(post_mul, 28 + c + 1)
                x_row = x_fin[:, c, :] if c < 3 else (x_mid if q < 2 else x_end)
                x_first = first if c < 3 else first % 2048
                pieces = ((o_fin[:, c, first:first + 1024], 0, 1024),) if q < 3 else (
                    (o_buf[:, 0, c, :], 0, 512), (o_fin[:, c, first + 512:first + 1024], 512, 512))
                for o_part, start, width in pieces:
                    x_part = x_row[:, x_first + start:x_first + start + width]
                    ins = dve.scalar_tensor_tensor(o_fin[:, c, first + start:first + start + width], o_part,
                                                   tiny[:, 16 + c:17 + c], x_part, ALU.mult, ALU.add)
                ins.then_inc(f_done, 1)

            def last_rows(B):
                done = iter(range(len(FINAL)))
                for n in range(SB):
                    out_row(B, n, o_fin[:, :, 7 * BW:8 * BW])
                    if n:
                        final(next(done))
                    row_sum(n)
                    row_rms(n)
                    for _ in range(3):
                        final(next(done))
                final(next(done))
            body(B_END - 1, evacuate=last_rows)

        @block.gpsimd
        def _(pool):
            start_counts(pool, l_b, l_ix, y_acc, y_free, o_free, rope_done)
            pool.memset(sq_acc[:, :], 0.0).then_inc(acc_zero, 1)

            def copied(B, n):
                pool.wait_ge(dve_evac if n % 2 else act_evac, 2 * B + n // 2 + 1)

            def store(B, dst, width=SEQ, rope=None, tiles=range(NT)):
                if 0 in tiles and not (isinstance(B, int) and B == 0):
                    pool.wait_ge(proj_stored, 64 * B)
                for n in tiles:
                    copied(B, n)
                    if width == N_MEM:
                        v = stage[:, n, 0:width]
                        pool.tensor_tensor(v, v, m_rms[:, :], ALU.mult).then_inc(kv_scaled, 1)
                        pool.wait_ge(kv_scaled, 4 * B + n + 1)
                    if rope is not None:
                        r = 4 * rope + n
                        pool.wait_ge(swapped, r + 1)
                        pool.tensor_tensor(rot[:, :], rot[:, :], rope_s[:, :], ALU.mult).then_inc(rope_mul, 1)
                        v = stage[0:ROT, n, :]
                        pool.tensor_tensor(v, v, rope_c[:, :], ALU.mult).then_inc(rope_mul, 1)
                        pool.wait_ge(rope_mul, 2 * r + 2)
                        pool.tensor_tensor(v, v, rot[:, :], ALU.add).then_inc(rope_done, 1)
                        pool.wait_ge(rope_done, FIRST + r + 1)
                    pool.dma_start(dst(n), stage[:, n, 0:width]).then_inc(proj_stored, 16)

            def kv_rows(B):
                return lambda n: kvT[bass.ds(B * BW + n * P, P), :]

            def proj_rows(B):
                return lambda n: projT[bass.ds((B - 4) * BW + n * P, P), :]

            pool.wait_ge(m_rms_set, 1)
            store(0, kv_rows(0), N_MEM)

            def x_scale(e):
                v = x_rows[:, :, bass.ds(e * P, P)]
                pool.tensor_tensor(v, v, x_rstd[:, :].unsqueeze(2).to_broadcast([P, SB, P]), ALU.mult)\
                    .then_inc(x_scl, 1)

            pool.wait_ge(x_rs, 1)
            with pool.Fori(0, 4) as e:
                x_scale(e)
            store(1, kv_rows(1), N_MEM)
            with pool.Fori(4, KT) as e:
                x_scale(e)
            with pool.Fori(2, B_MEM_END) as B:
                store(B, kv_rows(B), N_MEM)
            store(B_XLRU, proj_rows(B_XLRU))
            pool.memset(r_bc[:, 1:3, :], 0.0).then_inc(l_zero, 1)
            pool.memset(l_in[:, 0:2], 0.0)
            pool.memset(l_in[:, SEQ + 2:SEQ + 4], 0.0).then_inc(l_zero, 1)
            pool.wait_ge(l_zero, 2)
            pool.wait_ge(acc_zero, 1)
            pool.wait_ge(rope_in, 32)

            def lru_tile(T):
                for d in range(2):
                    pool.wait_ge(l_sig, FIRST + 4 * T + d + 3)
                    pool.wait_ge(conv, FIRST + 4 * T + 4)
                    pool.tensor_tensor(l_i[:, d, :], l_i[:, d, :], xc[:, :], ALU.mult).then_inc(l_ix, 1)
                for d in range(2):
                    pool.wait_ge(l_exp, 4 * T + 2 * d + 1)
                    pool.wait_ge(l_scan, FIRST + 2 * T)
                    pool.tensor_tensor(l_n[:, d, :], l_a[:, d, :], l_a[:, d, :], ALU.mult).then_inc(l_asq, 1)
                for d in range(2):
                    pool.wait_ge(l_mult, 2 * T + d + 1)
                    pool.wait_ge(l_ix, FIRST + 2 * T + d + 1)
                    pool.tensor_tensor(l_n[:, d, :], l_n[:, d, :], l_i[:, d, :], ALU.mult).then_inc(l_b, 1)
                pool.wait_ge(l_sum, T + 1)
                pool.dma_start(yT[bass.ds(T * P + 16 * P, P), :], l_y[:, :]).then_inc(y_stored, 16)
                pool.wait_ge(y_sq, FIRST + T + 1)
                pool.wait_ge(y_acc, FIRST + T)
                pool.tensor_tensor(r_bc[:, 1, :], r_bc[:, 1, :], sq_tmp[:, :], ALU.add).then_inc(y_acc, 1)
                pool.wait_ge(y_stored, 16 * T + 16)
                pool.sem_inc(y_free, 1)

            with pool.Fori(0, 2) as pair:
                store(2 * pair + (B_LRU - 1), proj_rows(2 * pair + (B_LRU - 1)))
                lru_tile(4 * pair)
                lru_tile(4 * pair + 1)
                store(2 * pair + B_LRU, proj_rows(2 * pair + B_LRU), rope=pair, tiles=(0, 1))
                lru_tile(4 * pair + 2)
                store(2 * pair + B_LRU, proj_rows(2 * pair + B_LRU), rope=pair, tiles=(2, 3))
                lru_tile(4 * pair + 3)

            def head_out(h):
                pool.wait_ge(y_out, h + 1)
                pool.dma_start(yT[bass.ds(h * P, P), :], y_sb[:, :]).then_inc(y_stored, 16)
                pool.wait_ge(y_sq, FIRST + LRU_TILES + h + 1)
                pool.wait_ge(y_acc, FIRST + LRU_TILES + h)
                pool.tensor_tensor(sq_acc[:, :], sq_acc[:, :], sq_tmp[:, :], ALU.add).then_inc(y_acc, 1)
                pool.wait_ge(y_stored, 16 * (LRU_TILES + 1) + 16 * h)
                pool.sem_inc(y_free, 1)

            with pool.Fori(B_ATT, B_MEMATT - 1) as B:
                for i, tiles in enumerate(((0, 1), (2,), (3,), ())):
                    store(B - 1, proj_rows(B - 1), rope=B - B_ATT + 2, tiles=tiles)
                    head_out(4 * (B - B_ATT) + i)
            store(B_MEMATT - 2, proj_rows(B_MEMATT - 2))
            for i in range(4):
                head_out(12 + i)

            store(B_MEMATT - 1, proj_rows(B_MEMATT - 1))
            for i in range(8):
                pool.wait_ge(y_out, HEADS + i + 1)
                v = m_y[:, i % 2, :]
                pool.dma_start(yT[(24 + i) * P:(25 + i) * P, :], v).then_inc(y_stored, 16)
                pool.wait_ge(y_acc, FIRST + 24 + i)
                pool.tensor_tensor(sq_tmp[:, :], v, v, ALU.mult).then_inc(my_sq, 1)
                pool.wait_ge(my_sq, i + 1)
                pool.tensor_tensor(r_bc[:, 2, :], r_bc[:, 2, :], sq_tmp[:, :], ALU.add).then_inc(y_acc, 1)

            with pool.Fori(0, 8) as z:
                for n in range(NT):
                    for part, made, dst in ((g_hi, g_hid, gT_hi), (g_lo, g_lod, gT_lo)):
                        pool.wait_ge(made, (FIRST if made is g_lod else 0) + 4 * z + n + 1)
                        pool.sem_inc(passed, 1)
                        pool.dma_start(dst[bass.ds(z * BW + n * P, P), :], f32(part[:, n % 2, :]))\
                            .then_inc(g_stored, 16)
                    pool.wait_ge(g_stored, 128 * z + 32 * n + 32)

            def out_gain(o, rows):
                pool.wait_ge(post_in, 16 * o + 16)
                for n in range(SB):
                    pool.wait_ge(o_out, 4 * o + n + 1)
                    pool.wait_ge(o_sq, 4 * o + n + 1)
                    pool.tensor_tensor(rows[:, n, :], rows[:, n, :], post_row[:, :], ALU.mult).then_inc(post_mul, 1)

            def out_store(o, buffer):
                out_gain(o, o_buf[:, buffer])
                pool.wait_ge(post_mul, 4 * o + 4)
                pool.sem_inc(passed, 1)
                pool.dma_start(o_rows[:, bass.ds(o * BW, BW)].rearrange("(b p) n -> p b n", p=P),
                               o_buf[:, buffer, :, :]).then_inc(o_stored, 16)
                pool.wait_ge(o_stored, 16 * o + 16)
                pool.sem_inc(o_free, 1)

            with pool.Fori(0, 3) as pair:
                out_store(2 * pair, 0)
                out_store(2 * pair + 1, 1)
            out_gain(6, o_buf[:, 0])
            out_gain(7, o_fin[:, :, 7 * BW:8 * BW])


_INS = ["x", "mem", "pre_norm_gain", "w_in", "att_sink", "conv_w", "conv_b", "lru_w_a", "lru_b_a", "lru_w_x",
        "lru_b_x", "lru_lambda", "mem_norm_gain", "w_mem_kv", "att_out_gain", "lru_out_gain", "mem_out_gain",
        "w_out", "post_norm_gain"]


def shape_constants():
    half = ROT // 2
    inv_freq = np.power(np.float32(500000.0), -np.arange(half, dtype=np.float32) * np.float32(2.0) / np.float32(ROT))
    ang = np.arange(SEQ, dtype=np.float32)[None, :] * inv_freq[:, None]
    cos, sin = np.cos(ang).astype(np.float32), np.sin(ang).astype(np.float32)
    q, k = np.arange(P)[:, None], np.arange(3 * P)[None, :] - P
    return {
        "rope_cos": np.concatenate([cos, cos]),
        "rope_sin": np.concatenate([-sin, sin]),
        "band_mask": np.where(np.abs(k - q) <= P, 0.0, MASKED).astype(np.float32),
        "identity": np.eye(P, dtype=np.float32),
    }


def kernel(**inputs):
    import concourse.bacc as bacc
    from concourse.bass_utils import run_bass_kernel_spmd

    nc = bacc.Bacc("TRN2", target_bir_lowering=False, num_devices=1)
    arrays, args = {}, []
    named = {name: np.ascontiguousarray(inputs[name]) for name in _INS}
    named.update(shape_constants())
    for name, a in named.items():
        arrays[f"in_{name}"] = a
        args.append(nc.dram_tensor(f"in_{name}", a.shape, mybir.dt.from_np(a.dtype), kind="ExternalInput").ap())
    out = nc.dram_tensor("out_0", (1, SEQ, D_MODEL), F32, kind="ExternalOutput").ap()
    hymba(nc, *args, out)
    return run_bass_kernel_spmd(nc, [arrays], core_ids=[0]).results[0]["out_0"]
```
